# Optimizing a Trainium2 kernel written in Bass

```python
import math, functools
import jax, jax.numpy as jnp
from jax import lax
import numpy as np

D_MODEL = 1024
BATCH = 1
SEQ = 2048
DEPTH = 1
DEC_BATCH = 8
DEC_SEQ = 1
PAST_LEN = 16384
PAGE_SIZE = 128

MIX_W = D_MODEL
RWKV_W = MIX_W // 2
CONV_W = MIX_W - RWKV_W
HEAD_SIZE = 64
N_RWKV_HEADS = RWKV_W // HEAD_SIZE
DECAY_LORA = 64
AAA_LORA = 64
MV_LORA = 32
GATE_LORA = 128
CONV_K = 3
N_MEM = 256
N_XHEADS = 4
XHEAD_DIM = D_MODEL // N_XHEADS
FFN_W = ((8 * D_MODEL // 3 + 127) // 128) * 128
FFN_K = 3
EPS = 1e-6
GN_EPS = HEAD_SIZE * 1e-5
RWKV_COLS = 3 * RWKV_W + DECAY_LORA + AAA_LORA + GATE_LORA
IN_COLS = RWKV_COLS + 3 * CONV_W
RWKV_SPLITS = (RWKV_W, 2 * RWKV_W, 3 * RWKV_W, 3 * RWKV_W + DECAY_LORA, 3 * RWKV_W + DECAY_LORA + AAA_LORA)

kernel_name = 'hymba_rwkv7_shortconv_convffn_memxattn_step'

def rmsnorm(x, g):
    xf = x.astype(jnp.float32)
    y = xf * lax.rsqrt(jnp.mean(xf * xf, axis=-1, keepdims=True) + EPS)
    return (y * g.astype(jnp.float32)).astype(x.dtype)

def causal_dwconv(u, prev, w):
    K = w.shape[0]
    T = u.shape[1]
    ext = jnp.concatenate([prev.astype(u.dtype), u], axis=1)
    out = w[0] * ext[:, 0:T]
    for j in range(1, K):
        out = out + w[j] * ext[:, j:j + T]
    return out, ext[:, -(K - 1):]

def wkv_scan(S0, r, decay, k, v, a, b):
    def step(S, inp):
        r_t, d_t, k_t, v_t, a_t, b_t = inp
        Sa = jnp.einsum('bhvk,bhk->bhv', S, a_t)
        S = S * d_t[:, :, None, :] + Sa[..., :, None] * b_t[..., None, :] + v_t[..., :, None] * k_t[..., None, :]
        return S, jnp.einsum('bhvk,bhk->bhv', S, r_t)
    xs = tuple(jnp.swapaxes(t, 0, 1) for t in (r, decay, k, v, a, b))
    S, ys = lax.scan(step, S0, xs)
    return S, jnp.swapaxes(ys, 0, 1)

def rwkv7_group(p_cur, p_prev, S0, v_first, l, P):
    B, T, _ = p_cur.shape
    f32 = jnp.float32
    p_shift = jnp.concatenate([p_prev.astype(p_cur.dtype), p_cur[:, :-1]], axis=1)
    z = p_cur + (p_shift - p_cur) * P['mu_shift'][l]
    r, k, v, wl, al, gl = jnp.split(z, RWKV_SPLITS, axis=-1)
    w = -jax.nn.softplus(-(P['w0'][l] + jnp.tanh(wl) @ P['w2'][l]).astype(f32)) - 0.5
    decay = jnp.exp(-jnp.exp(w))
    a = jax.nn.sigmoid((P['a0'][l] + al @ P['a2'][l]).astype(f32))
    g = jax.nn.sigmoid(gl) @ P['g2'][l]
    if v_first is None:
        v_first = v
    else:
        vmix = jax.nn.sigmoid(P['v0'][l - 1] + (v @ P['v1'][l - 1]) @ P['v2'][l - 1])
        v = v + (v_first - v) * vmix
    hs = lambda t: t.reshape(B, T, N_RWKV_HEADS, HEAD_SIZE).astype(f32)
    ph = lambda t: t.reshape(N_RWKV_HEADS, HEAD_SIZE).astype(f32)
    r_h, k_h, v_h, a_h, d_h = hs(r), hs(k), hs(v), hs(a), hs(decay)
    kk = k_h * ph(P['k_k'][l])
    kk = kk / jnp.maximum(jnp.sqrt(jnp.sum(kk * kk, axis=-1, keepdims=True)), 1e-12)
    k_h = k_h * (1.0 + (a_h - 1.0) * ph(P['k_a'][l]))
    S, y = wkv_scan(S0.astype(f32), r_h, d_h, k_h, v_h, -kk, kk * a_h)
    mean = jnp.mean(y, axis=-1, keepdims=True)
    var = jnp.mean(jnp.square(y - mean), axis=-1, keepdims=True)
    y = (y - mean) * lax.rsqrt(var + GN_EPS) * ph(P['ln_x_w'][l]) + ph(P['ln_x_b'][l])
    y = y + jnp.sum(r_h * k_h * ph(P['r_k'][l]), axis=-1, keepdims=True) * v_h
    out = y.reshape(B, T, RWKV_W).astype(p_cur.dtype) * g
    return out, S, v_first

def layer(x, l, mem_k, mem_v, shift_prev, wkv_prev, conv_prev, ffn_prev, v_first, P):
    B, T, _ = x.shape
    xn = rmsnorm(x, P['norm_mix'][l])
    w_in = P['w_in'][l]
    proj = xn @ w_in
    p_rwkv, p_conv = proj[..., :RWKV_COLS], proj[..., RWKV_COLS:]
    p_prev = (shift_prev.astype(xn.dtype) @ w_in[:, :RWKV_COLS])[:, None, :]
    y_a, wkv_new, v_first = rwkv7_group(p_rwkv, p_prev, wkv_prev, v_first, l, P)
    gate_b, gate_c, h_in = jnp.split(p_conv, 3, axis=-1)
    conv_out, conv_new = causal_dwconv(gate_c * h_in, conv_prev, P['conv_w'][l])
    y_b = gate_b * conv_out
    x = x + jnp.concatenate([y_a, y_b], axis=-1) @ P['w_out'][l]
    xq = rmsnorm(x, P['norm_x'][l])
    q = (xq @ P['wq'][l]).reshape(B, T, N_XHEADS, XHEAD_DIM)
    s = jnp.einsum('bthd,bmhd->bhtm', q, mem_k.astype(q.dtype)).astype(jnp.float32) * (XHEAD_DIM ** -0.5)
    p = jax.nn.softmax(s, axis=-1).astype(x.dtype)
    o = jnp.einsum('bhtm,bmhd->bthd', p, mem_v.astype(x.dtype)).reshape(B, T, D_MODEL)
    x = x + o @ P['wo'][l]
    xf = rmsnorm(x, P['norm_ffn'][l])
    up = xf @ P['w_up'][l]
    upc, ffn_new = causal_dwconv(up, ffn_prev, P['ffn_conv_w'][l])
    u, gt = jnp.split(upc, 2, axis=-1)
    x = x + (jax.nn.silu(gt) * u) @ P['w_down'][l]
    return x, xn[:, -1], wkv_new, conv_new, ffn_new, v_first

def trunk(x, mem_k, mem_v, shift0, wkv0, conv0, ffn0, P):
    v_first = None
    shs, wks, cvs, ffs = [], [], [], []
    for l in range(DEPTH):
        x, sh, S, cs, fs, v_first = layer(x, l, mem_k[l], mem_v[l], shift0[l], wkv0[l], conv0[l], ffn0[l], v_first, P)
        shs.append(sh)
        wks.append(S)
        cvs.append(cs)
        ffs.append(fs)
    y = rmsnorm(x, P['norm_final'])
    return y, jnp.stack(shs), jnp.stack(wks), jnp.stack(cvs), jnp.stack(ffs)

def setup_inputs(seed: int = 0) -> dict:
    key = jax.random.key(seed)
    ks = iter(jax.random.split(key, 48))
    nrm = lambda shape, scale: jax.random.normal(next(ks), shape, jnp.float32) * scale
    L = DEPTH
    D = D_MODEL
    H, N = N_RWKV_HEADS, HEAD_SIZE
    d = {}
    d['x_prompt'] = nrm((BATCH, SEQ, D), 1.0)
    d['x_sample'] = nrm((DEC_BATCH, DEC_SEQ, D), 1.0)
    d['mem_prompt'] = nrm((BATCH, N_MEM, D), 1.0)
    d['state_shift'] = nrm((L, DEC_BATCH, D), 1.0)
    d['state_wkv'] = nrm((L, DEC_BATCH, H, N, N), 0.3)
    d['state_conv'] = nrm((L, DEC_BATCH, CONV_K - 1, CONV_W), 1.0)
    d['state_ffn'] = nrm((L, DEC_BATCH, FFN_K - 1, 2 * FFN_W), 1.0)
    d['cache_mem_k'] = nrm((L, DEC_BATCH, N_MEM, N_XHEADS, XHEAD_DIM), 1.0)
    d['cache_mem_v'] = nrm((L, DEC_BATCH, N_MEM, N_XHEADS, XHEAD_DIM), 1.0)
    d['norm_mix'] = 1.0 + nrm((L, D), 0.02)
    d['w_in'] = nrm((L, D, IN_COLS), D ** -0.5)
    d['mu_shift'] = jax.random.uniform(next(ks), (L, RWKV_COLS), jnp.float32)
    d['w0'] = jax.random.uniform(next(ks), (L, RWKV_W), jnp.float32, -2.0, 1.0)
    d['w2'] = nrm((L, DECAY_LORA, RWKV_W), 0.1)
    d['a0'] = nrm((L, RWKV_W), 0.1)
    d['a2'] = nrm((L, AAA_LORA, RWKV_W), 0.1)
    d['g2'] = nrm((L, GATE_LORA, RWKV_W), GATE_LORA ** -0.5)
    d['v0'] = nrm((L - 1, RWKV_W), 0.1)
    d['v1'] = nrm((L - 1, RWKV_W, MV_LORA), RWKV_W ** -0.5)
    d['v2'] = nrm((L - 1, MV_LORA, RWKV_W), 0.1)
    d['k_k'] = 0.85 + nrm((L, RWKV_W), 0.02)
    d['k_a'] = 1.0 + nrm((L, RWKV_W), 0.02)
    d['r_k'] = nrm((L, RWKV_W), 0.1)
    d['ln_x_w'] = 1.0 + nrm((L, RWKV_W), 0.02)
    d['ln_x_b'] = nrm((L, RWKV_W), 0.02)
    d['conv_w'] = nrm((L, CONV_K, CONV_W), CONV_K ** -0.5)
    d['w_out'] = nrm((L, MIX_W, D), MIX_W ** -0.5)
    d['norm_x'] = 1.0 + nrm((L, D), 0.02)
    d['norm_mem'] = 1.0 + nrm((L, D), 0.02)
    d['wq'] = nrm((L, D, D), D ** -0.5)
    d['wk'] = nrm((L, D, D), D ** -0.5)
    d['wv'] = nrm((L, D, D), D ** -0.5)
    d['wo'] = nrm((L, D, D), D ** -0.5)
    d['norm_ffn'] = 1.0 + nrm((L, D), 0.02)
    d['w_up'] = nrm((L, D, 2 * FFN_W), D ** -0.5)
    d['ffn_conv_w'] = nrm((L, FFN_K, 2 * FFN_W), FFN_K ** -0.5)
    d['w_down'] = nrm((L, FFN_W, D), FFN_W ** -0.5)
    d['norm_final'] = 1.0 + nrm((D,), 0.02)
    return d

def reference(x_prompt, x_sample, mem_prompt, state_shift, state_wkv, state_conv, state_ffn,
              cache_mem_k, cache_mem_v, norm_mix, w_in, mu_shift, w0, w2, a0, a2, g2, v0, v1, v2,
              k_k, k_a, r_k, ln_x_w, ln_x_b, conv_w, w_out, norm_x, norm_mem, wq, wk, wv, wo,
              norm_ffn, w_up, ffn_conv_w, w_down, norm_final):
    P = dict(norm_mix=norm_mix, w_in=w_in, mu_shift=mu_shift, w0=w0, w2=w2, a0=a0, a2=a2, g2=g2,
             v0=v0, v1=v1, v2=v2, k_k=k_k, k_a=k_a, r_k=r_k, ln_x_w=ln_x_w, ln_x_b=ln_x_b,
             conv_w=conv_w, w_out=w_out, norm_x=norm_x, wq=wq, wo=wo, norm_ffn=norm_ffn,
             w_up=w_up, ffn_conv_w=ffn_conv_w, w_down=w_down, norm_final=norm_final)
    Bp, Mp = mem_prompt.shape[0], mem_prompt.shape[1]
    mks, mvs = [], []
    for l in range(DEPTH):
        mn = rmsnorm(mem_prompt, norm_mem[l])
        mks.append((mn @ wk[l]).reshape(Bp, Mp, N_XHEADS, XHEAD_DIM))
        mvs.append((mn @ wv[l]).reshape(Bp, Mp, N_XHEADS, XHEAD_DIM))
    mem_k_p = jnp.stack(mks)
    mem_v_p = jnp.stack(mvs)
    dt = x_prompt.dtype
    shift0 = jnp.zeros((DEPTH, Bp, D_MODEL), dt)
    wkv0 = jnp.zeros((DEPTH, Bp, N_RWKV_HEADS, HEAD_SIZE, HEAD_SIZE), jnp.float32)
    conv0 = jnp.zeros((DEPTH, Bp, CONV_K - 1, CONV_W), dt)
    ffn0 = jnp.zeros((DEPTH, Bp, FFN_K - 1, 2 * FFN_W), dt)
    y_prompt, shift_p, wkv_p, conv_p, ffn_p = trunk(x_prompt, mem_k_p, mem_v_p, shift0, wkv0, conv0, ffn0, P)
    y_sample, shift_s, wkv_s, conv_s, ffn_s = trunk(x_sample, cache_mem_k, cache_mem_v, state_shift, state_wkv, state_conv, state_ffn, P)
    return (y_prompt, y_sample, shift_p, wkv_p, conv_p, ffn_p, mem_k_p, mem_v_p, shift_s, wkv_s, conv_s, ffn_s)


_drawn_inputs = setup_inputs


def setup_inputs(seed=0):
    import zlib

    import numpy as np

    out = dict(_drawn_inputs(seed))
    spreads = {}
    factors = {'k_k': 8.0,
     'k_a': 2.68,
     'ln_x_w': 8.0,
     'ln_x_b': 8.0,
     'norm_x': 8.0,
     'norm_mem': 2.729,
     'norm_ffn': 2.851}
    for name, (base, spread) in spreads.items():
        noise = np.random.default_rng([zlib.crc32(name.encode()), seed]).standard_normal(out[name].shape)
        drawn = base * np.exp(spread * noise) if base else spread * noise
        out[name] = __import__('jax').numpy.asarray(drawn.astype(out[name].dtype))
    for name, factor in factors.items():
        out[name] = (out[name] * factor).astype(out[name].dtype)
    return out
```

```python
from contextlib import ExitStack, contextmanager

import numpy as np

import concourse.bass as bass
from concourse import mybir

F32 = mybir.dt.float32
F32R = mybir.dt.float32r
U8 = mybir.dt.uint8
BF16 = mybir.dt.bfloat16
ACT = mybir.ActivationFunctionType
ALU = mybir.AluOpType
AX = mybir.AxisListType

P = 128
D = 1024
KT = D // P
SEQ = 2048
TB = 512
NB = SEQ // TB
TT = TB // P
B = 8
H, N = 8, 64
NP = H // 2
C = 64
NC = TB // C
RW = H * N
NRW = 14
NIN = 26
NMEM = 256
NXH = 4
FFN = 2816
NF = FFN // P
EPS = 1e-6
GN_EPS = N * 1e-5
DECAY = float(np.exp(-0.5))
XSCALE = 1.0 / 16
MERGES = (1, 2, 4, 8, 16, 32)

PAR, NPAR = {}, 0
for _n, _k in (("mu_shift", NRW), ("w0", 4), ("a0", 4), ("k_k", 4), ("k_a", 4), ("r_k", 4), ("ln_x_w", 4),
               ("ln_x_b", 4), ("norm_mix", 8), ("norm_x", 8), ("norm_mem", 8), ("norm_ffn", 8),
               ("norm_final", 8), ("conv_w", 12)):
    PAR[_n] = (NPAR, _k)
    NPAR += _k

NLD = len(PAR) + 11

LOOPS = {
    "sync.in": dict(lo_ready0=1, lo_ready1=1),
    "sync.out": dict(lo_ready0=1, lo_ready1=1),
    "sync.q": dict(lo_ready0=1, lo_ready1=1),
    "sync.o": dict(lo_ready0=1, lo_ready1=1),
    "sync.ffn": dict(lo_ready0=3, lo_ready1=3),
    "sync.block": dict(lo_ready0=58, lo_ready1=58, xin_free=1, ws_free=1, y_go0=2, y_go1=2),
    "pool.mem": dict(hi_ready0=1, lo_ready0=1, hi_ready1=1, lo_ready1=1),
    "pool.in": dict(hi_ready0=1, lo_ready0=1, hi_ready1=1, lo_ready1=1),
    "pool.wkv": dict(gch=1, dec_readyG=1, ops_freeG=1),
    "pool.out": dict(hi_ready0=1, lo_ready0=1, hi_ready1=1, lo_ready1=1),
    "pool.q": dict(hi_ready0=1, lo_ready0=1, hi_ready1=1, lo_ready1=1),
    "pool.o": dict(hi_ready0=1, lo_ready0=1, hi_ready1=1, lo_ready1=1),
    "pool.ffn": dict(gch=4, hi_ready0=3, lo_ready0=3, hi_ready1=3, lo_ready1=3, eb_ready0=1, eb_ready1=1,
         eb_ready2=1, eb_ready3=1),
    "pool.block": dict(gch=52, hi_ready0=58, lo_ready0=58, hi_ready1=58, lo_ready1=58, wkv_inG=1, dec_readyG=8,
         ops_freeG=8, eb_ready0=11, eb_ready1=11, eb_ready2=11, eb_ready3=11),
    "pe.mem": dict(lo_ready0=1, free0=1, lo_ready1=1, free1=1),
    "pe.in": dict(lo_ready0=1, free0=1, lo_ready1=1, free1=1),
    "pe.wkv": dict(pool_ops=2, vec_ops0=1, wk_vec0=18, wk_vec1=18, wk_vec2=18, wk_vec3=18, wk_act0=16,
         wk_act1=16, wk_act2=16, wk_act3=16, vec_ops1=1),
    "pe.out": dict(lo_ready0=1, free0=1, lo_ready1=1, free1=1),
    "pe.q": dict(lo_ready0=1, free0=1, lo_ready1=1, free1=1),
    "pe.o": dict(lo_ready0=1, free0=1, lo_ready1=1, free1=1),
    "pe.ffn": dict(lo_ready0=3, free0=3, lo_ready1=3, free1=3, free2=3, free3=3, h_ready=2),
    "pe.block": dict(free4=24, free5=22, free6=22, free7=22, v2p=39, lo_ready0=58, free0=58, x_ready=40,
         lo_ready1=58, free1=58, xin_ready=16, a2p=10, pool_ops=8, vec_ops0=4, wk_vec0=72,
         wk_vec1=72, wk_vec2=72, wk_vec3=72, wk_act0=64, wk_act1=64, wk_act2=64, wk_act3=64,
         vec_ops1=4, kv_ready=32, free2=37, free3=37, h_ready=22),
    "pe.ins": dict(free4=1, free5=1, lo_ready0=1, free0=1, lo_ready1=1, free1=1),
    "pe.outs": dict(free4=1, free5=1, lo_ready0=1, free0=1, lo_ready1=1, free1=1),
    "pe.qs": dict(free4=1, free5=1, lo_ready0=1, free0=1, lo_ready1=1, free1=1),
    "pe.os": dict(free4=1, free5=1, lo_ready0=1, free0=1, lo_ready1=1, free1=1),
    "pe.ffns": dict(free4=2, free5=2, free6=1, v2p=1, lo_ready0=3, free0=3, lo_ready1=3, free1=3, free2=3,
         free3=3, h_ready=2),
    "act.mem": dict(raw_ready0=16, raw_ready1=16, slab_done0=1, slab_done1=1),
    "act.shift": dict(ach=2, raw_ready0=16, raw_ready1=16, slab_done0=1, slab_done1=1, shf_free0=1, shf_free1=1),
    "act.gate_b": dict(raw_ready0=16, raw_ready1=16, slab_done0=1, slab_done1=1),
    "act.gate_c": dict(ach=2, raw_ready0=16, raw_ready1=16, slab_done0=1, slab_done1=1),
    "act.h_in": dict(raw_ready0=16, raw_ready1=16, slab_done0=1, slab_done1=1),
    "act.wkv": dict(dec_freeV=2, dec_freeG=2, wk_mm0=30, wk_mm1=30, wk_mm2=30, wk_mm3=30),
    "act.out": dict(raw_ready0=16, raw_ready1=16, slab_done0=1, slab_done1=1, sq_free=2, xT_new=2),
    "act.q": dict(ach=2, raw_ready0=16, raw_ready1=16, slab_done0=1, slab_done1=1),
    "act.o": dict(raw_ready0=16, raw_ready1=16, slab_done0=1, slab_done1=1, sq_free=2, xT_new=2),
    "act.ffn": dict(ach=4, raw_ready0=48, raw_ready1=48, st_ready=2, slab_done0=3, slab_done1=3, v2a=2,
         eb_free0=1, eb_free1=1, eb_free2=1, eb_free3=1),
    "act.block": dict(ach=103, raw_ready0=928, raw_ready1=928, st_ready=62, slab_done0=58, slab_done1=58,
         fullA4=10, sq_free=40, fullA5=4, fullA6=16, fullA7=16, shf_free0=7, shf_free1=7, v2a=44,
         wkv_inA=1, dec_freeV=8, dec_freeG=8, wk_mm0=120, wk_mm1=120, wk_mm2=120, wk_mm3=120,
         xT_new=17, pT_free=4, eb_free0=11, eb_free1=11, eb_free2=11, eb_free3=11, y_st0=32, y_st1=32),
    "act.ffns": dict(ach=4, raw_ready0=48, raw_ready1=48, st_ready=2, slab_done0=3, slab_done1=3, v2a=3,
         eb_free0=1, eb_free1=1, eb_free2=1, eb_free3=1),
    "dve.mem": dict(vch=2, slab_done0=1, slab_done1=1),
    "dve.shift": dict(vch=2, slab_done0=1, slab_done1=1, shf0=1, shf1=1),
    "dve.gates": dict(slab_done0=1, slab_done1=1),
    "dve.h_in": dict(vch=2, slab_done0=1, slab_done1=1),
    "dve.wkv": dict(vch=34, dec_readyV=2, wk_mm0=30, wk_mm1=30, wk_mm2=30, wk_mm3=30, wk_act0=16, wk_act1=16,
         wk_act2=16, wk_act3=16, wk_vec0=2, wk_vec1=2, wk_vec2=2, wk_vec3=2),
    "dve.out": dict(vch=4, slab_done0=1, slab_done1=1, sq_ready=2),
    "dve.q": dict(slab_done0=1, slab_done1=1),
    "dve.o": dict(vch=4, slab_done0=1, slab_done1=1, sq_ready=2),
    "dve.ffn": dict(vch=20, a2v=2, sthi=2, slab_done0=3, slab_done1=3, st_ready=2, fullV2=2, fullV3=1,
         eb_carry0=1, eb_carry1=1, eb_carry2=1, eb_carry3=1, h_ready=2, fullV0=2, fullV1=2),
    "dve.block": dict(fullV4=13, vch=540, fullV5=17, fullV6=5, fullV7=5, a2v=49, sthi=62, x_ready=40,
         slab_done0=58, slab_done1=58, sq_ready=32, v2p=8, st_ready=50, shf0=7, shf1=7, dec_readyV=8,
         wk_mm0=120, wk_mm1=120, wk_mm2=120, wk_mm3=120, wk_act0=64, wk_act1=64, wk_act2=64,
         wk_act3=64, wk_vec0=8, wk_vec1=8, wk_vec2=8, wk_vec3=8, fullV2=26, fullV3=15, eb_carry0=11,
         eb_carry1=11, eb_carry2=11, eb_carry3=11, h_ready=22, fullV0=22, fullV1=22, y_st0=32,
         y_st1=32),
    "dve.shifts": dict(vch=4, slab_done0=1, slab_done1=1, shf0=1, shf1=1),
    "dve.gatess": dict(vch=2, slab_done0=1, slab_done1=1),
    "dve.h_ins": dict(vch=4, slab_done0=1, slab_done1=1),
    "dve.outs": dict(vch=6, slab_done0=1, slab_done1=1, sq_ready=2),
    "dve.qs": dict(vch=2, slab_done0=1, slab_done1=1),
    "dve.os": dict(vch=6, slab_done0=1, slab_done1=1, sq_ready=2),
    "dve.ffns": dict(vch=40, a2v=3, sthi=2, slab_done0=3, slab_done1=3, st_ready=2, fullV2=2, fullV3=1,
         eb_carry0=1, eb_carry1=1, eb_carry2=1, eb_carry3=1, h_ready=2, fullV0=2, fullV1=2),
}


class Counts:

    def __init__(self, eng, name, passed=None):
        self.eng, self.name, self.passed, self.n, self.turns = eng, name, passed, {}, []

    def __call__(self, sem, k=1):
        v = self.n[sem.name] = self.n.get(sem.name, 0) + k
        for i, per in self.turns:
            if per.get(sem.name):
                v = i * per[sem.name] + v
        return v

    def skip(self, sem, k):
        self.n[sem.name] = self.n.get(sem.name, 0) + k

    @contextmanager
    def loop(self, label, count):
        key = f"{self.name}.{label}"
        per, before = LOOPS.get(key, {}), dict(self.n)
        if self.passed is not None and self.turns:
            self.eng.sem_inc(self.passed, 1)
        with self.eng.Fori(0, count) as i:
            self.turns.append((i, per))
            yield i
            self.turns.pop()
        did = {s: v - before.get(s, 0) for s, v in self.n.items() if v != before.get(s, 0)}
        check_turn(key, per, did)
        for s, d in did.items():
            self.n[s] = before.get(s, 0) + d * count


def check_turn(key, per, did):
    assert per == did, f"{key}: a turn asks for {did}"


def hybrid_decoder_step(nc, I, O):
    ctx = ExitStack()
    with ctx:
        def sb(name, shape, dt=F32):
            return ctx.enter_context(nc.sbuf_tensor(name, shape, dt))

        def sem(name):
            return ctx.enter_context(nc.semaphore(name))

        def sems(name, n):
            return [sem(f"{name}{i}") for i in range(n)]

        psum = ctx.enter_context(nc.psum_tensor("psum", [P, 8, 512], F32))
        par = sb("par", [P, NPAR])
        omu = sb("omu", [P, NRW])
        oka = sb("oka", [P, 4])
        fcw = sb("fcw", [P, 3 * 2 * NF])
        lora_wa = sb("lora_wa", [P, RW])
        lora_g = sb("lora_g", [P, RW])
        ident = sb("ident", [P, P])
        ident64 = sb("ident64", [P, N])
        ones = sb("ones", [P, P])
        ones_bd = sb("ones_bd", [P, P])
        eps = sb("eps", [P, 2])
        gram_mask = sb("gram_mask", [P, 192])
        merge_mask = sb("merge_mask", [P, 6, 2, P], U8)
        scan_mask = sb("scan_mask", [P, NC * (C + 1)], BF16)
        carry = sb("carry", [P, NRW])
        ccarry = sb("ccarry", [P, 4, 2])
        fcarry = sb("fcarry", [P, 2 * NF, 2])

        xT = sb("xT", [P, KT, TB])
        xhi = sb("xhi", [P, KT, TB], F32R)
        xlo = sb("xlo", [P, KT, TB], F32R)
        wraw = [sb(f"wraw{i}", [P, KT, P]) for i in range(2)]
        whi = [sb(f"whi{i}", [P, KT, P], F32R) for i in range(2)]
        wlo = [sb(f"wlo{i}", [P, KT, P], F32R) for i in range(2)]
        stage = sb("stage", [P, 2, TB])
        hhi = sb("hhi", [P, 2, TB], F32R)
        hlo = sb("hlo", [P, 2, TB], F32R)
        zr = sb("zr", [P, NRW * TB])
        cl = sb("cl", [P, 4 * NC * (C + 1)])
        kka = sb("kka", [P, 4, TB])
        kkn_y = sb("kkn_y", [P, 8, TB])
        shifted = sb("shifted", [P, 2, TB + 1])
        ops_b = sb("ops_b", [P, NP, P])
        ops_k = sb("ops_k", [P, NP, P])
        ops_v = sb("ops_v", [P, NP, P])
        ops_ar = [sb(f"ops_ar{i}", [P, NP, 192]) for i in range(2)]
        gC = [sb(f"gC{i}", [P, NP]) for i in range(2)]
        ws = sb("ws", [P, NP * (384 + 512 + 256 + 128)])
        dec = sb("dec", [P, NP, C + 1])
        inv = sb("inv", [P, NP, C])
        S = sb("S", [P, NP, P])
        sm = sb("sm", [P, 96])
        xs = sb("xs", [P, KT, B])
        xsn = sb("xsn", [P, KT, 2 * B])
        xsh = sb("xsh", [P, KT, 2 * B], F32R)
        xsl = sb("xsl", [P, KT, 2 * B], F32R)
        sconv = sb("sconv", [P, 4, 2 * B])
        sffn = sb("sffn", [P, 2 * NF, 2 * B])
        sp = sb("sp", [P, NIN, 2 * B])
        sz = sb("sz", [P, NRW, B])
        sw = sb("sw", [P, 12, 4, B])
        shh = sb("shh", [P, 2, B], F32R)
        shl = sb("shl", [P, 2, B], F32R)
        shn = sb("shn", [P, KT, B + 1])
        sq_s = sb("sq_s", [P, KT, B])
        fin = sb("fin", [P, 176])

        Z = zr[:, :].rearrange("p (m t) -> p m t", m=NRW)
        q_sb = zr[:, 0:8 * TB].rearrange("p (m t) -> p m t", m=8)
        pT = zr[:, 8 * TB:12 * TB].rearrange("p (a m t) -> p a m t", a=2, m=2)
        pr = zr[:, 12 * TB:13 * TB].rearrange("p (a m) -> p a m", a=2)
        eb = zr[:, 0:4 * (TB + 2)].rearrange("p (a t) -> p a t", a=4)
        fc = zr[:, 5 * TB:9 * TB].rearrange("p (a t) -> p a t", a=4)
        yrow = zr[:, 10 * TB:14 * TB].rearrange("p (a d) -> p a d", a=2)
        cb = cl[:, 0:4 * (TB + 2)].rearrange("p (j t) -> p j t", j=4)
        L = cl[:, :].rearrange("p (j c t) -> p j c t", j=4, c=NC)
        Lf = cl[:, :].rearrange("p (j t) -> p j t", j=4)
        kkn, Y = kkn_y[:, 0:4, :], kkn_y[:, 4:8, :]
        kv_flat = kkn_y[:, :, :].rearrange("p a b -> p (a b)")
        xin = kv_flat.rearrange("p (t d) -> p t d", t=TT)
        GM = ws[:, 0:1536].rearrange("p (q a c) -> p q a c", q=NP, a=2)
        TM = ws[:, 1536:3584].rearrange("p (q c) -> p q c", q=NP)
        QT = ws[:, 3584:4608].rearrange("p (q a c) -> p q a c", q=NP, a=2)
        Zs = ws[:, 4608:5120].rearrange("p (q c) -> p q c", q=NP)
        Us = Zs
        kmT = ws[:, 0:8 * NMEM].rearrange("p (m t) -> p m t", m=8)
        Vm = ws[:, 8 * NMEM:16 * NMEM].rearrange("p (m d) -> p m d", m=2)
        qrep = zr[:, 10 * TB:12 * TB]
        gb = ws[:, 0:4 * TB].rearrange("p (j t) -> p j t", j=4)
        sscore = zr[:, 13 * TB:13 * TB + 64].rearrange("p (m c) -> p m c", m=2)
        sprobT = zr[:, 13 * TB + 64:13 * TB + 128]
        sprob = zr[:, 12 * TB:12 * TB + NMEM]
        sup = sp[:, :, :].rearrange("p a b -> p (a b)")[:, 0:2 * NF * B].rearrange("p (m b) -> p m b", b=B)
        acc = shifted[:, 0, 0:TB]
        kT_dram = nc.dram_tensor("mem_kT_scratch", (P, 8 * NMEM), F32, kind="Internal").ap()

        def pcol(name, j, k=1):
            r = PAR[name][0]
            return par[:, bass.ds(r + j, k)]

        def bc(ap, *shape):
            return ap.unsqueeze(len(ap.shape)).broadcast_to(list(shape))

        consts = sem("consts")
        ld = sem("ld")
        fullA, fullV = sems("fullA", 8), sems("fullV", 8)
        free = sems("free", 8)
        raw_ready = sems("raw_ready", 2)
        slab_done = sems("slab_done", 2)
        hi_ready = sems("hi_ready", 2)
        lo_ready = sems("lo_ready", 2)
        st_ready = sem("st_ready")
        sthi = sem("sthi")
        x_ready = sem("x_ready")
        h_ready = sem("h_ready")
        xin_ready, xin_free = sem("xin_ready"), sem("xin_free")
        sq_ready, sq_free = sem("sq_ready"), sem("sq_free")
        xT_new = sem("xT_new")
        v2a, a2v = sem("v2a"), sem("a2v")
        v2p, a2p = sem("v2p"), sem("a2p")
        wkv_inA, wkv_inG = sem("wkv_inA"), sem("wkv_inG")
        dec_readyV, dec_readyG = sem("dec_readyV"), sem("dec_readyG")
        dec_freeV, dec_freeG = sem("dec_freeV"), sem("dec_freeG")
        pool_ops, vec_ops = sem("pool_ops"), sems("vec_ops", 2)
        ops_freeG = sem("ops_freeG")
        wk_mm, wk_act, wk_vec = sems("wk_mm", NP), sems("wk_act", NP), sems("wk_vec", NP)
        shf, shf_free = sems("shf", 2), sems("shf_free", 2)
        ws_free = sem("ws_free")
        kv_ready = sem("kv_ready")
        eb_ready = sems("eb_ready", 4)
        eb_carry = sems("eb_carry", 4)
        eb_free = sems("eb_free", 4)
        pT_free = sem("pT_free")
        y_go, y_st = sems("y_go", 2), sems("y_st", 2)
        out_go, out_st = sem("out_go"), sem("out_st")
        cache_in, cache_free = sems("cache_in", 2), sems("cache_free", 2)
        cache_done = sems("cache_done", 2)
        s_state = sem("s_state")
        passedA, passedG, passedV = sem("passedA"), sem("passedG"), sem("passedV")
        vch, ach, gch = sem("vch"), sem("ach"), sem("gch")

        block = ctx.enter_context(nc.Block())

        def cols(w, m):
            return w[:, bass.ds(m * P, P)].rearrange("(k p) c -> p k c", p=P)

        w_in, w_out, wq, wk, wv, wo = (I[n][0] for n in ("w_in", "w_out", "wq", "wk", "wv", "wo"))
        w_up, w_down = I["w_up"][0], I["w_down"][0]

        @block.sync
        def _(e):
            c = Counts(e, "sync")

            def slab(i, src, first=False):
                if not first:
                    e.wait_ge(lo_ready[i], c(lo_ready[i]))
                e.dma_start(wraw[i][:, :, :], src).then_inc(raw_ready[i], 16)

            for name, (r, k) in PAR.items():
                src = I[name]
                if name == "conv_w":
                    src = src[0].rearrange("t (j p) -> (t j) p", p=P)
                elif name == "norm_final":
                    src = src.rearrange("(j p) -> j p", p=P)
                else:
                    src = src[0].rearrange("(j p) -> j p", p=P)
                e.dma_start(xT[r:r + k, 0, 0:P], src).then_inc(ld, 16)
            fw = I["ffn_conv_w"][0].rearrange("t (j p) -> (t j) p", p=P)
            e.dma_start(xT[:, 1, 0:P], fw[0:P, :]).then_inc(ld, 16)
            e.dma_start(xT[0:4, 2, 0:P], fw[P:3 * 2 * NF, :]).then_inc(ld, 16)
            e.dma_start(lora_wa[0:64, :], I["w2"][0]).then_inc(ld, 16)
            e.dma_start(lora_wa[64:128, :], I["a2"][0]).then_inc(ld, 16)
            e.dma_start(lora_g[:, :], I["g2"][0]).then_inc(ld, 16)
            for t in range(2):
                e.dma_start(xin[:, t, :], I["mem_prompt"][0, t * P:(t + 1) * P, :]).then_inc(ld, 16)
            e.dma_start(xin[0:B, 2, :], I["x_sample"][:, 0, :]).then_inc(ld, 16)
            e.dma_start(xin[B:2 * B, 2, :], I["state_shift"][0]).then_inc(ld, 16)
            e.dma_start(xin[0:2 * B, 3, 0:RW], I["state_conv"][0].rearrange("b r c -> (b r) c")).then_inc(ld, 16)
            e.dma_start(zr[0:2 * B, 0:2 * FFN], I["state_ffn"][0].rearrange("b r c -> (b r) c")).then_inc(ld, 16)
            for s in range(16):
                slab(s % 2, cols(wk if s < 8 else wv, s % 8), s < 2)

            def load_x(b):
                e.wait_ge(xin_free, c(xin_free))
                e.dma_start(xin, I["x_prompt"][0][bass.ds(b * TB, TB), :].rearrange("(t p) d -> p t d", p=P)
                            ).then_inc(xin_ready, 16)

            def ffn_up(i):
                for j in range(2):
                    slab(0, cols(w_up, 2 * i + j))
                    slab(1, cols(w_up, 2 * i + NF + j))

            def ffn_down(i):
                for j in range(2):
                    slab(j, w_down[bass.ds((2 * i + j) * P, P), :].rearrange("p (k c) -> p k c", k=KT))

            def one_block(b, last):
                with c.loop("in", NIN // 2 - 1) as i:
                    for j in range(2):
                        slab(j, cols(w_in, 2 * i + 2 + j))
                for name, w in (("out", w_out), ("q", wq), ("o", wo)):
                    for j in range(2):
                        slab(j, cols(w, j))
                    if name == "out":
                        memory_and_state(last)
                    if name == "o" and last:
                        sample_caches()
                    with c.loop(name, KT // 2 - 1) as i:
                        for j in range(2):
                            slab(j, cols(w, 2 * i + 2 + j))
                if not last:
                    load_x(b + 1)
                ffn_up(0)
                with c.loop("ffn", NF // 2 - 1) as i:
                    ffn_up(i + 1)
                    ffn_down(i)
                ffn_down(NF // 2 - 1)
                if not last:
                    for j in range(2):
                        slab(j, cols(w_in, j))
                for t in range(TT):
                    e.wait_ge(y_go[t % 2], c(y_go[t % 2]))
                    e.dma_start(O["y_prompt"][0][bass.ds(b * TB + t * P, P), :], yrow[:, t % 2, :]
                                ).then_inc(y_st[t % 2], 16)

            def memory_and_state(last):
                e.wait_ge(ws_free, c(ws_free))
                e.dma_start(ws[:, 0:8 * NMEM], kT_dram).then_inc(kv_ready, 16)
                e.dma_start(Vm, O["mem_v_p"][0, 0].rearrange("(m p) h d -> p m (h d)", p=P)
                            ).then_inc(kv_ready, 16)
                if last:
                    for h in range(2):
                        for s in range(2):
                            src = I["state_wkv"][0, 4 * s:4 * s + 4].rearrange("b (q h) v k -> h v q b k", h=2)[h]
                            dst = cl[64 * h:64 * h + 64, 0:2048].rearrange("v (q b k) -> v q b k", q=NP, b=B)
                            for q in range(NP):
                                e.dma_start(dst[:, q, 4 * s:4 * s + 4, :], src[:, q]).then_inc(s_state, 16)

            def sample_caches():
                for n, name in enumerate(("cache_mem_k", "cache_mem_v")):
                    for b in range(B):
                        e.wait_ge(cache_free[b % 2], c(cache_free[b % 2]))
                        e.dma_start(kv_flat[:, (b % 2) * 2048:(b % 2 + 1) * 2048].rearrange("p (m d) -> p m d", m=2),
                                    I[name][0, b].rearrange("(m p) h d -> p m (h d)", p=P)
                                    ).then_inc(cache_in[b % 2], 16)

            for n in range(2):
                e.wait_ge(out_go, c(out_go))
                e.dma_start(O["mem_v_p" if n else "mem_k_p"][0, 0].rearrange("(m p) h d -> p m (h d)", p=P),
                            kv_flat[:, n * 2048:(n + 1) * 2048].rearrange("p (m d) -> p m d", m=2)
                            ).then_inc(out_st, 16)
            e.dma_start(kT_dram, zr[:, 8 * NMEM:16 * NMEM]).then_inc(out_st, 16)
            e.wait_ge(out_st, c(out_st, 48))
            for j in range(2):
                slab(j, cols(w_in, j))
            load_x(0)
            with c.loop("block", NB - 1) as b:
                one_block(b, False)
            one_block(NB - 1, True)

            def put(dst, src):
                e.dma_start(dst, src).then_inc(out_st, 16)

            put(O["conv_s"][0, :, 0, :], I["state_conv"][0, :, 1, :])
            put(O["ffn_s"][0, :, 0, :], I["state_ffn"][0, :, 1, :])
            e.wait_ge(out_go, c(out_go))
            def rows(a, n):
                return zr[0:n, a:a + 8 * P].rearrange("m (b p) -> m b p", b=8)

            put(O["ffn_s"][0, :, 1, :].rearrange("b (m p) -> m b p", p=P), rows(0, 2 * NF))
            put(O["conv_s"][0, :, 1, :].rearrange("b (j p) -> j b p", p=P), rows(8 * P, 4))
            put(O["ffn_p"][0, 0].rearrange("r (m p) -> m r p", p=P), rows(16 * P, 2 * NF)[:, 0:2, :])
            put(O["shift_s"][0].rearrange("b (k p) -> (b k) p", p=P), zr[0:64, 18 * P:19 * P])
            put(O["y_sample"][:, 0, :].rearrange("b (k p) -> (b k) p", p=P), zr[0:64, 19 * P:20 * P])
            put(O["shift_p"][0, 0].rearrange("(k p) -> k p", p=P), zr[0:8, 20 * P:21 * P])
            put(O["conv_p"][0, 0].rearrange("r (j p) -> (r j) p", p=P), zr[0:8, 21 * P:22 * P])
            for h in range(2):
                put(O["wkv_p"][0, 0].rearrange("(q h) v k -> h v q k", h=2)[h],
                    zr[64 * h:64 * h + 64, 22 * P:26 * P].rearrange("v (q x) -> v q x", q=NP)[:, :, 64 * h:64 * h + 64])
                for q in range(NP):
                    put(O["wkv_s"][0].rearrange("b (q h) v k -> h q v b k", h=2)[h, q],
                        cl[64 * h:64 * h + 64, 0:2048].rearrange("v (q b k) -> v q b k", q=NP, b=B)[:, q])
            e.wait_ge(out_st, c(out_st, 16 * 19))
            e.wait_ge(y_st[0], c(y_st[0], 16 * NB * TT // 2))
            e.wait_ge(y_st[1], c(y_st[1], 16 * NB * TT // 2))

        @block.gpsimd
        def _(e):
            c = Counts(e, "pool", passedG)
            last = [0]

            def select(dst, src, op, fill, base, pattern, ch):
                e.affine_select(out=dst, in_=src, compare_op=op, fill=fill, base=base, pattern=pattern,
                                channel_multiplier=ch).then_inc(gch, 1)
                e.wait_ge(gch, c(gch))

            for t, v in ((ident, 0.0), (ones, 1.0), (ones_bd, 0.0), (S, 0.0), (carry, 0.0), (ccarry, 0.0),
                         (fcarry, 0.0), (gram_mask, 1.0), (ident64, 0.0),
                         (scan_mask, 1.0), *((t, 0.0) for t in (ops_b, ops_k, ops_v, *ops_ar))):
                e.memset(t[:], v).then_inc(gch, 1)
                e.wait_ge(gch, c(gch))
            e.memset(eps[:, 0:1], EPS).then_inc(gch, 1)
            e.wait_ge(gch, c(gch))
            e.memset(eps[:, 1:2], GN_EPS).then_inc(gch, 1)
            e.wait_ge(gch, c(gch))
            e.memset(scan_mask[:, :].rearrange("p (c t) -> p c t", c=NC)[:, :, 0:1], 0.0).then_inc(gch, 1)
            e.wait_ge(gch, c(gch))
            select(ident[:, :], ident[:, :], ALU.not_equal, 1.0, 0, [[-1, P]], 1)
            for h in range(2):
                a = slice(64 * h, 64 * h + 64)
                e.memset(ones_bd[a, a], 1.0).then_inc(gch, 1)
                e.wait_ge(gch, c(gch))
                select(ident64[a, :], ident64[a, :], ALU.not_equal, 1.0, 0, [[-1, N]], 1)
                e.memset(gram_mask[a, 64 * (1 - h):64 * (1 - h) + 64], 0.0).then_inc(gch, 1)
                e.wait_ge(gch, c(gch))
                select(gram_mask[a, a], gram_mask[a, a], ALU.is_gt, 0.0, 0, [[1, N]], -1)
                select(gram_mask[a, 128:192], gram_mask[a, 128:192], ALU.is_ge, 0.0, 0, [[1, N]], -1)
            for l, m in enumerate(MERGES):
                for side in range(2):
                    t, inner = stage[:, 1, 0:P], stage[:, 0, 0:P]
                    e.memset(t, 1.0).then_inc(gch, 1)
                    e.wait_ge(gch, c(gch))
                    e.memset(inner, 1.0).then_inc(gch, 1)
                    e.wait_ge(gch, c(gch))
                    for dst, w in ((t, 2 * m), (inner, m)):
                        v = dst.rearrange("p (q w) -> p q w", w=w)
                        select(v, v, ALU.is_ge, 0.0, 0, [[-w, P // w], [0, w]], 1)
                        select(v, v, ALU.is_ge, 0.0, w - 1, [[w, P // w], [0, w]], -1)
                    e.tensor_tensor(t, t, inner, ALU.subtract).then_inc(gch, 1)
                    e.wait_ge(gch, c(gch))
                    select(t, t, ALU.is_gt, 0.0, 0, [[-1 if side else 1, P]], 1 if side else -1)
                    e.tensor_copy(merge_mask[:, l, side, :], t).then_inc(gch, 1)
                    e.wait_ge(gch, c(gch))
            for i in range(2):
                e.sem_inc(shf_free[i], 1)
            for s in (dec_freeV, dec_freeG, ops_freeG):
                e.sem_inc(s, 1)
            for i in range(8):
                e.sem_inc(free[i], 1)
            for i in range(4):
                e.sem_inc(eb_free[i], 1)
            e.sem_inc(consts, 1)

            def split(i):
                e.wait_ge(hi_ready[i], c(hi_ready[i]))
                c.skip(lo_ready[i], 1)
                return e.tensor_tensor(wlo[i][:, :, :], wraw[i][:, :, :], whi[i][:, :, :].bitcast(F32),
                                       ALU.subtract).then_inc(lo_ready[i], 1)

            def splits(label, pairs):
                with c.loop(label, pairs):
                    split(0)
                    split(1)

            def operands(t0):
                e.wait_ge(dec_readyG, c(dec_readyG))
                e.sem_inc(passedG, 1)
                e.wait_ge(ops_freeG, c(ops_freeG))
                e.sem_inc(passedG, 1)
                for h in range(2):
                    a = slice(64 * h, 64 * h + 64)
                    e.tensor_tensor(ops_b[a, :, a], kka[a, :, bass.ds(t0, C)], inv[a, :, :], ALU.mult)
                    ins = e.tensor_tensor(ops_k[a, :, a], Z[a, 4:8, bass.ds(t0, C)], inv[a, :, :], ALU.mult)
                    if h:
                        ins.then_inc(dec_freeG, 1)
                    ins = e.tensor_copy(ops_v[a, :, a], Z[a, 8:12, bass.ds(t0, C)])
                ins.then_inc(gch, 1)
                e.wait_ge(gch, c(gch))
                e.sem_inc(pool_ops, 1)

            def carries(a, tile):
                e.wait_ge(eb_ready[a], c(eb_ready[a]))
                e.sem_inc(passedG, 1)
                e.tensor_copy(eb[:, a, 0:2], fcarry[:, bass.ds(tile, 1), :].rearrange("p a b -> p (a b)")).then_inc(gch, 1)
                e.wait_ge(gch, c(gch))
                e.sem_inc(passedG, 1)
                e.tensor_copy(fcarry[:, bass.ds(tile, 1), :].rearrange("p a b -> p (a b)"),
                              eb[:, a, TB:TB + 2]).then_inc(eb_carry[a], 1)

            def up(i, more):
                for a, tile in ((0, 2 * i), (1, 2 * i + NF), (2, 2 * i + 1), (3, 2 * i + NF + 1)):
                    carries(a, tile)
                    if more:
                        split(a % 2)

            def one_block(b, last):
                splits("in", NIN // 2)
                e.wait_ge(lo_ready[1], c(lo_ready[1], 0))
                e.wait_ge(wkv_inG, c(wkv_inG))
                operands(0)
                with c.loop("wkv", NC - 1) as j:
                    operands(j * C + C)
                splits("out", KT // 2)
                splits("q", KT // 2)
                splits("o", KT // 2)
                up(0, True)
                with c.loop("ffn", NF // 2 - 1) as i:
                    up(i + 1, True)
                    split(0)
                    split(1)
                if not last:
                    split(0)
                    split(1)

            split(0)
            split(1)
            splits("mem", 8)
            with c.loop("block", NB - 1) as b:
                one_block(b, False)
            one_block(NB - 1, True)

        @block.tensor
        def _(e):
            c = Counts(e, "pe")

            def mm(out, lhsT, rhs, start=True, stop=True):
                return e.matmul(out, lhsT, rhs, start=start, stop=stop)

            def tr(out, src):
                n = src.shape[0]
                return e.transpose(out, src, ident[0:n, 0:n])

            def three(out, i, k, hi, lo, start, stop):
                mm(out, whi[i][:, k, :], hi, start, False)
                mm(out, whi[i][:, k, :], lo, False, False)
                return mm(out, wlo[i][:, k, :], hi, False, stop)

            def dense(i, bk, sample=0, order=None, n=TB):
                e.wait_ge(lo_ready[i], c(lo_ready[i]))
                e.wait_ge(free[bk], c(free[bk]))
                if sample:
                    e.wait_ge(free[4 + i], c(free[4 + i]))
                    for k in range(KT):
                        three(psum[:, 4 + i, 0:sample], i, k, xsh[:, k, 0:sample], xsl[:, k, 0:sample],
                              k == 0, k == KT - 1)
                for j, k in enumerate(order or range(KT)):
                    if order:
                        e.wait_ge(x_ready, c(x_ready))
                    ins = three(psum[:, bk, 0:n], i, k, xhi[:, k, 0:n], xlo[:, k, 0:n], j == 0, j == KT - 1)
                ins.then_inc(slab_done[i], 1)

            def phase(label, pairs, sample=0, order=tuple(range(KT)), n=TB):
                if sample:
                    e.wait_ge(v2p, c(v2p))
                dense(0, 0, sample, order, n)
                dense(1, 1, sample, None, n)
                if pairs > 1:
                    with c.loop(label + "s" * bool(sample), pairs - 1):
                        dense(0, 0, sample, None, n)
                        dense(1, 1, sample, None, n)

            def stats():
                e.wait_ge(v2p, c(v2p))
                e.wait_ge(free[4], c(free[4]))
                for t in range(TT):
                    ins = mm(psum[:, 4, t:t + 1], acc[:, t * P:(t + 1) * P], ones[:, 0:1])
                ins.then_inc(fullA[4], 1)
                e.wait_ge(v2p, c(v2p))
                e.wait_ge(free[5], c(free[5]))
                for t in range(TT):
                    ins = tr(psum[:, 5, t * P:(t + 1) * P], sm[:, 4 + t:5 + t].broadcast_to([P, P]))
                ins.then_inc(fullV[5], 1)

            def sample_stats():
                e.wait_ge(v2p, c(v2p))
                e.wait_ge(free[6], c(free[6]))
                mm(psum[:, 6, 0:B], ones[:, :], sw[:, 11, 0, :]).then_inc(fullA[6], 1)

            e.wait_ge(consts, c(consts))
            e.wait_ge(ld, c(ld, 16 * NLD))
            e.wait_ge(free[4], c(free[4]))
            tr(psum[:, 4, 0:NPAR], xT[0:NPAR, 0, 0:P]).then_inc(fullV[4], 1)
            e.wait_ge(free[5], c(free[5]))
            tr(psum[:, 5, 0:P], xT[:, 1, 0:P])
            tr(psum[:, 5, P:P + 4], xT[0:4, 2, 0:P]).then_inc(fullV[5], 1)
            e.wait_ge(free[6], c(free[6]))
            for k in range(KT):
                tr(psum[:, 6, 16 * k:16 * k + 16], xin[0:16, 2, k * P:(k + 1) * P])
            for k in range(4):
                ins = tr(psum[:, 6, 128 + 16 * k:144 + 16 * k], xin[0:16, 3, k * P:(k + 1) * P])
            ins.then_inc(fullV[6], 1)
            for g in range(2):
                e.wait_ge(free[7], c(free[7]))
                for m in range(22):
                    a = (22 * g + m) * P
                    ins = tr(psum[:, 7, 16 * m:16 * m + 16], zr[0:16, a:a + P])
                ins.then_inc(fullV[7], 1)
            e.wait_ge(v2p, c(v2p))
            for k in range(KT):
                bk = 4 + k % 4
                e.wait_ge(free[bk], c(free[bk]))
                for t in range(2):
                    ins = tr(psum[:, bk, t * P:(t + 1) * P], xin[:, t, k * P:(k + 1) * P])
                ins.then_inc(fullV[bk], 1)
            phase("mem", 8, n=NMEM)
            for kv in range(2):
                e.wait_ge(v2p, c(v2p))
                for t in range(2):
                    for g in range(2):
                        bk = 4 + 2 * t + g
                        e.wait_ge(free[bk], c(free[bk]))
                        for k in range(4):
                            a = (8 + 8 * kv + 4 * g + k) * NMEM + t * P
                            ins = tr(psum[:, bk, k * P:(k + 1) * P], zr[:, a:a + P])
                        ins.then_inc(fullV[bk], 1)

            def wkv_chunk(i, first=False):
                e.wait_ge(pool_ops, c(pool_ops))
                e.wait_ge(vec_ops[i], c(vec_ops[i]))
                for p in range(NP):
                    if not first:
                        e.wait_ge(wk_vec[p], c(wk_vec[p]))
                    mm(psum[:, 4 + p, 0:192], ops_b[:, p, :], ops_ar[i][:, p, :])
                    mm(psum[:, 4 + p, 192:384], ops_k[:, p, :], ops_ar[i][:, p, :]).then_inc(wk_mm[p], 1)
                for p in range(NP):
                    e.wait_ge(wk_vec[p], c(wk_vec[p]))
                    for j, src in enumerate((ops_b[:, p, :], ops_k[:, p, :], ops_v[:, p, :], GM[:, p, 0, 0:P])):
                        ins = tr(psum[:, 4 + p, j * P:(j + 1) * P], src)
                    ins.then_inc(wk_mm[p], 1)
                for l in range(1, len(MERGES)):
                    for p in range(NP):
                        if l == 1:
                            e.wait_ge(wk_act[p], c(wk_act[p]))
                        e.wait_ge(wk_vec[p], c(wk_vec[p]))
                        mm(psum[:, 4 + p, 0:P], TM[:, p, 384:512], QT[:, p, 0, :]).then_inc(wk_mm[p], 1)
                    for p in range(NP):
                        e.wait_ge(wk_act[p], c(wk_act[p]))
                        ins = mm(psum[:, 4 + p, 0:P], QT[:, p, 1, :], Zs[:, p, :])
                        if l < len(MERGES) - 1:
                            ins = mm(psum[:, 4 + p, P:2 * P], Zs[:, p, :], QT[:, p, 1, :])
                        ins.then_inc(wk_mm[p], 1)
                for p in range(NP):
                    e.wait_ge(wk_vec[p], c(wk_vec[p]))
                    mm(psum[:, 4 + p, 0:P], ops_ar[i][:, p, 0:P], S[:, p, :], True, False)
                    mm(psum[:, 4 + p, 0:P], GM[:, p, 1, 0:P], TM[:, p, 256:384], False, True).then_inc(wk_mm[p], 1)
                for p in range(NP):
                    e.wait_ge(wk_act[p], c(wk_act[p]))
                    mm(psum[:, 4 + p, 0:P], QT[:, p, 0, :], Zs[:, p, :]).then_inc(wk_mm[p], 1)
                for p in range(NP):
                    e.wait_ge(wk_vec[p], c(wk_vec[p]))
                    y, s = psum[:, 4 + p, 0:C], psum[:, 4 + p, P:2 * P]
                    mm(y, S[:, p, :], ops_ar[i][:, p, P:192], True, False)
                    mm(y, Us[:, p, :], GM[:, p, 0, P:192], False, False)
                    mm(y, TM[:, p, 256:384], GM[:, p, 1, P:192], False, True)
                    mm(s, TM[:, p, 0:P], Us[:, p, :], True, False)
                    mm(s, TM[:, p, P:2 * P], TM[:, p, 256:384], False, True).then_inc(wk_mm[p], 1)
                    c.skip(wk_act[p], 1)

            def attention():
                e.wait_ge(kv_ready, c(kv_ready, 32))
                units = [(h, t) for h in range(NXH) for t in range(TT)]

                def scores(n):
                    h, t = units[n]
                    bk = 4 + n % 2
                    e.wait_ge(free[bk], c(free[bk]))
                    for d in range(2):
                        ins = mm(psum[:, bk, 0:NMEM], q_sb[:, 2 * h + d, t * P:(t + 1) * P], kmT[:, 2 * h + d, :],
                                 d == 0, d == 1)
                    ins.then_inc(fullV[bk], 1)

                e.wait_ge(a2p, c(a2p))
                scores(0)
                for n, (h, t) in enumerate(units):
                    if n + 1 < len(units):
                        scores(n + 1)
                    bk = 6 + n % 2
                    e.wait_ge(v2p, c(v2p))
                    e.wait_ge(free[bk], c(free[bk]))
                    for m in range(2):
                        ins = tr(psum[:, bk, m * P:(m + 1) * P], pr[:, n % 2, m * P:(m + 1) * P])
                    ins.then_inc(fullA[bk], 1)
                    if t == TT - 1:
                        e.wait_ge(a2p, c(a2p))
                        for d in range(2):
                            e.wait_ge(free[2 + d], c(free[2 + d]))
                            for m in range(2):
                                a = (2 * h + d) * P
                                ins = mm(psum[:, 2 + d, :], Vm[:, m, a:a + P], pT[:, h % 2, m, :], m == 0, m == 1)
                            ins.then_inc(fullV[2 + d], 1)

            def ffn_up(sample, order=None):
                for j in range(2):
                    dense(0, 2 * j, sample, order if j == 0 else None)
                    dense(1, 2 * j + 1, sample)

            def ffn_down(sample):
                e.wait_ge(h_ready, c(h_ready, 2))
                e.wait_ge(lo_ready[0], c(lo_ready[0]))
                e.wait_ge(lo_ready[1], c(lo_ready[1]))
                if sample:
                    e.wait_ge(v2p, c(v2p))
                    e.wait_ge(free[6], c(free[6]))
                    for k in range(KT):
                        for j in range(2):
                            three(psum[:, 6, k * B:(k + 1) * B], j, k, shh[:, j, :], shl[:, j, :], j == 0, j == 1)
                for k in range(KT):
                    e.wait_ge(free[k % 4], c(free[k % 4]))
                    ins = three(psum[:, k % 4, :], 0, k, hhi[:, 0, :], hlo[:, 0, :], True, False)
                    if k == KT - 1:
                        ins.then_inc(slab_done[0], 1)
                    ins = three(psum[:, k % 4, :], 1, k, hhi[:, 1, :], hlo[:, 1, :], False, True)
                    ins.then_inc(slab_done[1] if k == KT - 1 else fullV[k % 4], 1)

            def one_block(b, last):
                e.wait_ge(xin_ready, c(xin_ready, 16))
                for k in range(KT):
                    bk = 4 + k % 4
                    e.wait_ge(free[bk], c(free[bk]))
                    for t in range(TT):
                        ins = tr(psum[:, bk, t * P:(t + 1) * P], xin[:, t, k * P:(k + 1) * P])
                    ins.then_inc(fullA[bk], 1)
                stats()
                if last:
                    sample_stats()
                phase("in", NIN // 2, 2 * B if last else 0)
                e.wait_ge(a2p, c(a2p))
                for n in range(8):
                    p, bk = n // 2, 4 + n % 4
                    a = slice(64 * (n % 2), 64 * (n % 2) + 64)
                    e.wait_ge(free[bk], c(free[bk]))
                    mm(psum[:, bk, :], lora_wa[a, p * P:(p + 1) * P], Z[a, 12, :]).then_inc(fullA[bk], 1)
                e.wait_ge(v2p, c(v2p))
                e.wait_ge(free[4], c(free[4]))
                sq = (stage[:, 0, :], stage[:, 1, :], shifted[:, 0, 0:TB], shifted[:, 1, 0:TB])
                for p in range(NP):
                    for t in range(TT):
                        ins = mm(psum[:, 4, 8 * p + 2 * t:8 * p + 2 * t + 2], sq[p][:, t * P:(t + 1) * P], ones_bd[:, 0:P:N])
                ins.then_inc(fullA[4], 1)
                e.wait_ge(v2p, c(v2p))
                head_rows(8)
                for p in range(NP):
                    e.wait_ge(free[4 + p], c(free[4 + p]))
                wkv_chunk(0, True)
                with c.loop("wkv", NC // 2 - 1):
                    wkv_chunk(1)
                    wkv_chunk(0)
                wkv_chunk(1)
                for p in range(NP):
                    e.wait_ge(wk_vec[p], c(wk_vec[p]))
                    e.sem_inc(free[4 + p], 1)
                for p in range(NP):
                    e.wait_ge(v2p, c(v2p))
                    e.wait_ge(free[4 + p], c(free[4 + p]))
                    mm(psum[:, 4 + p, :], ones_bd[:, :], shifted[:, p % 2, 0:TB]).then_inc(fullV[4 + p], 1)
                for p in range(NP):
                    e.wait_ge(free[4 + p], c(free[4 + p]))
                    mm(psum[:, 4 + p, :], ones_bd[:, :], Y[:, p, :]).then_inc(fullV[4 + p], 1)
                e.wait_ge(a2p, c(a2p, NP))
                e.wait_ge(free[4], c(free[4]))
                for p in range(NP):
                    for t in range(TT):
                        ins = mm(psum[:, 4, 8 * p + 2 * t:8 * p + 2 * t + 2], kkn[:, p, t * P:(t + 1) * P], ones_bd[:, 0:P:N])
                ins.then_inc(fullA[4], 1)
                e.wait_ge(v2p, c(v2p))
                head_rows(8)
                for p in range(NP):
                    e.wait_ge(free[4 + p], c(free[4 + p]))
                    mm(psum[:, 4 + p, :], lora_g[:, p * P:(p + 1) * P], Z[:, 13, :]).then_inc(fullV[4 + p], 1)
                if last:
                    sample_wkv()
                phase("out", KT // 2, B if last else 0, (4, 5, 6, 7, 0, 1, 2, 3))
                stats()
                if last:
                    sample_stats()
                phase("q", KT // 2, B if last else 0)
                attention()
                if last:
                    sample_attention()
                phase("o", KT // 2, B if last else 0)
                stats()
                if last:
                    sample_stats()
                s = B if last else 0
                if s:
                    e.wait_ge(v2p, c(v2p))
                ffn_up(s, tuple(range(KT)))
                with c.loop("ffn" + "s" * last, NF // 2 - 1):
                    ffn_up(s)
                    ffn_down(s)
                ffn_down(s)
                stats()
                for t in range(TT):
                    for g in range(2):
                        bk = 6 + g
                        e.wait_ge(free[bk], c(free[bk]))
                        for k in range(4):
                            if t == 0:
                                e.wait_ge(v2p, c(v2p))
                            ins = tr(psum[:, bk, k * P:(k + 1) * P], xT[:, 4 * g + k, t * P:(t + 1) * P])
                        ins.then_inc(fullA[bk], 1)
                if last:
                    sample_stats()

            def head_rows(col):
                for p in range(NP):
                    e.wait_ge(free[4 + p], c(free[4 + p]))
                    for t in range(TT):
                        for h in range(2):
                            a = col + 32 + 8 * p + 2 * t + h
                            ins = mm(psum[64 * h:64 * h + 64, 4 + p, t * P:(t + 1) * P],
                                     sm[:, a:a + 1].broadcast_to([P, N]), ident[:, :])
                    ins.then_inc(fullV[4 + p], 1)

            def sample_wkv():
                e.wait_ge(a2p, c(a2p))
                e.wait_ge(free[6], c(free[6]))
                e.wait_ge(free[7], c(free[7]))
                for j in range(2):
                    a = slice(64 * j, 64 * j + 64)
                    for p in range(NP):
                        ins = mm(psum[:, 6 + j, 8 * p:8 * p + 8], lora_wa[a, p * P:(p + 1) * P], sz[a, 12, :])
                ins.then_inc(fullA[7], 1)
                for p in range(NP):
                    ins = mm(psum[:, 6, 64 + 8 * p:72 + 8 * p], lora_g[:, p * P:(p + 1) * P], sz[:, 13, :])
                ins.then_inc(fullA[6], 1)

                def head_sum():
                    e.wait_ge(v2p, c(v2p))
                    e.wait_ge(free[7], c(free[7]))
                    return mm(psum[:, 7, 0:4 * B], ones_bd[:, :], sw[:, 11, :, :].rearrange("p a b -> p (a b)"))

                head_sum().then_inc(fullA[7], 1)
                for j in range(5):
                    e.wait_ge(v2p, c(v2p))
                    for g in range(4):
                        e.wait_ge(free[4 + g], c(free[4 + g]))
                        ins = mm(psum[:, 4 + g, :], ones_bd[:, :],
                                 kkn_y[:, g, :])
                    ins.then_inc(fullV[7], 1)
                head_sum().then_inc(fullV[7], 1)
                head_sum().then_inc(fullV[7], 1)
                head_sum().then_inc(fullA[7], 1)

            def sample_attention():
                for b in range(B):
                    e.wait_ge(v2p, c(v2p))
                    for g in range(2):
                        e.wait_ge(free[4 + g], c(free[4 + g]))
                        ins = mm(psum[:, 4 + g, :], ones[:, :], zr[:, 8 * TB + g * TB:8 * TB + (g + 1) * TB])
                    ins.then_inc(fullV[5], 1)
                e.wait_ge(v2p, c(v2p))
                e.wait_ge(free[6], c(free[6]))
                for m in range(2):
                    ins = tr(psum[0:32, 6, m * P:(m + 1) * P], sscore[:, m, :])
                ins.then_inc(fullV[6], 1)
                e.wait_ge(v2p, c(v2p))
                e.wait_ge(free[7], c(free[7]))
                for m in range(2):
                    ins = tr(psum[:, 7, m * 32:(m + 1) * 32], sprob[0:32, m * P:(m + 1) * P])
                ins.then_inc(fullV[7], 1)
                e.wait_ge(v2p, c(v2p))
                e.wait_ge(free[6], c(free[6]))
                for b in range(B):
                    e.wait_ge(cache_in[b % 2], c(cache_in[b % 2], 16 * (B // 2 + 1) if b < 2 else 16))
                    for k in range(KT):
                        for m in range(2):
                            a = (b % 2) * 2048 + m * D + k * P
                            o = m * 32 + b * NXH + k // 2
                            ins = mm(psum[:, 6, k * B + b:k * B + b + 1], kv_flat[:, a:a + P], sprobT[:, o:o + 1],
                                     m == 0, m == 1)
                    ins.then_inc(cache_done[b % 2], 1)

            with c.loop("block", NB - 1) as b:
                one_block(b, False)
            one_block(NB - 1, True)
            e.wait_ge(v2p, c(v2p))
            new = fin[:, 80:112].rearrange("p (j b) -> p j b", j=4)
            for g in range(2):
                for src, bk, n in ((sup, 0, 2 * NF), (new, 2, 4)):
                    e.wait_ge(free[bk + g], c(free[bk + g]))
                    for b in range(4):
                        ins = tr(psum[0:n, bk + g, b * P:(b + 1) * P], src[:, :, 4 * g + b])
                    ins.then_inc(fullA[bk + g], 1)
            e.wait_ge(free[5], c(free[5]))
            for r in range(2):
                ins = tr(psum[0:2 * NF, 5, r * P:(r + 1) * P], fcarry[:, :, r])
            ins.then_inc(fullA[5], 1)
            e.wait_ge(free[4], c(free[4]))
            tr(psum[0:64, 4, 0:P], fin[:, 0:64])
            tr(psum[0:64, 4, P:2 * P], fin[:, 112:176])
            tr(psum[0:8, 4, 2 * P:3 * P], fin[:, 72:80])
            tr(psum[0:8, 4, 3 * P:4 * P], fin[:, 64:72]).then_inc(fullA[4], 1)
            e.wait_ge(free[6], c(free[6]))
            for p in range(NP):
                ins = tr(psum[:, 6, p * P:(p + 1) * P], S[:, p, :])
            ins.then_inc(fullA[6], 1)

        @block.scalar
        def _(e):
            c = Counts(e, "act", passedA)

            def act(out, src, func=ACT.Copy, **k):
                return e.activation(out, src, func, **k)

            def split_w(i):
                e.wait_ge(raw_ready[i], c(raw_ready[i], 16))
                act(whi[i][:, :, :], wraw[i][:, :, :]).then_inc(hi_ready[i], 1)

            def split_x(k, n=TB, tile=None, dst=None):
                e.wait_ge(st_ready, c(st_ready))
                act((xhi if dst is None else dst)[:, k, 0:n], stage[:, k % 2, 0:n]).then_inc(sthi, 1)

            def square(k, src, j):
                e.wait_ge(sq_free, c(sq_free))
                if k is None:
                    e.sem_inc(passedA, 1)
                return act(stage[:, j, :], src, ACT.Square)

            def stats():
                e.wait_ge(fullA[4], c(fullA[4]))
                act(sm[:, 0:4], psum[:, 4, 0:4], ACT.Sqrt, scale=1.0 / D, bias=eps[:, 0:1]).then_inc(a2v, 1)

            def sample_stats():
                e.wait_ge(fullA[6], c(fullA[6]))
                act(sm[:, 72:80], psum[:, 6, 0:B], ACT.Sqrt, scale=1.0 / D, bias=eps[:, 0:1]).then_inc(a2v, 1)

            e.wait_ge(ld, c(ld, 16 * NLD))
            e.wait_ge(consts, c(consts))
            for t in range(2):
                act(stage[:, :, :].rearrange("p a b -> p (a b)"), xin[:, t, :], ACT.Square, accum_out=sm[:, t:t + 1]).then_inc(ach, 1)
                e.wait_ge(ach, c(ach))
            act(sm[:, 2:4], sm[:, 0:2], ACT.Sqrt, scale=1.0 / D, bias=eps[:, 0:1]).then_inc(a2v, 1)
            split_w(0)
            split_w(1)
            for k in range(KT):
                split_x(k, NMEM)
            with c.loop("mem", 8):
                for j in range(2):
                    e.wait_ge(slab_done[j], c(slab_done[j]))
                    split_w(j)

            def dec_chunk(cc):
                e.wait_ge(dec_freeV, c(dec_freeV))
                e.wait_ge(dec_freeG, c(dec_freeG))
                e.sem_inc(passedA, 1)
                act(dec[:, :, :], Lf[:, :, bass.ds(cc * (C + 1), C + 1)], ACT.Exp, scale=-DECAY).then_inc(dec_readyV, 1)
                act(inv[:, :, :], Lf[:, :, bass.ds(cc * (C + 1) + 1, C)], ACT.Exp, scale=DECAY).then_inc(dec_readyG, 1)

            def wkv_steps(t0):
                for p in range(NP):
                    e.wait_ge(wk_mm[p], c(wk_mm[p], 2))
                    act(TM[:, p, :], psum[:, 4 + p, :]).then_inc(wk_act[p], 1)
                for l in range(1, len(MERGES)):
                    for p in range(NP):
                        e.wait_ge(wk_mm[p], c(wk_mm[p], 1 if l == 1 else 2))
                        act(Zs[:, p, :], psum[:, 4 + p, 0:P]).then_inc(wk_act[p], 1)
                for p in range(NP):
                    e.wait_ge(wk_mm[p], c(wk_mm[p], 2))
                    act(Zs[:, p, :], psum[:, 4 + p, 0:P]).then_inc(wk_act[p], 1)
                for p in range(NP):
                    e.wait_ge(wk_mm[p], c(wk_mm[p], 2))
                    e.sem_inc(passedA, 1)
                    act(Y[:, p, bass.ds(t0, C)], psum[:, 4 + p, 0:C]).then_inc(wk_act[p], 1)

            def residual(label):
                with c.loop(label, KT // 2) as i:
                    for j in range(2):
                        e.wait_ge(slab_done[j], c(slab_done[j]))
                        split_w(j)
                        e.wait_ge(xT_new, c(xT_new))
                        square(None, xT[:, bass.ds(2 * i + j, 1), :].rearrange("p a t -> p (a t)"), j).then_inc(sq_ready, 1)
                c.skip(sq_free, 2)

            def attention():
                units = [(h, t) for h in range(NXH) for t in range(TT)]

                def exps(n):
                    e.wait_ge(v2a, c(v2a))
                    act(pr[:, n % 2, :], psum[:, 4 + n % 2, 0:NMEM], ACT.Exp, scale=XSCALE,
                        bias=sm[:, 80 + n % 2:81 + n % 2], accum_out=sm[:, 82 + n % 2:83 + n % 2]).then_inc(a2v, 1)

                exps(0)
                for n, (h, t) in enumerate(units):
                    if n + 1 < len(units):
                        exps(n + 1)
                    bk = 6 + n % 2
                    if t == 0 and h >= 2:
                        e.wait_ge(pT_free, c(pT_free))
                    e.wait_ge(fullA[bk], c(fullA[bk]))
                    act(pT[:, h % 2, :, t * P:(t + 1) * P], psum[:, bk, 0:2 * P].rearrange("p (m t) -> p m t", m=2)).then_inc(ach, 1)
                    e.wait_ge(ach, c(ach))
                    e.sem_inc(free[bk], 1)
                    if t == TT - 1:
                        e.sem_inc(a2p, 1)
                    if n % 4 == 1 and n > 4:
                        split_x(2 * (h - 1))
                        split_x(2 * (h - 1) + 1)
                split_x(6)
                split_x(7)
                c.skip(pT_free, 2)

            def ffn_up(i):
                for a in range(4):
                    e.wait_ge(slab_done[a % 2], c(slab_done[a % 2]))
                    e.wait_ge(eb_free[a], c(eb_free[a]))
                    act(eb[:, a, 2:TB + 2], psum[:, a, :]).then_inc(ach, 1)
                    e.wait_ge(ach, c(ach))
                    e.sem_inc(eb_ready[a], 1)
                    e.sem_inc(free[a], 1)
                    split_w(a % 2)

            def ffn_silu(last):
                for a in (1, 3):
                    e.wait_ge(v2a, c(v2a))
                    act(fc[:, a, :], fc[:, a, :], ACT.Silu).then_inc(a2v, 1)
                if last:
                    e.wait_ge(v2a, c(v2a))
                    act(sw[:, 4:6, 0, :], sw[:, 2:4, 0, :], ACT.Silu).then_inc(a2v, 1)

            def ffn_hidden():
                for j in range(2):
                    split_x(j, dst=hhi)

            def one_block(b, last):
                for k in range(KT):
                    bk = 4 + k % 4
                    e.wait_ge(fullA[bk], c(fullA[bk]))
                    act(xT[:, k, :], psum[:, bk, :])
                    square(k, psum[:, bk, :], k % 2).then_inc(ach, 1)
                    e.wait_ge(ach, c(ach))
                    e.sem_inc(sq_ready, 1)
                    e.sem_inc(free[bk], 1)
                c.skip(sq_free, 2)
                stats()
                if last:
                    sample_stats()
                for k in range(KT):
                    split_x(k)
                with c.loop("shift", NRW // 2) as i:
                    for j in range(2):
                        m = 2 * i + j
                        e.wait_ge(slab_done[j], c(slab_done[j]))
                        e.wait_ge(shf_free[j], c(shf_free[j]))
                        e.sem_inc(passedA, 1)
                        act(shifted[:, j, 0:1], carry[:, bass.ds(m, 1)])
                        act(shifted[:, j, 1:TB + 1], psum[:, j, :], scale=pcol("mu_shift", m)).then_inc(ach, 1)
                        e.wait_ge(ach, c(ach))
                        e.sem_inc(passedA, 1)
                        act(carry[:, bass.ds(m, 1)], shifted[:, j, TB:TB + 1]).then_inc(shf[j], 1)
                        split_w(j)
                with c.loop("gate_b", 2) as i:
                    for j in range(2):
                        e.wait_ge(slab_done[j], c(slab_done[j]))
                        e.sem_inc(passedA, 1)
                        act(gb[:, bass.ds(2 * i + j, 1), :].rearrange("p a t -> p (a t)"), psum[:, j, :]).then_inc(free[j], 1)
                        split_w(j)
                with c.loop("gate_c", 2) as i:
                    for j in range(2):
                        e.wait_ge(slab_done[j], c(slab_done[j]))
                        e.sem_inc(passedA, 1)
                        act(cb[:, bass.ds(2 * i + j, 1), 2:TB + 2].rearrange("p a t -> p (a t)"), psum[:, j, :]).then_inc(ach, 1)
                        e.wait_ge(ach, c(ach))
                        e.sem_inc(free[j], 1)
                        e.sem_inc(a2v, 1)
                        split_w(j)
                with c.loop("h_in", 2):
                    for j in range(2):
                        e.wait_ge(slab_done[j], c(slab_done[j]))
                        split_w(j)
                e.wait_ge(v2a, c(v2a))
                act(Z[0:64, 12, :], Z[0:64, 12, :], ACT.Tanh)
                act(Z[:, 13, :], Z[:, 13, :], ACT.Sigmoid).then_inc(a2p, 1)
                for k in range(4, 8):
                    split_x(k)
                e.wait_ge(v2a, c(v2a))
                for n in range(8):
                    p, bk = n // 2, 4 + n % 4
                    e.wait_ge(fullA[bk], c(fullA[bk]))
                    if n % 2:
                        ins = act(kka[:, p, :], psum[:, bk, :], ACT.Sigmoid, bias=pcol("a0", p))
                    else:
                        ins = act(L[:, p, :, 1:C + 1], psum[:, bk, :].rearrange("p (c t) -> p c t", c=NC),
                                  ACT.Sigmoid, bias=pcol("w0", p))
                    if n < 7:
                        ins.then_inc(free[bk], 1)
                ins.then_inc(ach, 1)
                e.wait_ge(ach, c(ach))
                e.sem_inc(free[7], 1)
                e.sem_inc(a2v, 1)
                e.wait_ge(fullA[4], c(fullA[4]))
                act(sm[:, 8:40], psum[:, 4, 0:32], ACT.Sqrt).then_inc(a2v, 1)
                e.wait_ge(wkv_inA, c(wkv_inA))
                dec_chunk(0)
                dec_chunk(1)
                wkv_steps(0)
                with c.loop("wkv", NC // 2 - 1) as i:
                    dec_chunk(2 * i + 2)
                    wkv_steps(i * (2 * C) + C)
                    dec_chunk(2 * i + 3)
                    wkv_steps(i * (2 * C) + 2 * C)
                wkv_steps((NC - 1) * C)
                for p in range(NP):
                    e.wait_ge(v2a, c(v2a))
                    act(kkn[:, p, :], Y[:, p, :], ACT.Square).then_inc(a2p, 1)
                e.wait_ge(fullA[4], c(fullA[4]))
                act(sm[:, 8:40], psum[:, 4, 0:32], ACT.Sqrt, scale=1.0 / N, bias=eps[:, 1:2]).then_inc(a2v, 1)
                for k in range(4):
                    split_x(k)
                if last:
                    sample_wkv()
                residual("out")
                stats()
                if last:
                    sample_stats()
                for k in range(KT):
                    split_x(k)
                with c.loop("q", KT // 2) as i:
                    for j in range(2):
                        e.wait_ge(slab_done[j], c(slab_done[j]))
                        e.sem_inc(passedA, 1)
                        act(q_sb[:, bass.ds(2 * i + j, 1), :].rearrange("p a t -> p (a t)"), psum[:, j, :]).then_inc(ach, 1)
                        e.wait_ge(ach, c(ach))
                        e.sem_inc(free[j], 1)
                        split_w(j)
                e.sem_inc(a2p, 1)
                attention()
                if last:
                    sample_attention()
                residual("o")
                stats()
                if last:
                    sample_stats()
                for k in range(KT):
                    split_x(k)
                ffn_up(0)
                ffn_silu(last)
                ffn_hidden()
                with c.loop("ffn" + "s" * last, NF // 2 - 1) as i:
                    ffn_up(i + 1)
                    ffn_silu(last)
                    for j in range(2):
                        e.wait_ge(slab_done[j], c(slab_done[j]))
                        split_w(j)
                    ffn_hidden()
                for j in range(2):
                    e.wait_ge(slab_done[j], c(slab_done[j]))
                    if not last:
                        split_w(j)
                e.wait_ge(xT_new, c(xT_new))
                for k in range(KT):
                    square(k, xT[:, k, :], k % 2).then_inc(sq_ready, 1)
                c.skip(sq_free, 2)
                stats()
                for t in range(TT):
                    for g in range(2):
                        if t >= 2 and g == 0:
                            e.wait_ge(y_st[t % 2], c(y_st[t % 2], 16))
                        e.wait_ge(fullA[6 + g], c(fullA[6 + g]))
                        act(yrow[:, t % 2, g * TB:(g + 1) * TB], psum[:, 6 + g, :]).then_inc(ach, 1)
                        e.wait_ge(ach, c(ach))
                        e.sem_inc(free[6 + g], 1)
                    e.sem_inc(y_go[t % 2], 1)
                for j in range(2):
                    c.skip(y_st[j], 16)
                if last:
                    sample_stats()

            def sample_wkv():
                e.wait_ge(v2a, c(v2a))
                act(sz[0:64, 12, :], sz[0:64, 12, :], ACT.Tanh)
                act(sz[:, 13, :], sz[:, 13, :], ACT.Sigmoid).then_inc(a2p, 1)
                e.wait_ge(fullA[6], c(fullA[6]))
                e.wait_ge(fullA[7], c(fullA[7]))
                for p in range(NP):
                    act(sw[:, 0, p, :], psum[:, 6, 8 * p:8 * p + 8], ACT.Sigmoid, bias=pcol("w0", p))
                    act(sw[:, 1, p, :], psum[:, 7, 8 * p:8 * p + 8], ACT.Sigmoid, bias=pcol("a0", p))
                act(sw[:, 2, :, :], psum[:, 6, 64:96].rearrange("p (a b) -> p a b", a=4)).then_inc(ach, 1)
                e.wait_ge(ach, c(ach))
                act(sw[:, 0, :, :], sw[:, 0, :, :], ACT.Exp, scale=-DECAY).then_inc(a2v, 1)
                e.wait_ge(fullA[7], c(fullA[7]))
                act(sw[:, 3, :, :], psum[:, 7, 0:32].rearrange("p (a b) -> p a b", a=4), ACT.Sqrt).then_inc(a2v, 1)
                e.wait_ge(fullA[7], c(fullA[7]))
                act(sw[:, 3, :, :], psum[:, 7, 0:32].rearrange("p (a b) -> p a b", a=4), ACT.Sqrt, scale=1.0 / N,
                    bias=eps[:, 1:2]).then_inc(a2v, 1)

            def sample_attention():
                e.wait_ge(v2a, c(v2a))
                act(sprob[0:32, :], sprob[0:32, :], ACT.Exp, scale=XSCALE, bias=sm[0:32, 89:90],
                    accum_out=sm[0:32, 90:91]).then_inc(a2v, 1)

            with c.loop("block", NB - 1) as b:
                one_block(b, False)
            one_block(NB - 1, True)
            e.wait_ge(y_st[0], c(y_st[0], 0))
            e.wait_ge(y_st[1], c(y_st[1], 0))
            for g in range(2):
                e.wait_ge(fullA[g], c(fullA[g]))
                act(zr[0:2 * NF, 4 * g * P:4 * (g + 1) * P], psum[0:2 * NF, g, :])
                e.wait_ge(fullA[2 + g], c(fullA[2 + g]))
                act(zr[0:4, (8 + 4 * g) * P:(12 + 4 * g) * P], psum[0:4, 2 + g, :])
            e.wait_ge(fullA[5], c(fullA[5]))
            act(zr[0:2 * NF, 16 * P:18 * P], psum[0:2 * NF, 5, 0:2 * P])
            e.wait_ge(fullA[4], c(fullA[4]))
            act(zr[0:64, 18 * P:20 * P], psum[0:64, 4, 0:2 * P])
            act(zr[0:8, 20 * P:22 * P], psum[0:8, 4, 2 * P:4 * P])
            e.wait_ge(fullA[6], c(fullA[6]))
            act(zr[:, 22 * P:26 * P], psum[:, 6, :]).then_inc(out_go, 1)

        @block.vector
        def _(e):
            c = Counts(e, "dve", passedV)

            def tt(out, a, b, op=ALU.mult):
                return e.tensor_tensor(out, a, b, op)

            def stt(out, a, s, b, op0=ALU.mult, op1=ALU.mult):
                return e.scalar_tensor_tensor(out, a, s, b, op0, op1)

            def lo(k, n=TB, hi=None, lo_=None, ready=None):
                e.wait_ge(sthi, c(sthi))
                h, l = (xhi, xlo) if hi is None else (hi, lo_)
                tt(l[:, k, 0:n], stage[:, k % 2, 0:n], h[:, k, 0:n].bitcast(F32), ALU.subtract).then_inc(x_ready if ready is None else ready, 1)
                e.wait_ge(x_ready if ready is None else ready, c(x_ready if ready is None else ready))

            def split_tiles(order, produce, n=TB):
                before = None
                for k in order:
                    produce(k, stage[:, k % 2, 0:n]).then_inc(st_ready, 1)
                    e.wait_ge(st_ready, c(st_ready))
                    if before is not None:
                        lo(before, n)
                    before = k
                lo(before, n)

            def acc_start():
                e.memset(acc, 0.0).then_inc(vch, 1)
                e.wait_ge(vch, c(vch))
                e.sem_inc(sq_free, 2)

            def acc_add(j):
                e.wait_ge(sq_ready, c(sq_ready))
                tt(acc, acc, stage[:, j, :], ALU.add).then_inc(vch, 1)
                e.wait_ge(vch, c(vch))
                e.sem_inc(sq_free, 1)

            def stats(name, sample):
                e.sem_inc(v2p, 1)
                e.wait_ge(a2v, c(a2v))
                e.sem_inc(free[4], 1)
                e.reciprocal(sm[:, 4:8], sm[:, 0:4]).then_inc(v2p, 1)
                e.wait_ge(v2p, c(v2p))
                if sample:
                    sample_norm(name)

            def normalise(name, last=False):
                e.wait_ge(fullV[5], c(fullV[5]))

                def tile(k, out):
                    return stt(out, xT[:, k, :], pcol(name, k), psum[:, 5, :])

                split_tiles(range(KT), tile)
                e.sem_inc(free[5], 1)

            def bc8(ap):
                return ap.unsqueeze(2).broadcast_to([P, ap.shape[1], B])

            def sample_norm(name, split=True):
                tt(sw[:, 4:12, 0, :], xs[:, :, :], xs[:, :, :]).then_inc(vch, 1)
                e.wait_ge(vch, c(vch))
                e.tensor_reduce(sw[:, 10, 1, :], sw[:, 4:12, 0, :].rearrange("p k b -> p b k"), AX.X, ALU.add).then_inc(vch, 1)
                e.wait_ge(vch, c(vch))
                e.tensor_copy(sw[:, 11, 0, :], sw[:, 10, 1, :]).then_inc(v2p, 1)
                e.wait_ge(v2p, c(v2p))
                e.wait_ge(a2v, c(a2v))
                e.sem_inc(free[6], 1)
                e.reciprocal(sm[:, 72:80], sm[:, 72:80]).then_inc(vch, 1)
                e.wait_ge(vch, c(vch))
                tt(xsn[:, :, 0:B], xs[:, :, :], bc8(pcol(name, 0, KT))).then_inc(vch, 1)
                e.wait_ge(vch, c(vch))
                tt(xsn[:, :, 0:B], xsn[:, :, 0:B], sm[:, 72:80].unsqueeze(1).broadcast_to([P, KT, B])).then_inc(vch, 1)
                e.wait_ge(vch, c(vch))
                if name == "norm_mix":
                    e.tensor_copy(shn[:, :, 0:B], xsn[:, :, 0:B]).then_inc(vch, 1)
                    e.wait_ge(vch, c(vch))
                if split:
                    sample_split()

            def sample_split():
                e.tensor_copy(xsh[:, :, :], xsn[:, :, :]).then_inc(vch, 1)
                e.wait_ge(vch, c(vch))
                tt(xsl[:, :, :], xsn[:, :, :], xsh[:, :, :].bitcast(F32), ALU.subtract).then_inc(vch, 1)
                e.wait_ge(vch, c(vch))
                e.sem_inc(v2p, 1)

            e.wait_ge(consts, c(consts))
            e.wait_ge(fullV[4], c(fullV[4]))
            e.tensor_copy(par[:, :], psum[:, 4, 0:NPAR]).then_inc(vch, 1)
            e.wait_ge(vch, c(vch))
            e.sem_inc(free[4], 1)
            e.tensor_scalar(omu[:, :], pcol("mu_shift", 0, NRW), -1.0, 1.0, ALU.mult, ALU.add).then_inc(vch, 1)
            e.wait_ge(vch, c(vch))
            e.tensor_scalar(oka[:, :], pcol("k_a", 0, 4), -1.0, 1.0, ALU.mult, ALU.add).then_inc(vch, 1)
            e.wait_ge(vch, c(vch))
            e.wait_ge(fullV[5], c(fullV[5]))
            e.tensor_copy(fcw[:, :], psum[:, 5, 0:132]).then_inc(free[5], 1)
            e.wait_ge(fullV[6], c(fullV[6]))
            v = psum[:, 6, 0:128].rearrange("p (k b) -> p k b", k=KT)
            e.tensor_copy(xs[:, :, :], v[:, :, 0:B])
            e.tensor_copy(xsn[:, :, B:2 * B], v[:, :, B:2 * B])
            e.tensor_copy(sconv[:, :, :], psum[:, 6, 128:192].rearrange("p (k b) -> p k b", k=4)).then_inc(vch, 1)
            e.wait_ge(vch, c(vch))
            e.sem_inc(free[6], 1)
            for g in range(2):
                e.wait_ge(fullV[7], c(fullV[7]))
                e.tensor_copy(sffn[:, 22 * g:22 * g + 22, :], psum[:, 7, 0:352].rearrange("p (k b) -> p k b", k=22)).then_inc(vch, 1)
                e.wait_ge(vch, c(vch))
                e.sem_inc(free[7], 1)
            e.wait_ge(a2v, c(a2v))
            e.reciprocal(sm[:, 4:6], sm[:, 2:4]).then_inc(vch, 1)
            e.wait_ge(vch, c(vch))
            for t in range(2):
                e.tensor_scalar(xin[:, t, :], xin[:, t, :], sm[:, 4 + t:5 + t], None, ALU.mult).then_inc(vch, 1)
                e.wait_ge(vch, c(vch))
            e.sem_inc(v2p, 1)
            before = None
            for k in range(KT):
                bk = 4 + k % 4
                e.wait_ge(fullV[bk], c(fullV[bk]))
                e.tensor_scalar(stage[:, k % 2, 0:NMEM], psum[:, bk, 0:NMEM], pcol("norm_mem", k), None, ALU.mult).then_inc(vch, 1)
                e.wait_ge(vch, c(vch))
                e.sem_inc(free[bk], 1)
                e.sem_inc(st_ready, 1)
                if before is not None:
                    lo(before, NMEM)
                before = k
            lo(before, NMEM)
            with c.loop("mem", 8) as i:
                for j in range(2):
                    e.wait_ge(slab_done[j], c(slab_done[j]))
                    e.tensor_copy(zr[:, bass.ds((2 * i + j + 8) * NMEM, NMEM)], psum[:, j, 0:NMEM]).then_inc(vch, 1)
                    e.wait_ge(vch, c(vch))
                    e.sem_inc(free[j], 1)
            for kv in range(2):
                e.sem_inc(v2p, 1)
                for t in range(2):
                    for g in range(2):
                        bk = 4 + 2 * t + g
                        a = kv * 2048 + t * D + g * TB
                        e.wait_ge(fullV[bk], c(fullV[bk]))
                        e.tensor_copy(kv_flat[:, a:a + TB], psum[:, bk, :]).then_inc(vch, 1)
                        e.wait_ge(vch, c(vch))
                        e.sem_inc(free[bk], 1)
                e.sem_inc(out_go, 1)
            e.sem_inc(xin_free, 1)
            e.wait_ge(out_st, c(out_st, 48))

            def operands(i, t0):
                e.wait_ge(dec_readyV, c(dec_readyV))
                tt(ops_ar[i][:, :, P:192], Z[:, 0:4, bass.ds(t0, C)], dec[:, :, 1:C + 1])
                for h in range(2):
                    a = slice(64 * h, 64 * h + 64)
                    stt(ops_ar[i][a, :, a], kkn[a, :, bass.ds(t0, C)], -1.0, dec[a, :, 0:C])
                e.tensor_copy(gC[i][:, :], dec[:, :, C]).then_inc(vch, 1)
                e.wait_ge(vch, c(vch))
                e.sem_inc(vec_ops[i], 1)
                e.sem_inc(dec_freeV, 1)

            def wkv_steps(i):
                for p in range(NP):
                    e.wait_ge(wk_mm[p], c(wk_mm[p]))
                    tt(GM[:, p, :, :], psum[:, 4 + p, 0:384].rearrange("p (a c) -> p a c", a=2),
                           gram_mask[:, :].unsqueeze(1).broadcast_to([P, 2, 192])).then_inc(vch, 1)
                    e.wait_ge(vch, c(vch))
                    e.sem_inc(wk_vec[p], 1)
                    e.tensor_copy(QT[:, p, :, :], ident[:, :].unsqueeze(1).broadcast_to([P, 2, P])).then_inc(vch, 1)
                    e.wait_ge(vch, c(vch))
                    if p == NP - 1:
                        e.sem_inc(passedV, 1)
                for p in range(NP):
                    e.copy_predicated(QT[:, p, 0, :], merge_mask[:, 0, 0, :], GM[:, p, 0, 0:P])
                    e.wait_ge(wk_act[p], c(wk_act[p]))
                    e.sem_inc(passedV, 1)
                    e.copy_predicated(QT[:, p, 1, :], merge_mask[:, 0, 1, :], TM[:, p, 384:512]
                                      ).then_inc(wk_vec[p], 1)
                    c.skip(wk_mm[p], 1)
                for l in range(1, len(MERGES)):
                    for p in range(NP):
                        e.wait_ge(wk_mm[p], c(wk_mm[p], 2))
                        e.sem_inc(passedV, 1)
                        if l == 1 and p == NP - 1:
                            e.sem_inc(ops_freeG, 1)
                        if l < len(MERGES) - 1:
                            e.copy_predicated(QT[:, p, :, :].rearrange("p a c -> p (a c)"),
                                              merge_mask[:, l, :, :].rearrange("p a c -> p (a c)"),
                                              psum[:, 4 + p, 0:2 * P]).then_inc(wk_vec[p], 1)
                        else:
                            e.copy_predicated(QT[:, p, 0, :], merge_mask[:, l, 0, :],
                                              psum[:, 4 + p, 0:P]).then_inc(wk_vec[p], 1)
                for p in range(NP):
                    e.wait_ge(wk_mm[p], c(wk_mm[p], 2))
                    e.tensor_copy(Us[:, p, :], psum[:, 4 + p, 0:P]).then_inc(wk_vec[p], 1)
                    e.wait_ge(wk_vec[p], c(wk_vec[p]))
                for p in range(NP):
                    e.wait_ge(wk_mm[p], c(wk_mm[p]))
                    e.wait_ge(wk_act[p], c(wk_act[p], 7))
                    tt(S[:, p, :], S[:, p, :], psum[:, 4 + p, P:2 * P], ALU.add).then_inc(vch, 1)
                    e.wait_ge(vch, c(vch))
                    e.tensor_scalar(S[:, p, :], S[:, p, :], gC[i][:, p:p + 1], None, ALU.mult).then_inc(vch, 1)
                    e.wait_ge(vch, c(vch))
                    e.sem_inc(wk_vec[p], 1)

            def residual(label, last):
                acc_start()
                with c.loop(label + "s" * last, KT // 2) as i:
                    for j in range(2):
                        k = 2 * i + j
                        e.wait_ge(slab_done[j], c(slab_done[j]))
                        x = xT[:, bass.ds(k, 1), :].rearrange("p a t -> p (a t)")
                        tt(x, x, psum[:, j, :], ALU.add).then_inc(vch, 1)
                        e.wait_ge(vch, c(vch))
                        e.sem_inc(free[j], 1)
                        e.sem_inc(xT_new, 1)
                        if last:
                            y = xs[:, bass.ds(k, 1), :].rearrange("p a t -> p (a t)")
                            tt(y, y, psum[:, 4 + j, 0:B], ALU.add).then_inc(vch, 1)
                            e.wait_ge(vch, c(vch))
                            e.sem_inc(free[4 + j], 1)
                        acc_add(j)

            def attention():
                units = [(h, t) for h in range(NXH) for t in range(TT)]

                def maximum(n):
                    e.wait_ge(fullV[4 + n % 2], c(fullV[4 + n % 2]))
                    e.reduce_max(sm[:, 84 + n % 2:85 + n % 2], psum[:, 4 + n % 2, 0:NMEM], AX.X).then_inc(vch, 1)
                    e.wait_ge(vch, c(vch))
                    e.tensor_scalar(sm[:, 80 + n % 2:81 + n % 2], sm[:, 84 + n % 2:85 + n % 2], -XSCALE, None,
                                    ALU.mult).then_inc(v2a, 1)

                def head_out(h):
                    for d in range(2):
                        k = 2 * h + d
                        e.wait_ge(fullV[2 + d], c(fullV[2 + d]))
                        e.tensor_copy(stage[:, d, :], psum[:, 2 + d, :]).then_inc(vch, 1)
                        e.wait_ge(vch, c(vch))
                        e.sem_inc(free[2 + d], 1)
                        e.sem_inc(st_ready, 1)
                    e.sem_inc(pT_free, 1)
                    lo(2 * h)
                    lo(2 * h + 1)

                maximum(0)
                for n, (h, t) in enumerate(units):
                    if n + 1 < len(units):
                        maximum(n + 1)
                    e.wait_ge(a2v, c(a2v))
                    e.sem_inc(free[4 + n % 2], 1)
                    e.reciprocal(sm[:, 86 + n % 2:87 + n % 2], sm[:, 82 + n % 2:83 + n % 2]).then_inc(vch, 1)
                    e.wait_ge(vch, c(vch))
                    e.tensor_scalar(pr[:, n % 2, :], pr[:, n % 2, :], sm[:, 86 + n % 2:87 + n % 2], None,
                                    ALU.mult).then_inc(v2p, 1)
                    if n % 4 == 1 and n > 4:
                        head_out(h - 1)
                head_out(NXH - 1)

            def ffn_conv(i, last):
                for a, tile in ((0, 2 * i), (1, 2 * i + NF), (2, 2 * i + 1), (3, 2 * i + NF + 1)):
                    w = [fcw[:, bass.ds(tile + t * 2 * NF, 1)] for t in range(3)]
                    e.wait_ge(eb_carry[a], c(eb_carry[a]))
                    e.tensor_scalar(fc[:, a, :], eb[:, a, 0:TB], w[0], None, ALU.mult).then_inc(vch, 1)
                    e.wait_ge(vch, c(vch))
                    stt(fc[:, a, :], eb[:, a, 1:TB + 1], w[1], fc[:, a, :], ALU.mult, ALU.add).then_inc(vch, 1)
                    e.wait_ge(vch, c(vch))
                    stt(fc[:, a, :], eb[:, a, 2:TB + 2], w[2], fc[:, a, :], ALU.mult, ALU.add).then_inc(vch, 1)
                    e.wait_ge(vch, c(vch))
                    e.sem_inc(eb_free[a], 1)
                    if a % 2:
                        e.sem_inc(v2a, 1)
                    e.wait_ge(slab_done[a % 2], c(slab_done[a % 2]))
                    if last:
                        u = sup[:, bass.ds(tile, 1), :].rearrange("p a b -> p (a b)")
                        e.tensor_copy(u, psum[:, 4 + a % 2, 0:B]).then_inc(vch, 1)
                        e.wait_ge(vch, c(vch))
                        e.sem_inc(free[4 + a % 2], 1)
                        o = sw[:, (0, 2, 1, 3)[a], 0, :]
                        st = sffn[:, bass.ds(tile, 1), :].rearrange("p a (b r) -> p (a b) r", r=2)
                        e.tensor_scalar(o, st[:, :, 0], w[0], None, ALU.mult).then_inc(vch, 1)
                        e.wait_ge(vch, c(vch))
                        stt(o, st[:, :, 1], w[1], o, ALU.mult, ALU.add).then_inc(vch, 1)
                        e.wait_ge(vch, c(vch))
                        stt(o, u, w[2], o, ALU.mult, ALU.add).then_inc(vch, 1)
                        e.wait_ge(vch, c(vch))
                if last:
                    e.sem_inc(v2a, 1)

            def ffn_hidden(last):
                for j in range(2):
                    e.wait_ge(a2v, c(a2v))
                    tt(stage[:, j, :], fc[:, 2 * j, :], fc[:, 2 * j + 1, :]).then_inc(st_ready, 1)
                    e.wait_ge(st_ready, c(st_ready))
                for j in range(2):
                    lo(j, hi=hhi, lo_=hlo, ready=h_ready)
                if last:
                    e.wait_ge(a2v, c(a2v))
                    tt(sw[:, 6:8, 0, :], sw[:, 0:2, 0, :], sw[:, 4:6, 0, :]).then_inc(vch, 1)
                    e.wait_ge(vch, c(vch))
                    e.tensor_copy(shh[:, :, :], sw[:, 6:8, 0, :]).then_inc(vch, 1)
                    e.wait_ge(vch, c(vch))
                    tt(shl[:, :, :], sw[:, 6:8, 0, :], shh[:, :, :].bitcast(F32), ALU.subtract).then_inc(vch, 1)
                    e.wait_ge(vch, c(vch))
                    e.sem_inc(v2p, 1)

            def ffn_add(last):
                for k in range(KT):
                    if k < KT - 1:
                        e.wait_ge(fullV[k % 4], c(fullV[k % 4]))
                    else:
                        e.wait_ge(slab_done[0], c(slab_done[0]))
                        e.wait_ge(slab_done[1], c(slab_done[1]))
                    tt(xT[:, k, :], xT[:, k, :], psum[:, k % 4, :], ALU.add).then_inc(vch, 1)
                    e.wait_ge(vch, c(vch))
                    e.sem_inc(free[k % 4], 1)
                if last:
                    tt(xs[:, :, :], xs[:, :, :], psum[:, 6, 0:KT * B].rearrange("p (k b) -> p k b", k=KT), ALU.add).then_inc(vch, 1)
                    e.wait_ge(vch, c(vch))
                    e.sem_inc(free[6], 1)

            def one_block(b, last):
                acc_start()
                for k in range(KT):
                    acc_add(k % 2)
                stats("norm_mix", last)
                normalise("norm_mix")
                if last:
                    tt(shn[:, :, B], xhi[:, :, TB - 1].bitcast(F32), xlo[:, :, TB - 1].bitcast(F32), ALU.add).then_inc(vch, 1)
                    e.wait_ge(vch, c(vch))
                e.tensor_copy(cb[:, :, 0:2], ccarry[:, :, :]).then_inc(vch, 1)
                e.wait_ge(vch, c(vch))

                def sample_out(m, j):
                    if last:
                        e.tensor_copy(sp[:, bass.ds(m, 1), :].rearrange("p a b -> p (a b)"), psum[:, 4 + j, 0:2 * B]).then_inc(vch, 1)
                        e.wait_ge(vch, c(vch))
                        e.sem_inc(free[4 + j], 1)

                with c.loop("shift" + "s" * last, NRW // 2) as i:
                    for j in range(2):
                        m = 2 * i + j
                        e.wait_ge(shf[j], c(shf[j]))
                        e.wait_ge(slab_done[j], c(slab_done[j]))
                        stt(Z[:, bass.ds(m, 1), :].rearrange("p a t -> p (a t)"), psum[:, j, :],
                            omu[:, bass.ds(m, 1)], shifted[:, j, 0:TB], ALU.mult, ALU.add).then_inc(vch, 1)
                        e.wait_ge(vch, c(vch))
                        e.sem_inc(free[j], 1)
                        e.sem_inc(shf_free[j], 1)
                        sample_out(m, j)
                e.sem_inc(v2a, 1)
                with c.loop("gates" + "s" * last, 4) as i:
                    for j in range(2):
                        e.wait_ge(slab_done[j], c(slab_done[j]))
                        sample_out(2 * i + j + NRW, j)
                e.wait_ge(a2v, c(a2v, 4))
                with c.loop("h_in" + "s" * last, 2) as i:
                    for j in range(2):
                        e.wait_ge(slab_done[j], c(slab_done[j]))
                        v = cb[:, bass.ds(2 * i + j, 1), 2:TB + 2].rearrange("p a t -> p (a t)")
                        tt(v, v, psum[:, j, :]).then_inc(vch, 1)
                        e.wait_ge(vch, c(vch))
                        e.sem_inc(free[j], 1)
                        sample_out(2 * i + j + 22, j)

                def conv(k, out):
                    t, j = shifted[:, k % 2, 0:TB], k - 4
                    e.tensor_scalar(t, cb[:, j, 0:TB], pcol("conv_w", j), None, ALU.mult).then_inc(vch, 1)
                    e.wait_ge(vch, c(vch))
                    stt(t, cb[:, j, 1:TB + 1], pcol("conv_w", 4 + j), t, ALU.mult, ALU.add).then_inc(vch, 1)
                    e.wait_ge(vch, c(vch))
                    stt(t, cb[:, j, 2:TB + 2], pcol("conv_w", 8 + j), t, ALU.mult, ALU.add).then_inc(vch, 1)
                    e.wait_ge(vch, c(vch))
                    return tt(out, t, gb[:, j, :])

                split_tiles(range(4, 8), conv)
                e.tensor_copy(ccarry[:, :, :], cb[:, :, TB:TB + 2]).then_inc(vch, 1)
                e.wait_ge(vch, c(vch))
                e.memset(L[:, :, :, 0], 0.0).then_inc(vch, 1)
                e.wait_ge(vch, c(vch))
                e.sem_inc(v2a, 1)
                for p in range(NP):
                    e.tensor_scalar(kkn[:, p, :], Z[:, 4 + p, :], pcol("k_k", p), None, ALU.mult).then_inc(vch, 1)
                    e.wait_ge(vch, c(vch))
                    sq = stage[:, p, :] if p < 2 else shifted[:, p - 2, 0:TB]
                    tt(sq, kkn[:, p, :], kkn[:, p, :]).then_inc(vch, 1)
                    e.wait_ge(vch, c(vch))
                e.sem_inc(v2p, 1)
                e.wait_ge(a2v, c(a2v))
                for p in range(NP):
                    ins = e.tensor_tensor_scan(Lf[:, p, :], scan_mask[:, :], Lf[:, p, :], 0.0, ALU.mult, ALU.add)
                e.wait_ge(a2v, c(a2v))
                e.sem_inc(free[4], 1)
                e.tensor_scalar(sm[:, 8:40], sm[:, 8:40], 1e-12, None, ALU.max).then_inc(vch, 1)
                e.wait_ge(vch, c(vch))
                e.reciprocal(sm[:, 40:72], sm[:, 8:40]).then_inc(vch, 1)
                e.wait_ge(vch, c(vch))
                e.sem_inc(v2p, 1)
                for p in range(NP):
                    t = shifted[:, p % 2, 0:TB]
                    e.wait_ge(fullV[4 + p], c(fullV[4 + p]))
                    tt(kkn[:, p, :], kkn[:, p, :], psum[:, 4 + p, :]).then_inc(vch, 1)
                    e.wait_ge(vch, c(vch))
                    e.sem_inc(free[4 + p], 1)
                    e.tensor_scalar(t, kka[:, p, :], pcol("k_a", p), oka[:, p:p + 1], ALU.mult, ALU.add).then_inc(vch, 1)
                    e.wait_ge(vch, c(vch))
                    tt(Z[:, 4 + p, :], Z[:, 4 + p, :], t).then_inc(vch, 1)
                    e.wait_ge(vch, c(vch))
                    tt(kka[:, p, :], kka[:, p, :], kkn[:, p, :]).then_inc(vch, 1)
                    e.wait_ge(vch, c(vch))
                e.sem_inc(wkv_inA, 1)
                e.sem_inc(wkv_inG, 1)
                operands(0, 0)
                operands(1, C)
                wkv_steps(0)
                with c.loop("wkv", NC // 2 - 1) as i:
                    operands(0, i * (2 * C) + 2 * C)
                    wkv_steps(1)
                    operands(1, i * (2 * C) + 3 * C)
                    wkv_steps(0)
                wkv_steps(1)
                e.sem_inc(ws_free, 1)
                for p in range(NP + 1):
                    if p < NP:
                        t = shifted[:, p % 2, 0:TB]
                        if p >= 2:
                            pass
                        stt(t, Z[:, p, :], pcol("r_k", p), Z[:, 4 + p, :]).then_inc(v2p, 1)
                        e.wait_ge(v2p, c(v2p))
                    if p:
                        q = p - 1
                        e.wait_ge(fullV[4 + q], c(fullV[4 + q]))
                        tt(Z[:, q, :], Z[:, 8 + q, :], psum[:, 4 + q, :]).then_inc(vch, 1)
                        e.wait_ge(vch, c(vch))
                        e.sem_inc(free[4 + q], 1)
                for p in range(NP):
                    e.wait_ge(fullV[4 + p], c(fullV[4 + p]))
                    stt(Y[:, p, :], psum[:, 4 + p, :], -1.0 / N, Y[:, p, :], ALU.mult, ALU.add).then_inc(vch, 1)
                    e.wait_ge(vch, c(vch))
                    e.sem_inc(free[4 + p], 1)
                    e.sem_inc(v2a, 1)
                e.wait_ge(a2v, c(a2v))
                e.sem_inc(free[4], 1)
                e.reciprocal(sm[:, 40:72], sm[:, 8:40]).then_inc(vch, 1)
                e.wait_ge(vch, c(vch))
                e.sem_inc(v2p, 1)
                for p in range(NP):
                    e.wait_ge(fullV[4 + p], c(fullV[4 + p]))
                    tt(Y[:, p, :], Y[:, p, :], psum[:, 4 + p, :]).then_inc(vch, 1)
                    e.wait_ge(vch, c(vch))
                    e.sem_inc(free[4 + p], 1)
                    e.tensor_scalar(Y[:, p, :], Y[:, p, :], pcol("ln_x_w", p), pcol("ln_x_b", p), ALU.mult, ALU.add).then_inc(vch, 1)
                    e.wait_ge(vch, c(vch))
                    tt(Y[:, p, :], Y[:, p, :], Z[:, p, :], ALU.add).then_inc(vch, 1)
                    e.wait_ge(vch, c(vch))

                def gated(k, out):
                    e.wait_ge(fullV[4 + k], c(fullV[4 + k]))
                    tt(out, Y[:, k, :], psum[:, 4 + k, :]).then_inc(vch, 1)
                    e.wait_ge(vch, c(vch))
                    return e.sem_inc(free[4 + k], 1)

                before = None
                for k in range(NP):
                    gated(k, stage[:, k % 2, :])
                    e.sem_inc(st_ready, 1)
                    if before is not None:
                        lo(before)
                    before = k
                lo(before)
                if last:
                    sample_wkv()
                    for j in range(2):
                        e.sem_inc(cache_free[j], 1)
                else:
                    e.sem_inc(xin_free, 1)
                residual("out", last)
                stats("norm_x", last)
                normalise("norm_x")
                with c.loop("q" + "s" * last, KT // 2) as i:
                    for j in range(2):
                        e.wait_ge(slab_done[j], c(slab_done[j]))
                        if last:
                            e.tensor_copy(sq_s[:, bass.ds(2 * i + j, 1), :].rearrange("p a b -> p (a b)"), psum[:, 4 + j, 0:B]).then_inc(vch, 1)
                            e.wait_ge(vch, c(vch))
                            e.sem_inc(free[4 + j], 1)
                attention()
                if last:
                    sample_attention()
                residual("o", last)
                stats("norm_ffn", last)
                normalise("norm_ffn")
                ffn_conv(0, last)
                ffn_hidden(last)
                with c.loop("ffn" + "s" * last, NF // 2 - 1) as i:
                    ffn_conv(i + 1, last)
                    ffn_add(last)
                    ffn_hidden(last)
                ffn_add(last)
                acc_start()
                e.sem_inc(xT_new, 1)
                for k in range(KT):
                    acc_add(k % 2)
                stats("norm_final", False)
                e.wait_ge(fullV[5], c(fullV[5]))
                for k in range(KT):
                    stt(xT[:, k, :], xT[:, k, :], pcol("norm_final", k), psum[:, 5, :]).then_inc(vch, 1)
                    e.wait_ge(vch, c(vch))
                    e.sem_inc(v2p, 1)
                e.sem_inc(free[5], 1)
                for j in range(2):
                    e.wait_ge(y_st[j], c(y_st[j], 32))
                if last:
                    sample_norm("norm_final", split=False)

            def flat(t):
                return t.rearrange("p a b -> p (a b)")

            def sample_wkv():
                mu, om = bc8(pcol("mu_shift", 0, NRW)), bc8(omu[:, :])
                tt(sz[:, :, :], sp[:, 0:NRW, B:2 * B], mu).then_inc(vch, 1)
                e.wait_ge(vch, c(vch))
                tt(sp[:, 0:NRW, B:2 * B], sp[:, 0:NRW, 0:B], om).then_inc(vch, 1)
                e.wait_ge(vch, c(vch))
                tt(sz[:, :, :], sz[:, :, :], sp[:, 0:NRW, B:2 * B], ALU.add).then_inc(vch, 1)
                e.wait_ge(vch, c(vch))
                e.sem_inc(v2a, 1)
                r, k, v = sz[:, 0:4, :], sz[:, 4:8, :], sz[:, 8:12, :]
                W = [sw[:, n, :, :] for n in range(12)]
                new, t = W[10], W[9]
                st = sconv[:, :, :].rearrange("p j (b r) -> p j b r", r=2)
                tt(new, sp[:, 18:22, 0:B], sp[:, 22:26, 0:B]).then_inc(vch, 1)
                e.wait_ge(vch, c(vch))
                tt(W[8], st[:, :, :, 0], bc8(pcol("conv_w", 0, 4))).then_inc(vch, 1)
                e.wait_ge(vch, c(vch))
                tt(t, st[:, :, :, 1], bc8(pcol("conv_w", 4, 4))).then_inc(vch, 1)
                e.wait_ge(vch, c(vch))
                tt(W[8], W[8], t, ALU.add).then_inc(vch, 1)
                e.wait_ge(vch, c(vch))
                tt(t, new, bc8(pcol("conv_w", 8, 4))).then_inc(vch, 1)
                e.wait_ge(vch, c(vch))
                tt(W[8], W[8], t, ALU.add).then_inc(vch, 1)
                e.wait_ge(vch, c(vch))
                tt(xsn[:, 4:8, 0:B], W[8], sp[:, 14:18, 0:B]).then_inc(vch, 1)
                e.wait_ge(vch, c(vch))
                e.tensor_copy(fin[:, 80:112].rearrange("p (j b) -> p j b", j=4), new).then_inc(vch, 1)
                e.wait_ge(vch, c(vch))
                tt(W[4], k, bc8(pcol("k_k", 0, 4))).then_inc(vch, 1)
                e.wait_ge(vch, c(vch))
                tt(W[11], W[4], W[4]).then_inc(vch, 1)
                e.wait_ge(vch, c(vch))
                e.wait_ge(a2v, c(a2v))
                e.sem_inc(free[6], 1)
                e.sem_inc(free[7], 1)
                e.sem_inc(v2p, 1)
                e.wait_ge(a2v, c(a2v))
                e.sem_inc(free[7], 1)
                e.tensor_scalar(W[3], W[3], 1e-12, None, ALU.max).then_inc(vch, 1)
                e.wait_ge(vch, c(vch))
                e.reciprocal(W[3], W[3]).then_inc(vch, 1)
                e.wait_ge(vch, c(vch))
                tt(W[4], W[4], W[3]).then_inc(vch, 1)
                e.wait_ge(vch, c(vch))
                tt(W[5], W[1], bc8(pcol("k_a", 0, 4))).then_inc(vch, 1)
                e.wait_ge(vch, c(vch))
                tt(W[5], W[5], bc8(oka[:, :]), ALU.add).then_inc(vch, 1)
                e.wait_ge(vch, c(vch))
                tt(W[5], W[5], k).then_inc(vch, 1)
                e.wait_ge(vch, c(vch))
                tt(W[6], W[4], W[1]).then_inc(vch, 1)
                e.wait_ge(vch, c(vch))
                e.tensor_scalar(W[4], W[4], -1.0, None, ALU.mult).then_inc(vch, 1)
                e.wait_ge(vch, c(vch))
                e.wait_ge(s_state, c(s_state, 16 * 16))
                state = cl[:, 0:2048].rearrange("p (n k) -> p n k", k=N)
                work = flat(kka[:, :, :]).rearrange("p (n k) -> p n k", k=N)
                expand = flat(kkn).rearrange("p (n k) -> p n k", k=N)
                bcast = psum[:, 4:8, :].rearrange("p g (n k) -> p (g n) k", k=N)
                u = W[8]
                ubc = flat(u).unsqueeze(2).broadcast_to([P, 4 * B, N])
                vbc = flat(v).unsqueeze(2).broadcast_to([P, 4 * B, N])
                for j, q in enumerate((W[4], W[0], W[6], W[5], r)):
                    tt(expand, flat(q).unsqueeze(2).broadcast_to([P, 4 * B, N]),
                           ident64[:, :].unsqueeze(1).broadcast_to([P, 4 * B, N])).then_inc(vch, 1)
                    e.wait_ge(vch, c(vch))
                    e.sem_inc(v2p, 1)
                    e.wait_ge(fullV[7], c(fullV[7]))
                    if j == 0:
                        tt(work, state, bcast).then_inc(vch, 1)
                        e.wait_ge(vch, c(vch))
                        e.tensor_reduce(flat(u), work, AX.X, ALU.add).then_inc(vch, 1)
                        e.wait_ge(vch, c(vch))
                    elif j == 1:
                        tt(state, state, bcast).then_inc(vch, 1)
                        e.wait_ge(vch, c(vch))
                    elif j < 4:
                        tt(work, ubc if j == 2 else vbc, bcast).then_inc(vch, 1)
                        e.wait_ge(vch, c(vch))
                        tt(state, state, work, ALU.add).then_inc(vch, 1)
                        e.wait_ge(vch, c(vch))
                    else:
                        tt(work, state, bcast).then_inc(vch, 1)
                        e.wait_ge(vch, c(vch))
                        e.tensor_reduce(flat(W[7]), work, AX.X, ALU.add).then_inc(vch, 1)
                        e.wait_ge(vch, c(vch))
                    for g in range(4):
                        e.sem_inc(free[4 + g], 1)
                ps7 = psum[:, 7, 0:4 * B].rearrange("p (a b) -> p a b", a=4)
                tt(W[11], r, W[5]).then_inc(vch, 1)
                e.wait_ge(vch, c(vch))
                tt(W[11], W[11], bc8(pcol("r_k", 0, 4))).then_inc(vch, 1)
                e.wait_ge(vch, c(vch))
                e.sem_inc(v2p, 1)
                e.wait_ge(fullV[7], c(fullV[7]))
                tt(W[8], v, ps7).then_inc(vch, 1)
                e.wait_ge(vch, c(vch))
                e.sem_inc(free[7], 1)
                e.tensor_copy(W[11], W[7]).then_inc(vch, 1)
                e.wait_ge(vch, c(vch))
                e.sem_inc(v2p, 1)
                e.wait_ge(fullV[7], c(fullV[7]))
                stt(W[7], ps7, -1.0 / N, W[7], ALU.mult, ALU.add).then_inc(vch, 1)
                e.wait_ge(vch, c(vch))
                e.sem_inc(free[7], 1)
                tt(W[11], W[7], W[7]).then_inc(vch, 1)
                e.wait_ge(vch, c(vch))
                e.sem_inc(v2p, 1)
                e.wait_ge(a2v, c(a2v))
                e.sem_inc(free[7], 1)
                e.reciprocal(W[3], W[3]).then_inc(vch, 1)
                e.wait_ge(vch, c(vch))
                tt(W[7], W[7], W[3]).then_inc(vch, 1)
                e.wait_ge(vch, c(vch))
                tt(W[7], W[7], bc8(pcol("ln_x_w", 0, 4))).then_inc(vch, 1)
                e.wait_ge(vch, c(vch))
                tt(W[7], W[7], bc8(pcol("ln_x_b", 0, 4)), ALU.add).then_inc(vch, 1)
                e.wait_ge(vch, c(vch))
                tt(W[7], W[7], W[8], ALU.add).then_inc(vch, 1)
                e.wait_ge(vch, c(vch))
                tt(xsn[:, 0:4, 0:B], W[7], W[2]).then_inc(vch, 1)
                e.wait_ge(vch, c(vch))
                sample_split()

            def sample_attention():
                qb = zr[:, 8 * TB:10 * TB]
                prod = stage[:, :, :].rearrange("p a b -> p (a b)")
                for b in range(B):
                    tt(qb.rearrange("p (k x) -> p k x", k=KT),
                           sq_s[:, :, b:b + 1].broadcast_to([P, KT, P]),
                           ident[:, :].unsqueeze(1).broadcast_to([P, KT, P])).then_inc(vch, 1)
                    e.wait_ge(vch, c(vch))
                    e.sem_inc(v2p, 1)
                    e.wait_ge(fullV[5], c(fullV[5]))
                    e.tensor_copy(qrep, psum[:, 4:6, :].rearrange("p a b -> p (a b)")).then_inc(vch, 1)
                    e.wait_ge(vch, c(vch))
                    e.sem_inc(free[4], 1)
                    e.sem_inc(free[5], 1)
                    e.wait_ge(cache_in[b % 2], c(cache_in[b % 2], 16))
                    for m in range(2):
                        for h in range(NXH):
                            a = (b % 2) * 2048 + m * D + h * 256
                            e.tensor_tensor_reduce(prod[:, 0:256], kv_flat[:, a:a + 256], qrep[:, h * 256:(h + 1) * 256],
                                                   1.0, 0.0, ALU.mult, ALU.add, sscore[:, m, b * NXH + h:b * NXH + h + 1]).then_inc(vch, 1)
                            e.wait_ge(vch, c(vch))
                    e.sem_inc(cache_free[b % 2], 1)
                e.sem_inc(v2p, 1)
                e.wait_ge(fullV[6], c(fullV[6]))
                e.tensor_copy(sprob[0:32, :], psum[0:32, 6, 0:NMEM]).then_inc(vch, 1)
                e.wait_ge(vch, c(vch))
                e.sem_inc(free[6], 1)
                e.reduce_max(sm[0:32, 88:89], sprob[0:32, :], AX.X).then_inc(vch, 1)
                e.wait_ge(vch, c(vch))
                e.tensor_scalar(sm[0:32, 89:90], sm[0:32, 88:89], -XSCALE, None, ALU.mult).then_inc(vch, 1)
                e.wait_ge(vch, c(vch))
                e.sem_inc(v2a, 1)
                e.wait_ge(a2v, c(a2v))
                e.reciprocal(sm[0:32, 91:92], sm[0:32, 90:91]).then_inc(vch, 1)
                e.wait_ge(vch, c(vch))
                e.tensor_scalar(sprob[0:32, :], sprob[0:32, :], sm[0:32, 91:92], None, ALU.mult).then_inc(vch, 1)
                e.wait_ge(vch, c(vch))
                e.sem_inc(v2p, 1)
                e.wait_ge(fullV[7], c(fullV[7]))
                e.tensor_copy(sprobT[:, :], psum[:, 7, 0:64]).then_inc(vch, 1)
                e.wait_ge(vch, c(vch))
                e.sem_inc(free[7], 1)
                e.sem_inc(v2p, 1)
                for b in range(B):
                    e.wait_ge(cache_done[b % 2], c(cache_done[b % 2]))
                    if b < B - 2:
                        e.sem_inc(cache_free[b % 2], 1)
                e.tensor_copy(xsn[:, :, 0:B], psum[:, 6, 0:KT * B].rearrange("p (k b) -> p k b", k=KT)).then_inc(vch, 1)
                e.wait_ge(vch, c(vch))
                e.sem_inc(free[6], 1)
                sample_split()

            with c.loop("block", NB - 1) as b:
                one_block(b, False)
            one_block(NB - 1, True)
            e.tensor_copy(fin[:, 0:64].rearrange("p (b k) -> p k b", k=KT), shn[:, :, 0:B]).then_inc(vch, 1)
            e.wait_ge(vch, c(vch))
            e.tensor_copy(fin[:, 64:72].rearrange("p (r j) -> p j r", j=4), ccarry[:, :, :]).then_inc(vch, 1)
            e.wait_ge(vch, c(vch))
            e.tensor_copy(fin[:, 72:80], shn[:, :, B]).then_inc(vch, 1)
            e.wait_ge(vch, c(vch))
            e.tensor_copy(fin[:, 112:176].rearrange("p (b k) -> p k b", k=KT), xsn[:, :, 0:B]).then_inc(vch, 1)
            e.wait_ge(vch, c(vch))
            e.sem_inc(v2p, 1)


_OUTS = (("y_prompt", (1, SEQ, D)), ("y_sample", (B, 1, D)), ("shift_p", (1, 1, D)),
         ("wkv_p", (1, 1, H, N, N)), ("conv_p", (1, 1, 2, RW)), ("ffn_p", (1, 1, 2, 2 * FFN)),
         ("mem_k_p", (1, 1, NMEM, NXH, 256)), ("mem_v_p", (1, 1, NMEM, NXH, 256)), ("shift_s", (1, B, D)),
         ("wkv_s", (1, B, H, N, N)), ("conv_s", (1, B, 2, RW)), ("ffn_s", (1, B, 2, 2 * FFN)))
_UNUSED = ("v0", "v1", "v2")


def kernel(**inputs):
    import concourse.bacc as bacc
    from concourse.bass_utils import run_bass_kernel_spmd

    nc = bacc.Bacc("TRN2", target_bir_lowering=False, num_devices=1)
    arrays, I, O = {}, {}, {}
    for name, a in inputs.items():
        if name in _UNUSED:
            continue
        a = np.ascontiguousarray(a)
        arrays[f"in_{name}"] = a
        I[name] = nc.dram_tensor(f"in_{name}", a.shape, mybir.dt.from_np(a.dtype), kind="ExternalInput").ap()
    for name, shape in _OUTS:
        O[name] = nc.dram_tensor(f"out_{name}", shape, F32, kind="ExternalOutput").ap()
    hybrid_decoder_step(nc, I, O)
    r = run_bass_kernel_spmd(nc, [arrays], core_ids=[0])
    return tuple(r.results[0][f"out_{name}"] for name, _ in _OUTS)
```

```python
from contextlib import ExitStack, contextmanager

import numpy as np

import concourse.bass as bass
from concourse import mybir

F32 = mybir.dt.float32
F32R = mybir.dt.float32r
U8 = mybir.dt.uint8
BF16 = mybir.dt.bfloat16
ACT = mybir.ActivationFunctionType
ALU = mybir.AluOpType
AX = mybir.AxisListType

P = 128
D = 1024
KT = D // P
SEQ = 2048
TB = 512
NB = SEQ // TB
TT = TB // P
B = 8
H, N = 8, 64
NP = H // 2
C = 64
NC = TB // C
RW = H * N
NRW = 14
NIN = 26
NMEM = 256
NXH = 4
FFN = 2816
NF = FFN // P
EPS = 1e-6
GN_EPS = N * 1e-5
DECAY = float(np.exp(-0.5))
CACHE_OF = (0, 1, 2, 0, 1, 2, 0, 1, 2, 0, 1, 3, 4, 2, 0, 1)
NCACHE = max(CACHE_OF) + 1
XSCALE = 1.0 / 16
MERGES = (1, 2, 4, 8, 16, 32)

PAR, NPAR = {}, 0
for _n, _k in (("mu_shift", NRW), ("w0", 4), ("a0", 4), ("k_k", 4), ("k_a", 4), ("r_k", 4), ("ln_x_w", 4),
               ("ln_x_b", 4), ("norm_mix", 8), ("norm_x", 8), ("norm_mem", 8), ("norm_ffn", 8),
               ("norm_final", 8), ("conv_w", 12)):
    PAR[_n] = (NPAR, _k)
    NPAR += _k

NLD = len(PAR) + 11

LOOPS = {
    "sync.in": dict(lo_ready0=1, lo_ready1=1),
    "sync.out": dict(lo_ready0=1, lo_ready1=1),
    "sync.q": dict(lo_ready0=1, lo_ready1=1),
    "sync.o": dict(lo_ready0=1, lo_ready1=1),
    "sync.ffn": dict(lo_ready0=3, lo_ready1=3),
    "sync.block": dict(lo_ready0=58, lo_ready1=58, xin_free=1, x_whole=1, ws_free=1, x_out=16, y_go0=4, y_go1=4),
    "pool.mem": dict(hi_ready0=1, lo_ready0=1, hi_ready1=1, lo_ready1=1),
    "pool.in": dict(hi_ready0=1, lo_ready0=1, hi_ready1=1, lo_ready1=1),
    "pool.wkv": dict(gch=2, dec_readyG=2, ops_freeG=2, pool_qt=2, qt_free=2),
    "pool.out": dict(hi_ready0=1, lo_ready0=1, hi_ready1=1, lo_ready1=1),
    "pool.q": dict(hi_ready0=1, lo_ready0=1, hi_ready1=1, lo_ready1=1),
    "pool.o": dict(hi_ready0=1, lo_ready0=1, hi_ready1=1, lo_ready1=1),
    "pool.ffn": dict(gch=4, hi_ready0=3, lo_ready0=3, hi_ready1=3, lo_ready1=3, eb_ready0=1, eb_ready1=1,
         eb_ready2=1, eb_ready3=1),
    "pool.block": dict(gch=53, hi_ready0=58, lo_ready0=58, hi_ready1=58, lo_ready1=58, wkv_inG=1, dec_readyG=8,
         ops_freeG=8, pool_qt=8, qt_free=8, eb_ready0=11, eb_ready1=11, eb_ready2=11, eb_ready3=11),
    "pe.mem": dict(lo_ready0=1, free0=1, lo_ready1=1, free1=1),
    "pe.in": dict(lo_ready0=1, free0=1, lo_ready1=1, free1=1),
    "pe.gates": dict(lo_ready0=1, free0=1, lo_ready1=1, free1=1),
    "pe.wkv": dict(pool_ops=2, vec_ops0=1, vec_ops1=1, wk_vec4=9, wk_vec5=9, wk_vec6=9, wk_vec7=9, wk_vec0=9,
         wk_vec1=9, wk_vec2=9, wk_vec3=9, wk_act4=8, wk_act5=8, wk_act6=8, wk_act7=8, wk_act0=8,
         wk_act1=8, wk_act2=8, wk_act3=8),
    "pe.out": dict(lo_ready0=1, free0=1, lo_ready1=1, free1=1),
    "pe.q": dict(lo_ready0=1, free0=1, lo_ready1=1, free1=1),
    "pe.o": dict(lo_ready0=1, free0=1, lo_ready1=1, free1=1),
    "pe.ffn": dict(free4=1, free5=1, free6=1, free7=1, lo_ready0=3, free0=2, lo_ready1=3, free1=2, free3=2,
         free2=2, h_ready=2),
    "pe.block": dict(free4=32, free5=30, free6=33, free7=33, v2p=39, lo_ready0=58, free0=48, x_ready=40,
         lo_ready1=58, free1=53, xin_ready=16, free3=28, a2p=10, free2=27, pool_ops=8, vec_ops0=4,
         vec_ops1=4, wk_vec4=36, wk_vec5=36, wk_vec6=36, wk_vec7=36, wk_vec0=36, wk_vec1=36,
         wk_vec2=36, wk_vec3=36, wk_act4=32, wk_act5=32, wk_act6=32, wk_act7=32, wk_act0=32,
         wk_act1=32, wk_act2=32, wk_act3=32, kv_ready=32, h_ready=22),
    "pe.ins": dict(free4=1, free5=1, lo_ready0=1, free0=1, lo_ready1=1, free1=1),
    "pe.gatess": dict(free4=1, free5=1, lo_ready0=1, free0=1, lo_ready1=1, free1=1),
    "pe.outs": dict(free4=1, free5=1, lo_ready0=1, free0=1, lo_ready1=1, free1=1),
    "pe.qs": dict(free4=1, free5=1, lo_ready0=1, free0=1, lo_ready1=1, free1=1),
    "pe.os": dict(free4=1, free5=1, lo_ready0=1, free0=1, lo_ready1=1, free1=1),
    "pe.ffns": dict(free4=2, free5=2, free6=1, v2p=1, lo_ready0=3, free0=3, lo_ready1=3, free1=3, free3=3,
         free2=3, h_ready=2),
    "act.mem": dict(raw_ready0=16, raw_ready1=16, slab_done0=1, slab_done1=1),
    "act.shift": dict(ach=2, raw_ready0=16, raw_ready1=16, slab_done0=1, slab_done1=1, shf_free0=1, shf_free1=1),
    "act.gate_c": dict(ach=2, raw_ready0=16, raw_ready1=16, slab_done0=1, slab_done1=1),
    "act.h_in": dict(raw_ready0=16, raw_ready1=16, slab_done0=1, slab_done1=1),
    "act.wkv": dict(dec_freeV=2, dec_freeG=2, wk_mm4=15, wk_mm5=15, wk_mm6=15, wk_mm7=15, wk_mm0=15, wk_mm1=15,
         wk_mm2=15, wk_mm3=15),
    "act.out": dict(raw_ready0=16, raw_ready1=16, slab_done0=1, slab_done1=1, sq_free=2, xT_new=2),
    "act.q": dict(ach=2, raw_ready0=16, raw_ready1=16, slab_done0=1, slab_done1=1),
    "act.o": dict(raw_ready0=16, raw_ready1=16, slab_done0=1, slab_done1=1, sq_free=2, xT_new=2),
    "act.ffn": dict(ach=4, raw_ready0=48, raw_ready1=48, st_ready=2, slab_done0=3, slab_done1=3, v2a=2,
         eb_free0=1, eb_free1=1, eb_free2=1, eb_free3=1),
    "act.block": dict(ach=106, raw_ready0=928, raw_ready1=928, st_ready=58, slab_done0=58, slab_done1=58,
         fullA4=9, sq_free=40, fullA5=4, fullA6=16, fullA7=12, shf_free0=7, shf_free1=7, v2a=44,
         fullA3=1, wkv_inA=1, dec_freeV=8, dec_freeG=8, wk_mm4=60, wk_mm5=60, wk_mm6=60, wk_mm7=60,
         wk_mm0=60, wk_mm1=60, wk_mm2=60, wk_mm3=60, xT_new=24, pT_free=4, eb_free0=11, eb_free1=11,
         eb_free2=11, eb_free3=11, y_st0=32, y_st1=32),
    "act.ffns": dict(ach=4, raw_ready0=48, raw_ready1=48, st_ready=2, slab_done0=3, slab_done1=3, v2a=3,
         eb_free0=1, eb_free1=1, eb_free2=1, eb_free3=1),
    "dve.mem": dict(vch=2, slab_done0=1, slab_done1=1),
    "dve.shift": dict(vch=2, slab_done0=1, slab_done1=1, shf0=1, shf1=1),
    "dve.gate_c": dict(slab_done0=1, slab_done1=1),
    "dve.h_in": dict(vch=10, slab_done0=1, slab_done1=1),
    "dve.wkv": dict(vch=26, dec_readyV=2, wk_mm4=15, wk_mm5=15, wk_mm6=15, wk_mm7=15, wk_mm0=15, wk_mm1=15,
         wk_mm2=15, wk_mm3=15, pool_qt=2, wk_act4=8, wk_act5=8, wk_act6=8, wk_act7=8, wk_act0=8,
         wk_act1=8, wk_act2=8, wk_act3=8, wk_vec4=1, wk_vec5=1, wk_vec6=1, wk_vec7=1, wk_vec0=1,
         wk_vec1=1, wk_vec2=1, wk_vec3=1),
    "dve.out": dict(vch=4, slab_done0=1, slab_done1=1, sq_ready=2),
    "dve.q": dict(slab_done0=1, slab_done1=1),
    "dve.o": dict(vch=4, slab_done0=1, slab_done1=1, sq_ready=2),
    "dve.ffn": dict(fullV4=1, vch=20, fullV5=1, fullV6=1, a2v=2, sthi=2, slab_done0=3, slab_done1=3, st_ready=2,
         fullV1=1, fullV2=1, eb_carry0=1, eb_carry1=1, eb_carry2=1, eb_carry3=1, h_ready=2, fullV0=1),
    "dve.block": dict(fullV4=22, vch=517, fullV5=25, fullV6=16, fullV7=9, a2v=50, sthi=62, x_ready=40,
         slab_done0=58, slab_done1=58, sq_ready=32, v2p=8, st_ready=46, shf0=7, shf1=7, x_out=16,
         dec_readyV=8, wk_mm4=60, wk_mm5=60, wk_mm6=60, wk_mm7=60, wk_mm0=60, wk_mm1=60, wk_mm2=60,
         wk_mm3=60, pool_qt=8, wk_act4=32, wk_act5=32, wk_act6=32, wk_act7=32, wk_act0=32,
         wk_act1=32, wk_act2=32, wk_act3=32, wk_vec4=4, wk_vec5=4, wk_vec6=4, wk_vec7=4, wk_vec0=4,
         wk_vec1=4, wk_vec2=4, wk_vec3=4, x_back=16, fullV1=16, fullV2=15, fullV3=4, eb_carry0=11,
         eb_carry1=11, eb_carry2=11, eb_carry3=11, h_ready=22, fullV0=11, y_st0=32, y_st1=32),
    "dve.shifts": dict(vch=6, slab_done0=1, slab_done1=1, shf0=1, shf1=1),
    "dve.gate_cs": dict(vch=4, slab_done0=1, slab_done1=1),
    "dve.h_ins": dict(vch=14, slab_done0=1, slab_done1=1),
    "dve.outs": dict(vch=8, slab_done0=1, slab_done1=1, sq_ready=2),
    "dve.qs": dict(vch=4, slab_done0=1, slab_done1=1),
    "dve.os": dict(vch=8, slab_done0=1, slab_done1=1, sq_ready=2),
    "dve.ffns": dict(vch=45, a2v=3, sthi=2, slab_done0=3, slab_done1=3, st_ready=2, fullV1=2, fullV2=2,
         eb_carry0=1, eb_carry1=1, eb_carry2=1, eb_carry3=1, h_ready=2, fullV0=2),
}


class Counts:

    def __init__(self, eng, name, passed=None):
        self.eng, self.name, self.passed, self.n, self.turns = eng, name, passed, {}, []

    def __call__(self, sem, k=1):
        v = self.n[sem.name] = self.n.get(sem.name, 0) + k
        for i, per in self.turns:
            if per.get(sem.name):
                v = i * per[sem.name] + v
        return v

    def skip(self, sem, k):
        self.n[sem.name] = self.n.get(sem.name, 0) + k

    @contextmanager
    def loop(self, label, count):
        key = f"{self.name}.{label}"
        per, before = LOOPS.get(key, {}), dict(self.n)
        if self.passed is not None and self.turns:
            self.eng.sem_inc(self.passed, 1)
        with self.eng.Fori(0, count) as i:
            self.turns.append((i, per))
            yield i
            self.turns.pop()
        did = {s: v - before.get(s, 0) for s, v in self.n.items() if v != before.get(s, 0)}
        check_turn(key, per, did)
        for s, d in did.items():
            self.n[s] = before.get(s, 0) + d * count


def check_turn(key, per, did):
    assert per == did, f"{key}: a turn asks for {did}"


def hybrid_decoder_step(nc, I, O):
    ctx = ExitStack()
    with ctx:
        def sb(name, shape, dt=F32):
            return ctx.enter_context(nc.sbuf_tensor(name, shape, dt))

        def sem(name):
            return ctx.enter_context(nc.semaphore(name))

        def sems(name, n):
            return [sem(f"{name}{i}") for i in range(n)]

        psum = ctx.enter_context(nc.psum_tensor("psum", [P, 8, 512], F32))
        par = sb("par", [P, NPAR])
        omu = sb("omu", [P, NRW])
        oka = sb("oka", [P, 4])
        fcw = sb("fcw", [P, 3 * 2 * NF])
        lora_wa = sb("lora_wa", [P, RW])
        lora_g = sb("lora_g", [P, RW])
        ident = sb("ident", [P, P])
        ident64 = sb("ident64", [P, N])
        ones = sb("ones", [P, P])
        ones_bd = sb("ones_bd", [P, P])
        eps = sb("eps", [P, 2])
        gram_mask = sb("gram_mask", [P, 192])
        merge_mask = sb("merge_mask", [P, 6, 2, 64], U8)
        scan_mask = sb("scan_mask", [P, NC * (C + 1)], BF16)
        carry = sb("carry", [P, NRW])
        ccarry = sb("ccarry", [P, 4, 2])
        fcarry = sb("fcarry", [P, 2 * NF, 2])

        xT = sb("xT", [P, KT, TB])
        xhi = sb("xhi", [P, KT, TB], F32R)
        xlo = sb("xlo", [P, KT, TB], F32R)
        hhi = sb("hhi", [P, 2, TB], F32R)
        hlo = sb("hlo", [P, 2, TB], F32R)
        wraw = [sb(f"wraw{i}", [P, KT, P]) for i in range(2)]
        whi = [sb(f"whi{i}", [P, KT, P], F32R) for i in range(2)]
        wlo = [sb(f"wlo{i}", [P, KT, P], F32R) for i in range(2)]
        stage = sb("stage", [P, 2, TB])
        zr = sb("zr", [P, NRW * TB])
        cl = sb("cl", [P, 4 * NC * (C + 1)])
        kka = sb("kka", [P, 4, TB])
        kkn_y = sb("kkn_y", [P, 8, TB])
        shifted = sb("shifted", [P, 2, TB + 1])
        ops_b0 = sb("ops_b0", [P, NP, P])
        ops_k0 = sb("ops_k0", [P, NP, P])
        ops_v0 = sb("ops_v0", [P, NP, P])
        ops_ar = [sb(f"ops_ar{i}", [P, NP, 192]) for i in range(2)]
        gC = [sb(f"gC{i}", [P, NP]) for i in range(2)]
        ws = sb("ws", [P, NP * (384 + 512 + 256 + 128)])
        dec = sb("dec", [P, NP, C + 1])
        inv = sb("inv", [P, NP, C])
        S = sb("S", [P, NP, P])
        sm = sb("sm", [P, 96])
        xs = sb("xs", [P, KT, B])
        xsn = sb("xsn", [P, KT, 2 * B])
        xs2 = sb("xs2", [P, KT, 2, 2 * B], F32R)
        sconv = sb("sconv", [P, 4, 2 * B])
        sffn = sb("sffn", [P, 2 * NF, 2 * B])
        sp = sb("sp", [P, NIN, 2 * B])
        sz = sb("sz", [P, NRW, B])
        sw = sb("sw", [P, 12, 4, B])
        sh2 = sb("sh2", [P, 2, 2, B], F32R)
        shn = sb("shn", [P, KT, B + 1])
        sq_s = sb("sq_s", [P, KT, B])
        fin = sb("fin", [P, 176])

        Z = zr[:, :].rearrange("p (m t) -> p m t", m=NRW)
        q_sb = zr[:, 0:8 * TB].rearrange("p (m t) -> p m t", m=8)
        pT = zr[:, 8 * TB:12 * TB].rearrange("p (a m t) -> p a m t", a=2, m=2)
        pr = [zr[:, 12 * TB:12 * TB + NMEM], zr[:, 12 * TB + NMEM:13 * TB], zr[:, 13 * TB + 128:13 * TB + 128 + NMEM]]
        SCORE = (4, 5, 1)
        eb = zr[:, 0:4 * (TB + 2)].rearrange("p (a t) -> p a t", a=4)
        fc = zr[:, 5 * TB:9 * TB].rearrange("p (a t) -> p a t", a=4)
        yrow = zr[:, 10 * TB:14 * TB].rearrange("p (a d) -> p a d", a=2)
        cb = ws[:, 4 * TB:8 * TB + 8].rearrange("p (j t) -> p j t", j=4)
        L = cl[:, :].rearrange("p (j c t) -> p j c t", j=4, c=NC)
        Lf = cl[:, :].rearrange("p (j t) -> p j t", j=4)
        kkn, Y = kkn_y[:, 0:4, :], kkn_y[:, 4:8, :]
        kv_flat = kkn_y[:, :, :].rearrange("p a b -> p (a b)")
        xin = kv_flat.rearrange("p (t d) -> p t d", t=TT)
        def flat(t):
            return t.rearrange("p a b -> p (a b)")

        odd = flat(xT[:, :, :])

        def by_pair(t, a=None):
            return t.rearrange("p (q c) -> p q c", q=NP) if a is None else t.rearrange("p (q a c) -> p q a c", q=NP, a=a)

        GM = [by_pair(t, 2) for t in (ws[:, 0:1536], odd[:, 0:1536])]
        TM = [by_pair(t) for t in (ws[:, 1536:3584], odd[:, 1536:3584])]
        QT = [by_pair(t, 2) for t in (ws[:, 3584:4608], flat(stage[:, :, :]))]
        Zs = [by_pair(t) for t in (ws[:, 4608:5120], odd[:, 3584:4096])]
        Us = Zs
        ops_b = [ops_b0, by_pair(Z[:, 12, :])]
        ops_k = [ops_k0, by_pair(flat(shifted[:, :, :])[:, 0:TB])]
        ops_v = [ops_v0, by_pair(flat(shifted[:, :, :])[:, TB:2 * TB])]
        kmT = ws[:, 0:8 * NMEM].rearrange("p (m t) -> p m t", m=8)
        Vm = ws[:, 8 * NMEM:16 * NMEM].rearrange("p (m d) -> p m d", m=2)
        cache_buf = [kv_flat[:, 0:2048], kv_flat[:, 2048:4096], kka[:, :, :].rearrange("p a t -> p (a t)"),
                     ws[:, 0:2048], ws[:, 2048:4096]]
        gb = ws[:, 0:4 * TB].rearrange("p (j t) -> p j t", j=4)
        sscore = zr[:, 13 * TB:13 * TB + 64].rearrange("p (m c) -> p m c", m=2)
        sprobT = zr[:, 13 * TB + 64:13 * TB + 128]
        sprob = zr[:, 12 * TB:12 * TB + NMEM]
        sup = sp[:, :, :].rearrange("p a b -> p (a b)")[:, 0:2 * NF * B].rearrange("p (m b) -> p m b", b=B)
        acc = shifted[:, 0, 0:TB]
        kT_dram = nc.dram_tensor("mem_kT_scratch", (P, 8 * NMEM), F32, kind="Internal").ap()

        xT_dram = nc.dram_tensor("xT_scratch", (P, KT * TB), F32, kind="Internal").ap()

        def down_bank(k, samples):
            return k % 4 if samples else k

        def pcol(name, j, k=1):
            r = PAR[name][0]
            return par[:, bass.ds(r + j, k)]

        def half(ap, m, h):
            return ap.rearrange("p (q h w) -> p q h w", h=2, w=m)[:, :, h, :]

        consts = sem("consts")
        ld = sem("ld")
        fullA, fullV = sems("fullA", 8), sems("fullV", 8)
        free = sems("free", 8)
        raw_ready = sems("raw_ready", 2)
        slab_done = sems("slab_done", 2)
        hi_ready = sems("hi_ready", 2)
        lo_ready = sems("lo_ready", 2)
        st_ready = sem("st_ready")
        sthi = sem("sthi")
        x_ready = sem("x_ready")
        h_ready = sem("h_ready")
        xin_ready, xin_free = sem("xin_ready"), sem("xin_free")
        sq_ready, sq_free = sem("sq_ready"), sem("sq_free")
        xT_new = sem("xT_new")
        v2a, a2v = sem("v2a"), sem("a2v")
        v2p, a2p = sem("v2p"), sem("a2p")
        wkv_inA, wkv_inG = sem("wkv_inA"), sem("wkv_inG")
        dec_readyV, dec_readyG = sem("dec_readyV"), sem("dec_readyG")
        dec_freeV, dec_freeG = sem("dec_freeV"), sem("dec_freeG")
        pool_ops, vec_ops = sem("pool_ops"), sems("vec_ops", 2)
        ops_freeG = sem("ops_freeG")
        wk_mm, wk_act, wk_vec = sems("wk_mm", 8), sems("wk_act", 8), sems("wk_vec", 8)
        qt_free, pool_qt = sem("qt_free"), sem("pool_qt")
        shf, shf_free = sems("shf", 2), sems("shf_free", 2)
        ws_free = sem("ws_free")
        x_whole, x_out, x_back = sem("x_whole"), sem("x_out"), sem("x_back")
        kv_ready = sem("kv_ready")
        eb_ready = sems("eb_ready", 4)
        eb_carry = sems("eb_carry", 4)
        eb_free = sems("eb_free", 4)
        pT_free = sem("pT_free")
        y_go, y_st = sems("y_go", 2), sems("y_st", 2)
        out_go, out_st = sem("out_go"), sem("out_st")
        cache_in, cache_free = sems("cache_in", NCACHE), sems("cache_free", NCACHE)
        cache_done = sems("cache_done", NCACHE)
        s_state = sem("s_state")
        passedA, passedG, passedV = sem("passedA"), sem("passedG"), sem("passedV")
        vch, ach, gch = sem("vch"), sem("ach"), sem("gch")

        block = ctx.enter_context(nc.Block())

        def cols(w, m):
            return w[:, bass.ds(m * P, P)].rearrange("(k p) c -> p k c", p=P)

        w_in, w_out, wq, wk, wv, wo = (I[n][0] for n in ("w_in", "w_out", "wq", "wk", "wv", "wo"))
        w_up, w_down = I["w_up"][0], I["w_down"][0]

        @block.sync
        def _(e):
            c = Counts(e, "sync")

            def slab(i, src, first=False):
                if not first:
                    e.wait_ge(lo_ready[i], c(lo_ready[i]))
                e.dma_start(wraw[i][:, :, :], src).then_inc(raw_ready[i], 16)

            for name, (r, k) in PAR.items():
                src = I[name]
                if name == "conv_w":
                    src = src[0].rearrange("t (j p) -> (t j) p", p=P)
                elif name == "norm_final":
                    src = src.rearrange("(j p) -> j p", p=P)
                else:
                    src = src[0].rearrange("(j p) -> j p", p=P)
                e.dma_start(xT[r:r + k, 0, 0:P], src).then_inc(ld, 16)
            fw = I["ffn_conv_w"][0].rearrange("t (j p) -> (t j) p", p=P)
            e.dma_start(xT[:, 1, 0:P], fw[0:P, :]).then_inc(ld, 16)
            e.dma_start(xT[0:4, 2, 0:P], fw[P:3 * 2 * NF, :]).then_inc(ld, 16)
            e.dma_start(lora_wa[0:64, :], I["w2"][0]).then_inc(ld, 16)
            e.dma_start(lora_wa[64:128, :], I["a2"][0]).then_inc(ld, 16)
            e.dma_start(lora_g[:, :], I["g2"][0]).then_inc(ld, 16)
            for t in range(2):
                e.dma_start(xin[:, t, :], I["mem_prompt"][0, t * P:(t + 1) * P, :]).then_inc(ld, 16)
            e.dma_start(xin[0:B, 2, :], I["x_sample"][:, 0, :]).then_inc(ld, 16)
            e.dma_start(xin[B:2 * B, 2, :], I["state_shift"][0]).then_inc(ld, 16)
            e.dma_start(xin[0:2 * B, 3, 0:RW], I["state_conv"][0].rearrange("b r c -> (b r) c")).then_inc(ld, 16)
            e.dma_start(zr[0:2 * B, 0:2 * FFN], I["state_ffn"][0].rearrange("b r c -> (b r) c")).then_inc(ld, 16)
            for s in range(16):
                slab(s % 2, cols(wk if s < 8 else wv, s % 8), s < 2)

            def load_x(b):
                e.wait_ge(xin_free, c(xin_free))
                e.dma_start(xin, I["x_prompt"][0][bass.ds(b * TB, TB), :].rearrange("(t p) d -> p t d", p=P)
                            ).then_inc(xin_ready, 16)

            def ffn_up(i):
                for j in range(2):
                    slab(0, cols(w_up, 2 * i + j))
                    slab(1, cols(w_up, 2 * i + NF + j))

            def ffn_down(i):
                for j in range(2):
                    e.wait_ge(lo_ready[j], c(lo_ready[j]))
                    e.dma_start(wraw[j][:, :, :].rearrange("p (r k) c -> p r (k c)", r=2),
                                w_down[bass.ds(2 * i * P, 2 * P), j * TB:(j + 1) * TB].rearrange("(r p) c -> p r c", p=P)
                                ).then_inc(raw_ready[j], 16)

            def one_block(b, last):
                e.wait_ge(x_whole, c(x_whole))
                e.dma_start(xT_dram, xT[:, :, :].rearrange("p k t -> p (k t)")).then_inc(x_out, 16)
                with c.loop("in", NIN // 2 - 1) as i:
                    for j in range(2):
                        slab(j, cols(w_in, 2 * i + 2 + j))
                for name, w in (("out", w_out), ("q", wq), ("o", wo)):
                    for j in range(2):
                        slab(j, cols(w, j))
                    if name == "out":
                        memory_and_state(last)
                    if name == "o" and last:
                        sample_caches()
                    with c.loop(name, KT // 2 - 1) as i:
                        for j in range(2):
                            slab(j, cols(w, 2 * i + 2 + j))
                if not last:
                    load_x(b + 1)
                ffn_up(0)
                with c.loop("ffn", NF // 2 - 1) as i:
                    ffn_up(i + 1)
                    ffn_down(i)
                ffn_down(NF // 2 - 1)
                if not last:
                    for j in range(2):
                        slab(j, cols(w_in, j))
                for t in range(TT):
                    e.wait_ge(y_go[t % 2], c(y_go[t % 2], 2))
                    e.dma_start(O["y_prompt"][0][bass.ds(b * TB + t * P, P), :], yrow[:, t % 2, :]
                                ).then_inc(y_st[t % 2], 16)

            def memory_and_state(last):
                e.wait_ge(ws_free, c(ws_free))
                e.wait_ge(x_out, c(x_out, 16))
                e.dma_start(xT[:, :, :].rearrange("p k t -> p (k t)"), xT_dram).then_inc(x_back, 16)
                e.dma_start(ws[:, 0:8 * NMEM], kT_dram).then_inc(kv_ready, 16)
                e.dma_start(Vm, O["mem_v_p"][0, 0].rearrange("(m p) h d -> p m (h d)", p=P)
                            ).then_inc(kv_ready, 16)
                if last:
                    for h in range(2):
                        for s in range(2):
                            src = I["state_wkv"][0, 4 * s:4 * s + 4].rearrange("b (q h) v k -> h v q b k", h=2)[h]
                            dst = cl[64 * h:64 * h + 64, 0:2048].rearrange("v (q b k) -> v q b k", q=NP, b=B)
                            for q in range(NP):
                                e.dma_start(dst[:, q, 4 * s:4 * s + 4, :], src[:, q]).then_inc(s_state, 16)

            def sample_caches():
                for n in range(2 * B):
                    i, src = CACHE_OF[n], I["cache_mem_k" if n < B else "cache_mem_v"][0, n % B]
                    e.wait_ge(cache_free[i], c(cache_free[i]))
                    e.dma_start(cache_buf[i].rearrange("p (m d) -> p m d", m=2),
                                src.rearrange("(m p) h d -> p m (h d)", p=P)).then_inc(cache_in[i], 16)

            for n in range(2):
                e.wait_ge(out_go, c(out_go))
                e.dma_start(O["mem_v_p" if n else "mem_k_p"][0, 0].rearrange("(m p) h d -> p m (h d)", p=P),
                            kv_flat[:, n * 2048:(n + 1) * 2048].rearrange("p (m d) -> p m d", m=2)
                            ).then_inc(out_st, 16)
            e.dma_start(kT_dram, zr[:, 8 * NMEM:16 * NMEM]).then_inc(out_st, 16)
            e.wait_ge(out_st, c(out_st, 48))
            for j in range(2):
                slab(j, cols(w_in, j))
            load_x(0)
            with c.loop("block", NB - 1) as b:
                one_block(b, False)
            one_block(NB - 1, True)

            def put(dst, src):
                e.dma_start(dst, src).then_inc(out_st, 16)

            put(O["conv_s"][0, :, 0, :], I["state_conv"][0, :, 1, :])
            put(O["ffn_s"][0, :, 0, :], I["state_ffn"][0, :, 1, :])
            e.wait_ge(out_go, c(out_go))
            def rows(a, n):
                return zr[0:n, a:a + 8 * P].rearrange("m (b p) -> m b p", b=8)

            put(O["ffn_s"][0, :, 1, :].rearrange("b (m p) -> m b p", p=P), rows(0, 2 * NF))
            put(O["conv_s"][0, :, 1, :].rearrange("b (j p) -> j b p", p=P), rows(8 * P, 4))
            put(O["ffn_p"][0, 0].rearrange("r (m p) -> m r p", p=P), rows(16 * P, 2 * NF)[:, 0:2, :])
            put(O["shift_s"][0].rearrange("b (k p) -> (b k) p", p=P), zr[0:64, 18 * P:19 * P])
            put(O["y_sample"][:, 0, :].rearrange("b (k p) -> (b k) p", p=P), zr[0:64, 19 * P:20 * P])
            put(O["shift_p"][0, 0].rearrange("(k p) -> k p", p=P), zr[0:8, 20 * P:21 * P])
            put(O["conv_p"][0, 0].rearrange("r (j p) -> (r j) p", p=P), zr[0:8, 21 * P:22 * P])
            for h in range(2):
                put(O["wkv_p"][0, 0].rearrange("(q h) v k -> h v q k", h=2)[h],
                    zr[64 * h:64 * h + 64, 22 * P:26 * P].rearrange("v (q x) -> v q x", q=NP)[:, :, 64 * h:64 * h + 64])
                for q in range(NP):
                    put(O["wkv_s"][0].rearrange("b (q h) v k -> h q v b k", h=2)[h, q],
                        cl[64 * h:64 * h + 64, 0:2048].rearrange("v (q b k) -> v q b k", q=NP, b=B)[:, q])
            e.wait_ge(out_st, c(out_st, 16 * 19))
            e.wait_ge(y_st[0], c(y_st[0], 16 * NB * TT // 2))
            e.wait_ge(y_st[1], c(y_st[1], 16 * NB * TT // 2))

        @block.gpsimd
        def _(e):
            c = Counts(e, "pool", passedG)
            last = [0]

            def select(dst, src, op, fill, base, pattern, ch):
                e.affine_select(out=dst, in_=src, compare_op=op, fill=fill, base=base, pattern=pattern,
                                channel_multiplier=ch).then_inc(gch, 1)
                e.wait_ge(gch, c(gch))

            for t, v in ((ident, 0.0), (ones, 1.0), (ones_bd, 0.0), (S, 0.0), (carry, 0.0), (ccarry, 0.0),
                         (fcarry, 0.0), (Zs[0], 0.0), (gram_mask, 1.0), (ident64, 0.0),
                         (scan_mask, 1.0), *((t, 0.0) for t in (ops_b0, ops_k0, ops_v0, *ops_ar))):
                e.memset(t[:], v).then_inc(gch, 1)
                e.wait_ge(gch, c(gch))
            e.memset(eps[:, 0:1], EPS).then_inc(gch, 1)
            e.wait_ge(gch, c(gch))
            e.memset(eps[:, 1:2], GN_EPS).then_inc(gch, 1)
            e.wait_ge(gch, c(gch))
            e.memset(scan_mask[:, :].rearrange("p (c t) -> p c t", c=NC)[:, :, 0:1], 0.0).then_inc(gch, 1)
            e.wait_ge(gch, c(gch))
            select(ident[:, :], ident[:, :], ALU.not_equal, 1.0, 0, [[-1, P]], 1)
            for h in range(2):
                a = slice(64 * h, 64 * h + 64)
                e.memset(ones_bd[a, a], 1.0).then_inc(gch, 1)
                e.wait_ge(gch, c(gch))
                select(ident64[a, :], ident64[a, :], ALU.not_equal, 1.0, 0, [[-1, N]], 1)
                e.memset(gram_mask[a, 64 * (1 - h):64 * (1 - h) + 64], 0.0).then_inc(gch, 1)
                e.wait_ge(gch, c(gch))
                select(gram_mask[a, a], gram_mask[a, a], ALU.is_gt, 0.0, 0, [[1, N]], -1)
                select(gram_mask[a, 128:192], gram_mask[a, 128:192], ALU.is_ge, 0.0, 0, [[1, N]], -1)
            for l, m in enumerate(MERGES):
                for side in range(2):
                    t, inner = stage[:, 1, 0:P], stage[:, 0, 0:P]
                    e.memset(t, 1.0).then_inc(gch, 1)
                    e.wait_ge(gch, c(gch))
                    e.memset(inner, 1.0).then_inc(gch, 1)
                    e.wait_ge(gch, c(gch))
                    for dst, w in ((t, 2 * m), (inner, m)):
                        v = dst.rearrange("p (q w) -> p q w", w=w)
                        select(v, v, ALU.is_ge, 0.0, 0, [[-w, P // w], [0, w]], 1)
                        select(v, v, ALU.is_ge, 0.0, w - 1, [[w, P // w], [0, w]], -1)
                    e.tensor_tensor(t, t, inner, ALU.subtract).then_inc(gch, 1)
                    e.wait_ge(gch, c(gch))
                    select(t, t, ALU.is_gt, 0.0, 0, [[-1 if side else 1, P]], 1 if side else -1)
                    e.tensor_copy(merge_mask[:, l, side, :].rearrange("p (q w) -> p q w", w=m),
                                  t.rearrange("p (q h w) -> p q h w", h=2, w=m)[:, :, 1 - side, :]).then_inc(gch, 1)
                    e.wait_ge(gch, c(gch))
            for i in range(2):
                e.sem_inc(shf_free[i], 1)
            for s in (dec_freeV, dec_freeG, ops_freeG, ops_freeG):
                e.sem_inc(s, 1)
            for i in range(8):
                e.sem_inc(free[i], 1)
            for i in range(4):
                e.sem_inc(eb_free[i], 1)
            e.sem_inc(consts, 1)

            def split(i):
                e.wait_ge(hi_ready[i], c(hi_ready[i]))
                c.skip(lo_ready[i], 1)
                return e.tensor_tensor(wlo[i][:, :, :], wraw[i][:, :, :], whi[i][:, :, :].bitcast(F32),
                                       ALU.subtract).then_inc(lo_ready[i], 1)

            def splits(label, pairs):
                with c.loop(label, pairs):
                    split(0)
                    split(1)

            def unit(i):
                e.tensor_copy(QT[i][:, :, :, :], ident[:, :].unsqueeze(1).unsqueeze(1).broadcast_to([P, NP, 2, P])
                              ).then_inc(pool_qt, 1)
                c.skip(pool_qt, 1)
                e.wait_ge(pool_qt, c(pool_qt, 0))

            def operands(i, t0, first=False):
                e.wait_ge(dec_readyG, c(dec_readyG))
                e.sem_inc(passedG, 1)
                e.wait_ge(ops_freeG, c(ops_freeG))
                e.sem_inc(passedG, 1)
                for h in range(2):
                    a = slice(64 * h, 64 * h + 64)
                    e.tensor_tensor(ops_b[i][a, :, a], kka[a, :, bass.ds(t0, C)], inv[a, :, :], ALU.mult)
                    ins = e.tensor_tensor(ops_k[i][a, :, a], Z[a, 4:8, bass.ds(t0, C)], inv[a, :, :], ALU.mult)
                    if h:
                        ins.then_inc(dec_freeG, 1)
                    ins = e.tensor_copy(ops_v[i][a, :, a], Z[a, 8:12, bass.ds(t0, C)])
                ins.then_inc(gch, 1)
                e.wait_ge(gch, c(gch))
                e.sem_inc(pool_ops, 1)
                if not first:
                    e.wait_ge(qt_free, c(qt_free))
                    e.sem_inc(passedG, 1)
                unit(i)

            def carries(a, tile):
                e.wait_ge(eb_ready[a], c(eb_ready[a]))
                e.sem_inc(passedG, 1)
                e.tensor_copy(eb[:, a, 0:2], fcarry[:, bass.ds(tile, 1), :].rearrange("p a b -> p (a b)")).then_inc(gch, 1)
                e.wait_ge(gch, c(gch))
                e.sem_inc(passedG, 1)
                e.tensor_copy(fcarry[:, bass.ds(tile, 1), :].rearrange("p a b -> p (a b)"),
                              eb[:, a, TB:TB + 2]).then_inc(eb_carry[a], 1)

            def up(i):
                for a, tile in ((0, 2 * i), (1, 2 * i + NF), (2, 2 * i + 1), (3, 2 * i + NF + 1)):
                    split(a % 2)
                    carries(a, tile)

            def one_block(b, last):
                splits("in", NIN // 2)
                e.wait_ge(lo_ready[1], c(lo_ready[1], 0))
                e.wait_ge(wkv_inG, c(wkv_inG))
                e.sem_inc(passedG, 1)
                for h in range(2):
                    a = slice(64 * h, 64 * h + 64)
                    for t in (ops_b[1], ops_k[1], ops_v[1]):
                        ins = e.memset(t[a, :, 64 * (1 - h):64 * (1 - h) + 64], 0.0)
                ins.then_inc(gch, 1)
                e.wait_ge(gch, c(gch))
                operands(0, 0, True)
                operands(1, C, True)
                with c.loop("wkv", NC // 2 - 1) as j:
                    operands(0, j * (2 * C) + 2 * C)
                    operands(1, j * (2 * C) + 3 * C)
                c.skip(qt_free, 2)
                splits("out", KT // 2)
                splits("q", KT // 2)
                splits("o", KT // 2)
                up(0)
                with c.loop("ffn", NF // 2 - 1) as i:
                    up(i + 1)
                    split(0)
                    split(1)
                if not last:
                    split(0)
                    split(1)

            split(0)
            split(1)
            splits("mem", 8)
            with c.loop("block", NB - 1) as b:
                one_block(b, False)
            one_block(NB - 1, True)

        @block.tensor
        def _(e):
            c = Counts(e, "pe")

            def mm(out, lhsT, rhs, start=True, stop=True):
                return e.matmul(out, lhsT, rhs, start=start, stop=stop)

            def tr(out, src):
                n = src.shape[0]
                return e.transpose(out, src, ident[0:n, 0:n])

            def three(out, i, k, hi, lo, start, stop):
                mm(out, whi[i][:, k, :], hi, start, False)
                mm(out, whi[i][:, k, :], lo, False, False)
                return mm(out, wlo[i][:, k, :], hi, False, stop)

            def two(out, i, k, x, start, stop):
                n = x.shape[2]
                mm(out, whi[i][:, k, :], x, start, False)
                mm(out[:, 0:n], wlo[i][:, k, :], x[:, 0, :], False, stop)

            def dense(i, bk, sample=0, order=None, n=TB):
                e.wait_ge(lo_ready[i], c(lo_ready[i]))
                e.wait_ge(free[bk], c(free[bk]))
                if sample:
                    e.wait_ge(free[4 + i], c(free[4 + i]))
                    for k in range(KT):
                        two(psum[:, 4 + i, 0:4 * B], i, k, xs2[:, k, :, :], k == 0, k == KT - 1)
                for j, k in enumerate(order or range(KT)):
                    if order:
                        e.wait_ge(x_ready, c(x_ready))
                    ins = three(psum[:, bk, 0:n], i, k, xhi[:, k, 0:n], xlo[:, k, 0:n], j == 0, j == KT - 1)
                ins.then_inc(slab_done[i], 1)

            def phase(label, pairs, sample=0, order=tuple(range(KT)), n=TB):
                if sample:
                    e.wait_ge(v2p, c(v2p))
                dense(0, 0, sample, order, n)
                dense(1, 1, sample, None, n)
                if pairs > 1:
                    with c.loop(label + "s" * bool(sample), pairs - 1):
                        dense(0, 0, sample, None, n)
                        dense(1, 1, sample, None, n)

            def stats():
                e.wait_ge(v2p, c(v2p))
                e.wait_ge(free[4], c(free[4]))
                for t in range(TT):
                    ins = mm(psum[:, 4, t:t + 1], acc[:, t * P:(t + 1) * P], ones[:, 0:1])
                ins.then_inc(fullA[4], 1)
                e.wait_ge(v2p, c(v2p))
                e.wait_ge(free[5], c(free[5]))
                for t in range(TT):
                    ins = tr(psum[:, 5, t * P:(t + 1) * P], sm[:, 4 + t:5 + t].broadcast_to([P, P]))
                ins.then_inc(fullV[5], 1)

            def sample_stats():
                e.wait_ge(v2p, c(v2p))
                e.wait_ge(free[6], c(free[6]))
                mm(psum[:, 6, 0:B], ones[:, :], sw[:, 11, 0, :]).then_inc(fullA[6], 1)

            e.wait_ge(consts, c(consts))
            e.wait_ge(ld, c(ld, 16 * NLD))
            e.wait_ge(free[4], c(free[4]))
            tr(psum[:, 4, 0:NPAR], xT[0:NPAR, 0, 0:P]).then_inc(fullV[4], 1)
            e.wait_ge(free[5], c(free[5]))
            tr(psum[:, 5, 0:P], xT[:, 1, 0:P])
            tr(psum[:, 5, P:P + 4], xT[0:4, 2, 0:P]).then_inc(fullV[5], 1)
            e.wait_ge(free[6], c(free[6]))
            for k in range(KT):
                tr(psum[:, 6, 16 * k:16 * k + 16], xin[0:16, 2, k * P:(k + 1) * P])
            for k in range(4):
                ins = tr(psum[:, 6, 128 + 16 * k:144 + 16 * k], xin[0:16, 3, k * P:(k + 1) * P])
            ins.then_inc(fullV[6], 1)
            for g in range(2):
                e.wait_ge(free[7], c(free[7]))
                for m in range(22):
                    a = (22 * g + m) * P
                    ins = tr(psum[:, 7, 16 * m:16 * m + 16], zr[0:16, a:a + P])
                ins.then_inc(fullV[7], 1)
            e.wait_ge(v2p, c(v2p))
            for k in range(KT):
                bk = 4 + k % 4
                e.wait_ge(free[bk], c(free[bk]))
                for t in range(2):
                    ins = tr(psum[:, bk, t * P:(t + 1) * P], xin[:, t, k * P:(k + 1) * P])
                ins.then_inc(fullV[bk], 1)
            phase("mem", 8, n=NMEM)
            for kv in range(2):
                e.wait_ge(v2p, c(v2p))
                for t in range(2):
                    for g in range(2):
                        bk = 4 + 2 * t + g
                        e.wait_ge(free[bk], c(free[bk]))
                        for k in range(4):
                            a = (8 + 8 * kv + 4 * g + k) * NMEM + t * P
                            ins = tr(psum[:, bk, k * P:(k + 1) * P], zr[:, a:a + P])
                        ins.then_inc(fullV[bk], 1)

            def wkv_pair(first=False):
                both = [(i, p) for i in range(2) for p in range(NP)]

                def bank(i, p):
                    return 4 * (1 - i) + p

                for i in range(2):
                    e.wait_ge(pool_ops, c(pool_ops))
                    e.wait_ge(vec_ops[i], c(vec_ops[i]))
                    for p in range(NP):
                        bk = bank(i, p)
                        if i and not first:
                            e.wait_ge(wk_vec[bk], c(wk_vec[bk]))
                        mm(psum[:, bk, 0:192], ops_b[i][:, p, :], ops_ar[i][:, p, :])
                        mm(psum[:, bk, 192:384], ops_k[i][:, p, :], ops_ar[i][:, p, :]).then_inc(wk_mm[bk], 1)
                for i, p in both:
                    bk = bank(i, p)
                    e.wait_ge(wk_vec[bk], c(wk_vec[bk]))
                    for j, src in enumerate((ops_b[i][:, p, :], ops_k[i][:, p, :], ops_v[i][:, p, :], GM[i][:, p, 0, 0:P])):
                        ins = tr(psum[:, bk, j * P:(j + 1) * P], src)
                    ins.then_inc(wk_mm[bk], 1)
                for l in range(1, len(MERGES)):
                    m = MERGES[l]
                    for i, p in both:
                        bk = bank(i, p)
                        if l == 1:
                            e.wait_ge(wk_act[bk], c(wk_act[bk]))
                        e.wait_ge(wk_vec[bk], c(wk_vec[bk]))
                        mm(psum[:, bk, 0:64], TM[i][:, p, 384:512], half(QT[i][:, p, 0, :], m, 1)).then_inc(wk_mm[bk], 1)
                    for i, p in both:
                        bk = bank(i, p)
                        e.wait_ge(wk_act[bk], c(wk_act[bk]))
                        ins = mm(psum[:, bk, 0:64], QT[i][:, p, 1, :], half(Zs[i][:, p, :], m, 1))
                        if l < len(MERGES) - 1:
                            ins = mm(psum[:, bk, 64:128], Zs[i][:, p, :], half(QT[i][:, p, 1, :], m, 0))
                        ins.then_inc(wk_mm[bk], 1)
                for i in range(2):
                    for p in range(NP):
                        bk = bank(i, p)
                        e.wait_ge(wk_vec[bk], c(wk_vec[bk]))
                        if i:
                            e.wait_ge(wk_vec[bank(0, p)], c(wk_vec[bank(0, p)]))
                        mm(psum[:, bk, 0:P], ops_ar[i][:, p, 0:P], S[:, p, :], True, False)
                        mm(psum[:, bk, 0:P], GM[i][:, p, 1, 0:P], TM[i][:, p, 256:384], False, True).then_inc(wk_mm[bk], 1)
                    for p in range(NP):
                        bk = bank(i, p)
                        e.wait_ge(wk_act[bk], c(wk_act[bk]))
                        mm(psum[:, bk, 0:P], QT[i][:, p, 0, :], Zs[i][:, p, :]).then_inc(wk_mm[bk], 1)
                    for p in range(NP):
                        bk = bank(i, p)
                        e.wait_ge(wk_vec[bk], c(wk_vec[bk]))
                        y, s = psum[:, bk, 0:C], psum[:, bk, P:2 * P]
                        mm(s, TM[i][:, p, 0:P], Us[i][:, p, :], True, False)
                        mm(s, TM[i][:, p, P:2 * P], TM[i][:, p, 256:384], False, True)
                        mm(y, S[:, p, :], ops_ar[i][:, p, P:192], True, False)
                        mm(y, Us[i][:, p, :], GM[i][:, p, 0, P:192], False, False)
                        mm(y, TM[i][:, p, 256:384], GM[i][:, p, 1, P:192], False, True).then_inc(wk_mm[bk], 1)
                        c.skip(wk_act[bk], 1)

            def attention(last):
                e.wait_ge(kv_ready, c(kv_ready, 32))
                units = [(h, t) for h in range(NXH) for t in range(TT)]

                def sample_query(s):
                    e.wait_ge(v2p, c(v2p))
                    e.wait_ge(free[0], c(free[0]))
                    mm(psum[:, 0, :], ones[:, :], shifted[:, s % 2, 0:TB]).then_inc(fullV[0], 1)

                def scores(n):
                    h, t = units[n]
                    bk = SCORE[n % 3]
                    e.wait_ge(free[bk], c(free[bk]))
                    for d in range(2):
                        ins = mm(psum[:, bk, 0:NMEM], q_sb[:, 2 * h + d, t * P:(t + 1) * P], kmT[:, 2 * h + d, :],
                                 d == 0, d == 1)
                    ins.then_inc(fullV[bk], 1)

                e.wait_ge(a2p, c(a2p))
                scores(0)
                scores(1)
                for n, (h, t) in enumerate(units):
                    if n + 2 < len(units):
                        scores(n + 2)
                    bk = 6 + n % 2
                    e.wait_ge(v2p, c(v2p))
                    e.wait_ge(free[bk], c(free[bk]))
                    for m in range(2):
                        ins = tr(psum[:, bk, m * P:(m + 1) * P], pr[n % 3][:, m * P:(m + 1) * P])
                    ins.then_inc(fullA[bk], 1)
                    if t == TT - 1:
                        e.wait_ge(a2p, c(a2p))
                        for d in range(2):
                            e.wait_ge(free[2 + d], c(free[2 + d]))
                            for m in range(2):
                                a = (2 * h + d) * P
                                ins = mm(psum[:, 2 + d, :], Vm[:, m, a:a + P], pT[:, h % 2, m, :], m == 0, m == 1)
                            ins.then_inc(fullV[2 + d], 1)
                    if last and n:
                        sample_query(n - 1)
                if last:
                    sample_query(2 * B - 1)

            def ffn_up(sample, order=None):
                for j in range(2):
                    dense(0, 2 * j, sample, order if j == 0 else None)
                    dense(1, 2 * j + 1, sample)

            def ffn_down(sample):
                e.wait_ge(h_ready, c(h_ready, 2))
                if sample:
                    e.wait_ge(v2p, c(v2p))
                    e.wait_ge(free[6], c(free[6]))
                for i in range(2):
                    e.wait_ge(lo_ready[i], c(lo_ready[i]))
                    if sample:
                        for k in range(4):
                            a = (4 * i + k) * 2 * B
                            for j in range(2):
                                two(psum[:, 6, a:a + 2 * B], i, 4 * j + k, sh2[:, j, :, :], j == 0, j == 1)
                    for k in range(4):
                        bk = down_bank(4 * i + k, sample)
                        e.wait_ge(free[bk], c(free[bk]))
                        three(psum[:, bk, :], i, k, hhi[:, 0, :], hlo[:, 0, :], True, False)
                        ins = three(psum[:, bk, :], i, 4 + k, hhi[:, 1, :], hlo[:, 1, :], False, True)
                        ins.then_inc(slab_done[i] if k == 3 else fullV[bk], 1)

            def one_block(b, last):
                e.wait_ge(xin_ready, c(xin_ready, 16))
                for k in range(KT):
                    bk = 4 + k % 4
                    e.wait_ge(free[bk], c(free[bk]))
                    for t in range(TT):
                        ins = tr(psum[:, bk, t * P:(t + 1) * P], xin[:, t, k * P:(k + 1) * P])
                    ins.then_inc(fullA[bk], 1)
                stats()
                if last:
                    sample_stats()
                s = 2 * B if last else 0
                phase("in", NRW // 2, s)

                def lora(a):
                    for p in range(NP):
                        e.wait_ge(free[4 + p], c(free[4 + p]))
                        mm(psum[:, 4 + p, :], lora_wa[a, p * P:(p + 1) * P], Z[a, 12, :]).then_inc(fullA[4 + p], 1)

                dense(0, 0, s)
                dense(1, 1, s)
                e.wait_ge(v2p, c(v2p))
                e.wait_ge(free[3], c(free[3]))
                sq = (stage[:, 0, :], stage[:, 1, :], shifted[:, 0, 0:TB], shifted[:, 1, 0:TB])
                for p in range(NP):
                    for t in range(TT):
                        ins = mm(psum[:, 3, 8 * p + 2 * t:8 * p + 2 * t + 2], sq[p][:, t * P:(t + 1) * P], ones_bd[:, 0:P:N])
                ins.then_inc(fullA[3], 1)
                e.wait_ge(a2p, c(a2p))
                lora(slice(64, 128))
                dense(0, 0, s)
                dense(1, 1, s)
                e.wait_ge(v2p, c(v2p))
                head_rows(8)
                with c.loop("gates" + "s" * last, 4):
                    dense(0, 0, s)
                    dense(1, 1, s)
                lora(slice(0, 64))
                for p in range(8):
                    e.wait_ge(free[p], c(free[p]))
                wkv_pair(True)
                with c.loop("wkv", NC // 2 - 1):
                    wkv_pair()
                for p in range(NP):
                    e.wait_ge(wk_vec[p], c(wk_vec[p]))
                    e.sem_inc(free[4 + p], 1)
                    e.sem_inc(free[p], 1)
                for p in range(NP):
                    e.wait_ge(v2p, c(v2p))
                    e.wait_ge(free[4 + p], c(free[4 + p]))
                    mm(psum[:, 4 + p, :], ones_bd[:, :], shifted[:, p % 2, 0:TB]).then_inc(fullV[4 + p], 1)
                for p in range(NP):
                    e.wait_ge(free[4 + p], c(free[4 + p]))
                    mm(psum[:, 4 + p, :], ones_bd[:, :], Y[:, p, :]).then_inc(fullV[4 + p], 1)
                e.wait_ge(a2p, c(a2p, NP))
                e.wait_ge(free[4], c(free[4]))
                for p in range(NP):
                    for t in range(TT):
                        ins = mm(psum[:, 4, 8 * p + 2 * t:8 * p + 2 * t + 2], kkn[:, p, t * P:(t + 1) * P], ones_bd[:, 0:P:N])
                ins.then_inc(fullA[4], 1)
                e.wait_ge(v2p, c(v2p))
                head_rows(8)
                for p in range(NP):
                    e.wait_ge(free[4 + p], c(free[4 + p]))
                    mm(psum[:, 4 + p, :], lora_g[:, p * P:(p + 1) * P], Z[:, 13, :]).then_inc(fullV[4 + p], 1)
                if last:
                    sample_wkv()
                phase("out", KT // 2, B if last else 0, (4, 5, 6, 7, 0, 1, 2, 3))
                stats()
                if last:
                    sample_stats()
                phase("q", KT // 2, B if last else 0)
                attention(last)
                if last:
                    sample_attention()
                phase("o", KT // 2, B if last else 0)
                stats()
                if last:
                    sample_stats()
                s = B if last else 0
                if s:
                    e.wait_ge(v2p, c(v2p))
                ffn_up(s, tuple(range(KT)))
                with c.loop("ffn" + "s" * last, NF // 2 - 1):
                    ffn_up(s)
                    ffn_down(s)
                ffn_down(s)
                stats()
                for t in range(TT):
                    for g in range(2):
                        bk = 6 + g
                        e.wait_ge(free[bk], c(free[bk]))
                        for k in range(4):
                            if t == 0:
                                e.wait_ge(v2p, c(v2p))
                            ins = tr(psum[:, bk, k * P:(k + 1) * P], xT[:, 4 * g + k, t * P:(t + 1) * P])
                        ins.then_inc(fullV[7] if g else fullA[6], 1)
                if last:
                    sample_stats()

            def head_rows(col):
                for p in range(NP):
                    e.wait_ge(free[4 + p], c(free[4 + p]))
                    for t in range(TT):
                        for h in range(2):
                            a = col + 32 + 8 * p + 2 * t + h
                            ins = mm(psum[64 * h:64 * h + 64, 4 + p, t * P:(t + 1) * P],
                                     sm[:, a:a + 1].broadcast_to([P, N]), ident[:, :])
                    ins.then_inc(fullV[4 + p], 1)

            def sample_wkv():
                e.wait_ge(a2p, c(a2p))
                e.wait_ge(free[6], c(free[6]))
                e.wait_ge(free[7], c(free[7]))
                for j in range(2):
                    a = slice(64 * j, 64 * j + 64)
                    for p in range(NP):
                        ins = mm(psum[:, 6 + j, 8 * p:8 * p + 8], lora_wa[a, p * P:(p + 1) * P], sz[a, 12, :])
                ins.then_inc(fullA[7], 1)
                for p in range(NP):
                    ins = mm(psum[:, 6, 64 + 8 * p:72 + 8 * p], lora_g[:, p * P:(p + 1) * P], sz[:, 13, :])
                ins.then_inc(fullA[6], 1)

                def head_sum():
                    e.wait_ge(v2p, c(v2p))
                    e.wait_ge(free[7], c(free[7]))
                    return mm(psum[:, 7, 0:4 * B], ones_bd[:, :], sw[:, 11, :, :].rearrange("p a b -> p (a b)"))

                head_sum().then_inc(fullA[7], 1)
                for j in range(5):
                    a = 4 * (j % 2)
                    e.wait_ge(v2p, c(v2p))
                    for g in range(a, a + 4):
                        e.wait_ge(free[g], c(free[g]))
                        ins = mm(psum[:, g, :], ones_bd[:, :], kkn_y[:, g, :])
                    ins.then_inc(fullV[a + 3], 1)
                head_sum().then_inc(fullV[7], 1)
                head_sum().then_inc(fullV[7], 1)
                head_sum().then_inc(fullA[7], 1)

            def sample_attention():
                e.wait_ge(v2p, c(v2p))
                e.wait_ge(free[6], c(free[6]))
                for m in range(2):
                    ins = tr(psum[0:32, 6, m * P:(m + 1) * P], sscore[:, m, :])
                ins.then_inc(fullV[6], 1)
                e.wait_ge(v2p, c(v2p))
                e.wait_ge(free[7], c(free[7]))
                for m in range(2):
                    ins = tr(psum[:, 7, m * 32:(m + 1) * 32], sprob[0:32, m * P:(m + 1) * P])
                ins.then_inc(fullV[7], 1)
                e.wait_ge(v2p, c(v2p))
                e.wait_ge(free[6], c(free[6]))
                for b in range(B):
                    n = B + b
                    i = CACHE_OF[n]
                    e.wait_ge(cache_in[i], c(cache_in[i], 16 * CACHE_OF[:n + 1].count(i) if i not in CACHE_OF[B:n] else 16))
                    for k in range(KT):
                        for m in range(2):
                            a = m * D + k * P
                            o = m * 32 + b * NXH + k // 2
                            ins = mm(psum[:, 6, k * B + b:k * B + b + 1], cache_buf[i][:, a:a + P], sprobT[:, o:o + 1],
                                     m == 0, m == 1)
                    ins.then_inc(cache_done[i], 1)

            with c.loop("block", NB - 1) as b:
                one_block(b, False)
            one_block(NB - 1, True)
            e.wait_ge(v2p, c(v2p))
            new = fin[:, 80:112].rearrange("p (j b) -> p j b", j=4)
            for g in range(2):
                for src, bk, n in ((sup, 0, 2 * NF), (new, 2, 4)):
                    e.wait_ge(free[bk + g], c(free[bk + g]))
                    for b in range(4):
                        ins = tr(psum[0:n, bk + g, b * P:(b + 1) * P], src[:, :, 4 * g + b])
                    ins.then_inc(fullA[bk + g], 1)
            e.wait_ge(free[5], c(free[5]))
            for r in range(2):
                ins = tr(psum[0:2 * NF, 5, r * P:(r + 1) * P], fcarry[:, :, r])
            ins.then_inc(fullA[5], 1)
            e.wait_ge(free[4], c(free[4]))
            tr(psum[0:64, 4, 0:P], fin[:, 0:64])
            tr(psum[0:64, 4, P:2 * P], fin[:, 112:176])
            tr(psum[0:8, 4, 2 * P:3 * P], fin[:, 72:80])
            tr(psum[0:8, 4, 3 * P:4 * P], fin[:, 64:72]).then_inc(fullA[4], 1)
            e.wait_ge(free[6], c(free[6]))
            for p in range(NP):
                ins = tr(psum[:, 6, p * P:(p + 1) * P], S[:, p, :])
            ins.then_inc(fullA[6], 1)

        @block.scalar
        def _(e):
            c = Counts(e, "act", passedA)

            def act(out, src, func=ACT.Copy, **k):
                return e.activation(out, src, func, **k)

            def split_w(i):
                e.wait_ge(raw_ready[i], c(raw_ready[i], 16))
                act(whi[i][:, :, :], wraw[i][:, :, :]).then_inc(hi_ready[i], 1)

            def split_x(k, n=TB, tile=None, dst=None):
                e.wait_ge(st_ready, c(st_ready))
                act((xhi if dst is None else dst)[:, k, 0:n], stage[:, k % 2, 0:n]).then_inc(sthi, 1)

            def square(k, src, j):
                e.wait_ge(sq_free, c(sq_free))
                if k is None:
                    e.sem_inc(passedA, 1)
                return act(stage[:, j, :], src, ACT.Square)

            def stats():
                e.wait_ge(fullA[4], c(fullA[4]))
                act(sm[:, 0:4], psum[:, 4, 0:4], ACT.Sqrt, scale=1.0 / D, bias=eps[:, 0:1]).then_inc(a2v, 1)

            def sample_stats():
                e.wait_ge(fullA[6], c(fullA[6]))
                act(sm[:, 72:80], psum[:, 6, 0:B], ACT.Sqrt, scale=1.0 / D, bias=eps[:, 0:1]).then_inc(a2v, 1)

            e.wait_ge(ld, c(ld, 16 * NLD))
            e.wait_ge(consts, c(consts))
            for t in range(2):
                act(stage[:, :, :].rearrange("p a b -> p (a b)"), xin[:, t, :], ACT.Square, accum_out=sm[:, t:t + 1]).then_inc(ach, 1)
                e.wait_ge(ach, c(ach))
            act(sm[:, 2:4], sm[:, 0:2], ACT.Sqrt, scale=1.0 / D, bias=eps[:, 0:1]).then_inc(a2v, 1)
            split_w(0)
            split_w(1)
            for k in range(KT):
                split_x(k, NMEM)
            with c.loop("mem", 8):
                for j in range(2):
                    e.wait_ge(slab_done[j], c(slab_done[j]))
                    split_w(j)

            def dec_chunk(cc):
                e.wait_ge(dec_freeV, c(dec_freeV))
                e.wait_ge(dec_freeG, c(dec_freeG))
                e.sem_inc(passedA, 1)
                act(dec[:, :, :], Lf[:, :, bass.ds(cc * (C + 1), C + 1)], ACT.Exp, scale=-DECAY).then_inc(dec_readyV, 1)
                act(inv[:, :, :], Lf[:, :, bass.ds(cc * (C + 1) + 1, C)], ACT.Exp, scale=DECAY).then_inc(dec_readyG, 1)

            def wkv_pair(t0, more):
                both = [(i, p, 4 * (1 - i) + p) for i in range(2) for p in range(NP)]
                for i, p, bk in both:
                    e.wait_ge(wk_mm[bk], c(wk_mm[bk], 2))
                    act(TM[i][:, p, :], psum[:, bk, :]).then_inc(wk_act[bk], 1)
                if more is not None:
                    dec_chunk(more)
                for l in range(1, len(MERGES)):
                    m = MERGES[l]
                    for i, p, bk in both:
                        e.wait_ge(wk_mm[bk], c(wk_mm[bk], 1 if l == 1 else 2))
                        act(half(Zs[i][:, p, :], m, 1), psum[:, bk, 0:64].rearrange("p (q w) -> p q w", w=m)
                            ).then_inc(wk_act[bk], 1)
                for i in range(2):
                    for p in range(NP):
                        bk = 4 * (1 - i) + p
                        e.wait_ge(wk_mm[bk], c(wk_mm[bk], 2))
                        act(Zs[i][:, p, :], psum[:, bk, 0:P]).then_inc(wk_act[bk], 1)
                    if i and more is not None:
                        dec_chunk(more + 1)
                    for p in range(NP):
                        bk = 4 * (1 - i) + p
                        e.wait_ge(wk_mm[bk], c(wk_mm[bk], 2))
                        e.sem_inc(passedA, 1)
                        act(Y[:, p, bass.ds(t0 + i * C, C)], psum[:, bk, 0:C]).then_inc(wk_act[bk], 1)

            def residual(label):
                with c.loop(label, KT // 2) as i:
                    for j in range(2):
                        e.wait_ge(slab_done[j], c(slab_done[j]))
                        split_w(j)
                        e.wait_ge(xT_new, c(xT_new))
                        square(None, xT[:, bass.ds(2 * i + j, 1), :].rearrange("p a t -> p (a t)"), j).then_inc(sq_ready, 1)
                c.skip(sq_free, 2)

            def attention():
                units = [(h, t) for h in range(NXH) for t in range(TT)]

                def exps(n):
                    e.wait_ge(v2a, c(v2a))
                    j = n % 3
                    act(pr[j], psum[:, SCORE[j], 0:NMEM], ACT.Exp, scale=XSCALE,
                        bias=sm[:, 80 + j:81 + j], accum_out=sm[:, 8 + j:9 + j]).then_inc(a2v, 1)

                exps(0)
                exps(1)
                for n, (h, t) in enumerate(units):
                    bk = 6 + n % 2
                    if t == 0 and h >= 2:
                        e.wait_ge(pT_free, c(pT_free))
                    e.wait_ge(fullA[bk], c(fullA[bk]))
                    act(pT[:, h % 2, :, t * P:(t + 1) * P], psum[:, bk, 0:2 * P].rearrange("p (m t) -> p m t", m=2)).then_inc(ach, 1)
                    e.wait_ge(ach, c(ach))
                    e.sem_inc(free[bk], 1)
                    if t == TT - 1:
                        e.sem_inc(a2p, 1)
                    if n + 2 < len(units):
                        exps(n + 2)
                    if n % 4 == 1 and n > 4:
                        split_x(2 * (h - 1))
                        split_x(2 * (h - 1) + 1)
                split_x(6)
                split_x(7)
                c.skip(pT_free, 2)

            def ffn_up(i):
                for a in range(4):
                    e.wait_ge(slab_done[a % 2], c(slab_done[a % 2]))
                    split_w(a % 2)
                    e.wait_ge(eb_free[a], c(eb_free[a]))
                    act(eb[:, a, 2:TB + 2], psum[:, a, :]).then_inc(ach, 1)
                    e.wait_ge(ach, c(ach))
                    e.sem_inc(eb_ready[a], 1)
                    e.sem_inc(free[a], 1)

            def ffn_silu(last):
                for a in (1, 3):
                    e.wait_ge(v2a, c(v2a))
                    act(fc[:, a, :], fc[:, a, :], ACT.Silu).then_inc(a2v, 1)
                if last:
                    e.wait_ge(v2a, c(v2a))
                    act(sw[:, 4:6, 0, :], sw[:, 2:4, 0, :], ACT.Silu).then_inc(a2v, 1)

            def ffn_hidden():
                for j in range(2):
                    split_x(j, dst=hhi)

            def one_block(b, last):
                for k in range(KT):
                    bk = 4 + k % 4
                    e.wait_ge(fullA[bk], c(fullA[bk]))
                    act(xT[:, k, :], psum[:, bk, :])
                    square(k, psum[:, bk, :], k % 2).then_inc(ach, 1)
                    e.wait_ge(ach, c(ach))
                    e.sem_inc(sq_ready, 1)
                    e.sem_inc(free[bk], 1)
                e.sem_inc(x_whole, 1)
                c.skip(sq_free, 2)
                stats()
                if last:
                    sample_stats()
                for k in range(KT):
                    split_x(k)
                with c.loop("shift", NRW // 2) as i:
                    for j in range(2):
                        m = 2 * i + j
                        e.wait_ge(slab_done[j], c(slab_done[j]))
                        e.wait_ge(shf_free[j], c(shf_free[j]))
                        e.sem_inc(passedA, 1)
                        act(shifted[:, j, 0:1], carry[:, bass.ds(m, 1)])
                        act(shifted[:, j, 1:TB + 1], psum[:, j, :], scale=pcol("mu_shift", m)).then_inc(ach, 1)
                        e.wait_ge(ach, c(ach))
                        e.sem_inc(passedA, 1)
                        act(carry[:, bass.ds(m, 1)], shifted[:, j, TB:TB + 1]).then_inc(shf[j], 1)
                        split_w(j)
                e.wait_ge(v2a, c(v2a))
                act(Z[0:64, 12, :], Z[0:64, 12, :], ACT.Tanh)
                act(Z[:, 13, :], Z[:, 13, :], ACT.Sigmoid).then_inc(a2p, 1)

                def gate_b(i):
                    for j in range(2):
                        e.wait_ge(slab_done[j], c(slab_done[j]))
                        act(gb[:, 2 * i + j, :], psum[:, j, :]).then_inc(free[j], 1)
                        split_w(j)

                gate_b(0)
                e.wait_ge(fullA[3], c(fullA[3]))
                act(sm[:, 8:40], psum[:, 3, 0:32], ACT.Sqrt).then_inc(a2v, 1)
                for p in range(NP):
                    e.wait_ge(fullA[4 + p], c(fullA[4 + p]))
                    act(kka[:, p, :], psum[:, 4 + p, :], ACT.Sigmoid, bias=pcol("a0", p)).then_inc(ach, 1)
                    e.wait_ge(ach, c(ach))
                    e.sem_inc(free[4 + p], 1)
                e.sem_inc(a2v, 1)
                gate_b(1)
                with c.loop("gate_c", 2) as i:
                    for j in range(2):
                        e.wait_ge(slab_done[j], c(slab_done[j]))
                        e.sem_inc(passedA, 1)
                        act(cb[:, bass.ds(2 * i + j, 1), 2:TB + 2].rearrange("p a t -> p (a t)"), psum[:, j, :]).then_inc(ach, 1)
                        e.wait_ge(ach, c(ach))
                        e.sem_inc(free[j], 1)
                        e.sem_inc(a2v, 1)
                        split_w(j)
                with c.loop("h_in", 2):
                    for j in range(2):
                        e.wait_ge(slab_done[j], c(slab_done[j]))
                        split_w(j)
                for p in range(NP):
                    e.wait_ge(fullA[4 + p], c(fullA[4 + p]))
                    act(L[:, p, :, 1:C + 1], psum[:, 4 + p, :].rearrange("p (c t) -> p c t", c=NC),
                        ACT.Sigmoid, bias=pcol("w0", p)).then_inc(ach, 1)
                    e.wait_ge(ach, c(ach))
                    e.sem_inc(free[4 + p], 1)
                e.sem_inc(a2v, 1)
                e.wait_ge(v2a, c(v2a))
                for j in range(4):
                    act(xhi[:, 4 + j, :], gb[:, j, :]).then_inc(sthi, 1)
                e.wait_ge(wkv_inA, c(wkv_inA))
                dec_chunk(0)
                dec_chunk(1)
                with c.loop("wkv", NC // 2 - 1) as i:
                    wkv_pair(i * (2 * C), 2 * i + 2)
                wkv_pair((NC - 2) * C, None)
                for p in range(NP):
                    e.wait_ge(v2a, c(v2a))
                    act(kkn[:, p, :], Y[:, p, :], ACT.Square).then_inc(a2p, 1)
                e.wait_ge(fullA[4], c(fullA[4]))
                act(sm[:, 8:40], psum[:, 4, 0:32], ACT.Sqrt, scale=1.0 / N, bias=eps[:, 1:2]).then_inc(a2v, 1)
                for k in range(4):
                    split_x(k)
                if last:
                    sample_wkv()
                residual("out")
                stats()
                if last:
                    sample_stats()
                for k in range(KT):
                    split_x(k)
                with c.loop("q", KT // 2) as i:
                    for j in range(2):
                        e.wait_ge(slab_done[j], c(slab_done[j]))
                        e.sem_inc(passedA, 1)
                        act(q_sb[:, bass.ds(2 * i + j, 1), :].rearrange("p a t -> p (a t)"), psum[:, j, :]).then_inc(ach, 1)
                        e.wait_ge(ach, c(ach))
                        e.sem_inc(free[j], 1)
                        split_w(j)
                e.sem_inc(a2p, 1)
                attention()
                if last:
                    sample_attention()
                residual("o")
                stats()
                if last:
                    sample_stats()
                for k in range(KT):
                    split_x(k)
                ffn_up(0)
                ffn_silu(last)
                ffn_hidden()
                with c.loop("ffn" + "s" * last, NF // 2 - 1) as i:
                    ffn_up(i + 1)
                    ffn_silu(last)
                    for j in range(2):
                        e.wait_ge(slab_done[j], c(slab_done[j]))
                        split_w(j)
                    ffn_hidden()
                for k in range(KT):
                    e.wait_ge(xT_new, c(xT_new))
                    square(k, xT[:, k, :], k % 2).then_inc(sq_ready, 1)
                    if k % 4 == 3:
                        e.wait_ge(slab_done[k // 4], c(slab_done[k // 4]))
                        if not last:
                            split_w(k // 4)
                c.skip(sq_free, 2)
                stats()
                for t in range(TT):
                    if t >= 2:
                        e.wait_ge(y_st[t % 2], c(y_st[t % 2], 16))
                    e.wait_ge(fullA[6], c(fullA[6]))
                    act(yrow[:, t % 2, 0:TB], psum[:, 6, :]).then_inc(ach, 1)
                    e.wait_ge(ach, c(ach))
                    e.sem_inc(free[6], 1)
                    e.sem_inc(y_go[t % 2], 1)
                for j in range(2):
                    c.skip(y_st[j], 16)
                if last:
                    sample_stats()

            def sample_wkv():
                e.wait_ge(v2a, c(v2a))
                act(sz[0:64, 12, :], sz[0:64, 12, :], ACT.Tanh)
                act(sz[:, 13, :], sz[:, 13, :], ACT.Sigmoid).then_inc(a2p, 1)
                e.wait_ge(fullA[6], c(fullA[6]))
                e.wait_ge(fullA[7], c(fullA[7]))
                for p in range(NP):
                    act(sw[:, 0, p, :], psum[:, 6, 8 * p:8 * p + 8], ACT.Sigmoid, bias=pcol("w0", p))
                    act(sw[:, 1, p, :], psum[:, 7, 8 * p:8 * p + 8], ACT.Sigmoid, bias=pcol("a0", p))
                act(sw[:, 2, :, :], psum[:, 6, 64:96].rearrange("p (a b) -> p a b", a=4)).then_inc(ach, 1)
                e.wait_ge(ach, c(ach))
                act(sw[:, 0, :, :], sw[:, 0, :, :], ACT.Exp, scale=-DECAY).then_inc(a2v, 1)
                e.wait_ge(fullA[7], c(fullA[7]))
                act(sw[:, 3, :, :], psum[:, 7, 0:32].rearrange("p (a b) -> p a b", a=4), ACT.Sqrt).then_inc(a2v, 1)
                e.wait_ge(fullA[7], c(fullA[7]))
                act(sw[:, 3, :, :], psum[:, 7, 0:32].rearrange("p (a b) -> p a b", a=4), ACT.Sqrt, scale=1.0 / N,
                    bias=eps[:, 1:2]).then_inc(a2v, 1)

            def sample_attention():
                e.wait_ge(v2a, c(v2a))
                act(sprob[0:32, :], sprob[0:32, :], ACT.Exp, scale=XSCALE, bias=sm[0:32, 89:90],
                    accum_out=sm[0:32, 90:91]).then_inc(a2v, 1)

            with c.loop("block", NB - 1) as b:
                one_block(b, False)
            one_block(NB - 1, True)
            e.wait_ge(y_st[0], c(y_st[0], 0))
            e.wait_ge(y_st[1], c(y_st[1], 0))
            for g in range(2):
                e.wait_ge(fullA[g], c(fullA[g]))
                act(zr[0:2 * NF, 4 * g * P:4 * (g + 1) * P], psum[0:2 * NF, g, :])
                e.wait_ge(fullA[2 + g], c(fullA[2 + g]))
                act(zr[0:4, (8 + 4 * g) * P:(12 + 4 * g) * P], psum[0:4, 2 + g, :])
            e.wait_ge(fullA[5], c(fullA[5]))
            act(zr[0:2 * NF, 16 * P:18 * P], psum[0:2 * NF, 5, 0:2 * P])
            e.wait_ge(fullA[4], c(fullA[4]))
            act(zr[0:64, 18 * P:20 * P], psum[0:64, 4, 0:2 * P])
            act(zr[0:8, 20 * P:22 * P], psum[0:8, 4, 2 * P:4 * P])
            e.wait_ge(fullA[6], c(fullA[6]))
            act(zr[:, 22 * P:26 * P], psum[:, 6, :]).then_inc(out_go, 1)

        @block.vector
        def _(e):
            c = Counts(e, "dve", passedV)

            def tt(out, a, b, op=ALU.mult):
                return e.tensor_tensor(out, a, b, op)

            def stt(out, a, s, b, op0=ALU.mult, op1=ALU.mult):
                return e.scalar_tensor_tensor(out, a, s, b, op0, op1)

            def lo(k, n=TB, hi=None, lo_=None, ready=None):
                e.wait_ge(sthi, c(sthi))
                h, l = (xhi, xlo) if hi is None else (hi, lo_)
                tt(l[:, k, 0:n], stage[:, k % 2, 0:n], h[:, k, 0:n].bitcast(F32), ALU.subtract).then_inc(x_ready if ready is None else ready, 1)
                e.wait_ge(x_ready if ready is None else ready, c(x_ready if ready is None else ready))

            def split_tiles(order, produce, n=TB):
                before = None
                for k in order:
                    produce(k, stage[:, k % 2, 0:n]).then_inc(st_ready, 1)
                    e.wait_ge(st_ready, c(st_ready))
                    if before is not None:
                        lo(before, n)
                    before = k
                lo(before, n)

            def acc_start():
                e.memset(acc, 0.0).then_inc(vch, 1)
                e.wait_ge(vch, c(vch))
                e.sem_inc(sq_free, 2)

            def acc_add(j):
                e.wait_ge(sq_ready, c(sq_ready))
                tt(acc, acc, stage[:, j, :], ALU.add).then_inc(vch, 1)
                e.wait_ge(vch, c(vch))
                e.sem_inc(sq_free, 1)

            def stats(name, sample):
                e.sem_inc(v2p, 1)
                e.wait_ge(a2v, c(a2v))
                e.sem_inc(free[4], 1)
                e.reciprocal(sm[:, 4:8], sm[:, 0:4]).then_inc(v2p, 1)
                e.wait_ge(v2p, c(v2p))
                if sample:
                    sample_norm(name)

            def normalise(name, last=False):
                e.wait_ge(fullV[5], c(fullV[5]))

                def tile(k, out):
                    return stt(out, xT[:, k, :], pcol(name, k), psum[:, 5, :])

                split_tiles(range(KT), tile)
                e.sem_inc(free[5], 1)

            def bc8(ap):
                return ap.unsqueeze(2).broadcast_to([P, ap.shape[1], B])

            def sample_norm(name, split=True):
                tt(sw[:, 4:12, 0, :], xs[:, :, :], xs[:, :, :]).then_inc(vch, 1)
                e.wait_ge(vch, c(vch))
                e.tensor_reduce(sw[:, 10, 1, :], sw[:, 4:12, 0, :].rearrange("p k b -> p b k"), AX.X, ALU.add).then_inc(vch, 1)
                e.wait_ge(vch, c(vch))
                e.tensor_copy(sw[:, 11, 0, :], sw[:, 10, 1, :]).then_inc(v2p, 1)
                e.wait_ge(v2p, c(v2p))
                e.wait_ge(a2v, c(a2v))
                e.sem_inc(free[6], 1)
                e.reciprocal(sm[:, 72:80], sm[:, 72:80]).then_inc(vch, 1)
                e.wait_ge(vch, c(vch))
                tt(xsn[:, :, 0:B], xs[:, :, :], bc8(pcol(name, 0, KT))).then_inc(vch, 1)
                e.wait_ge(vch, c(vch))
                tt(xsn[:, :, 0:B], xsn[:, :, 0:B], sm[:, 72:80].unsqueeze(1).broadcast_to([P, KT, B])).then_inc(vch, 1)
                e.wait_ge(vch, c(vch))
                if name == "norm_mix":
                    e.tensor_copy(shn[:, :, 0:B], xsn[:, :, 0:B]).then_inc(vch, 1)
                    e.wait_ge(vch, c(vch))
                if split:
                    sample_split()

            def sample_split():
                e.tensor_copy(xs2[:, :, 0, :], xsn[:, :, :]).then_inc(vch, 1)
                e.wait_ge(vch, c(vch))
                tt(xs2[:, :, 1, :], xsn[:, :, :], xs2[:, :, 0, :].bitcast(F32), ALU.subtract).then_inc(vch, 1)
                e.wait_ge(vch, c(vch))
                e.sem_inc(v2p, 1)

            e.wait_ge(consts, c(consts))
            e.wait_ge(fullV[4], c(fullV[4]))
            e.tensor_copy(par[:, :], psum[:, 4, 0:NPAR]).then_inc(vch, 1)
            e.wait_ge(vch, c(vch))
            e.sem_inc(free[4], 1)
            e.tensor_scalar(omu[:, :], pcol("mu_shift", 0, NRW), -1.0, 1.0, ALU.mult, ALU.add).then_inc(vch, 1)
            e.wait_ge(vch, c(vch))
            e.tensor_scalar(oka[:, :], pcol("k_a", 0, 4), -1.0, 1.0, ALU.mult, ALU.add).then_inc(vch, 1)
            e.wait_ge(vch, c(vch))
            e.wait_ge(fullV[5], c(fullV[5]))
            e.tensor_copy(fcw[:, :], psum[:, 5, 0:132]).then_inc(free[5], 1)
            e.wait_ge(fullV[6], c(fullV[6]))
            v = psum[:, 6, 0:128].rearrange("p (k b) -> p k b", k=KT)
            e.tensor_copy(xs[:, :, :], v[:, :, 0:B])
            e.tensor_copy(xsn[:, :, B:2 * B], v[:, :, B:2 * B])
            e.tensor_copy(sconv[:, :, :], psum[:, 6, 128:192].rearrange("p (k b) -> p k b", k=4)).then_inc(vch, 1)
            e.wait_ge(vch, c(vch))
            e.sem_inc(free[6], 1)
            for g in range(2):
                e.wait_ge(fullV[7], c(fullV[7]))
                e.tensor_copy(sffn[:, 22 * g:22 * g + 22, :], psum[:, 7, 0:352].rearrange("p (k b) -> p k b", k=22)).then_inc(vch, 1)
                e.wait_ge(vch, c(vch))
                e.sem_inc(free[7], 1)
            e.wait_ge(a2v, c(a2v))
            e.reciprocal(sm[:, 4:6], sm[:, 2:4]).then_inc(vch, 1)
            e.wait_ge(vch, c(vch))
            for t in range(2):
                e.tensor_scalar(xin[:, t, :], xin[:, t, :], sm[:, 4 + t:5 + t], None, ALU.mult).then_inc(vch, 1)
                e.wait_ge(vch, c(vch))
            e.sem_inc(v2p, 1)
            before = None
            for k in range(KT):
                bk = 4 + k % 4
                e.wait_ge(fullV[bk], c(fullV[bk]))
                e.tensor_scalar(stage[:, k % 2, 0:NMEM], psum[:, bk, 0:NMEM], pcol("norm_mem", k), None, ALU.mult).then_inc(vch, 1)
                e.wait_ge(vch, c(vch))
                e.sem_inc(free[bk], 1)
                e.sem_inc(st_ready, 1)
                if before is not None:
                    lo(before, NMEM)
                before = k
            lo(before, NMEM)
            with c.loop("mem", 8) as i:
                for j in range(2):
                    e.wait_ge(slab_done[j], c(slab_done[j]))
                    e.tensor_copy(zr[:, bass.ds((2 * i + j + 8) * NMEM, NMEM)], psum[:, j, 0:NMEM]).then_inc(vch, 1)
                    e.wait_ge(vch, c(vch))
                    e.sem_inc(free[j], 1)
            for kv in range(2):
                e.sem_inc(v2p, 1)
                for t in range(2):
                    for g in range(2):
                        bk = 4 + 2 * t + g
                        a = kv * 2048 + t * D + g * TB
                        e.wait_ge(fullV[bk], c(fullV[bk]))
                        e.tensor_copy(kv_flat[:, a:a + TB], psum[:, bk, :]).then_inc(vch, 1)
                        e.wait_ge(vch, c(vch))
                        e.sem_inc(free[bk], 1)
                e.sem_inc(out_go, 1)
            e.sem_inc(xin_free, 1)
            e.wait_ge(out_st, c(out_st, 48))

            def operands(i, t0):
                e.wait_ge(dec_readyV, c(dec_readyV))
                tt(ops_ar[i][:, :, P:192], Z[:, 0:4, bass.ds(t0, C)], dec[:, :, 1:C + 1])
                for h in range(2):
                    a = slice(64 * h, 64 * h + 64)
                    stt(ops_ar[i][a, :, a], kkn[a, :, bass.ds(t0, C)], -1.0, dec[a, :, 0:C])
                e.tensor_copy(gC[i][:, :], dec[:, :, C]).then_inc(vch, 1)
                e.wait_ge(vch, c(vch))
                e.sem_inc(vec_ops[i], 1)
                e.sem_inc(dec_freeV, 1)

            def wkv_pair(t_next):
                both = [(i, p, 4 * (1 - i) + p) for i in range(2) for p in range(NP)]

                def merge(i, p, l, side, data):
                    m = MERGES[l]
                    return e.copy_predicated(half(QT[i][:, p, side, :], m, 1 - side),
                                             merge_mask[:, l, side, :].rearrange("p (q w) -> p q w", w=m), data)

                for i, p, bk in both:
                    e.wait_ge(wk_mm[bk], c(wk_mm[bk]))
                    tt(GM[i][:, p, :, :], psum[:, bk, 0:384].rearrange("p (a c) -> p a c", a=2),
                           gram_mask[:, :].unsqueeze(1).broadcast_to([P, 2, 192])).then_inc(vch, 1)
                    e.wait_ge(vch, c(vch))
                    e.sem_inc(wk_vec[bk], 1)
                for i, p, bk in both:
                    if p == 0:
                        e.wait_ge(pool_qt, c(pool_qt))
                        e.sem_inc(passedV, 1)
                    merge(i, p, 0, 0, half(GM[i][:, p, 0, 0:P], 1, 1))
                    e.wait_ge(wk_act[bk], c(wk_act[bk]))
                    e.sem_inc(passedV, 1)
                    merge(i, p, 0, 1, half(TM[i][:, p, 384:512], 1, 0)).then_inc(wk_vec[bk], 1)
                    c.skip(wk_mm[bk], 1)
                for l in range(1, len(MERGES)):
                    for i, p, bk in both:
                        e.wait_ge(wk_mm[bk], c(wk_mm[bk], 2))
                        e.sem_inc(passedV, 1)
                        if l == 1 and p == NP - 1:
                            e.sem_inc(ops_freeG, 1)
                        new = psum[:, bk, 0:P].rearrange("p (a q w) -> p a q w", a=2, w=MERGES[l])
                        ins = merge(i, p, l, 0, new[:, 0])
                        if l < len(MERGES) - 1:
                            ins = merge(i, p, l, 1, new[:, 1])
                        ins.then_inc(wk_vec[bk], 1)
                for i in range(2):
                    for p in range(NP):
                        bk = 4 * (1 - i) + p
                        e.wait_ge(wk_mm[bk], c(wk_mm[bk], 2))
                        e.tensor_copy(Us[i][:, p, :], psum[:, bk, 0:P]).then_inc(wk_vec[bk], 1)
                        e.wait_ge(wk_vec[bk], c(wk_vec[bk]))
                    e.sem_inc(qt_free, 1)
                    for p in range(NP):
                        bk = 4 * (1 - i) + p
                        e.wait_ge(wk_mm[bk], c(wk_mm[bk]))
                        e.wait_ge(wk_act[bk], c(wk_act[bk], 7))
                        tt(S[:, p, :], S[:, p, :], psum[:, bk, P:2 * P], ALU.add).then_inc(vch, 1)
                        e.wait_ge(vch, c(vch))
                        e.tensor_scalar(S[:, p, :], S[:, p, :], gC[i][:, p:p + 1], None, ALU.mult).then_inc(vch, 1)
                        e.wait_ge(vch, c(vch))
                        e.sem_inc(wk_vec[bk], 1)
                    if t_next is not None:
                        operands(i, t_next + i * C)

            def residual(label, last):
                acc_start()
                with c.loop(label + "s" * last, KT // 2) as i:
                    for j in range(2):
                        k = 2 * i + j
                        e.wait_ge(slab_done[j], c(slab_done[j]))
                        x = xT[:, bass.ds(k, 1), :].rearrange("p a t -> p (a t)")
                        tt(x, x, psum[:, j, :], ALU.add).then_inc(vch, 1)
                        e.wait_ge(vch, c(vch))
                        e.sem_inc(free[j], 1)
                        e.sem_inc(xT_new, 1)
                        if last:
                            y = xs[:, bass.ds(k, 1), :].rearrange("p a t -> p (a t)")
                            tt(y, y, psum[:, 4 + j, 0:B], ALU.add).then_inc(vch, 1)
                            e.wait_ge(vch, c(vch))
                            tt(y, y, psum[:, 4 + j, 2 * B:3 * B], ALU.add).then_inc(vch, 1)
                            e.wait_ge(vch, c(vch))
                            e.sem_inc(free[4 + j], 1)
                        acc_add(j)

            def attention(last):
                units = [(h, t) for h in range(NXH) for t in range(TT)]

                def maximum(n):
                    j = n % 3
                    e.wait_ge(fullV[SCORE[j]], c(fullV[SCORE[j]]))
                    e.reduce_max(sm[:, 84 + j:85 + j], psum[:, SCORE[j], 0:NMEM], AX.X).then_inc(vch, 1)
                    e.wait_ge(vch, c(vch))
                    e.tensor_scalar(sm[:, 80 + j:81 + j], sm[:, 84 + j:85 + j], -XSCALE, None,
                                    ALU.mult).then_inc(v2a, 1)

                def query(s):
                    b, g = s // 2, s % 2
                    tt(shifted[:, g, 0:TB].rearrange("p (k x) -> p k x", k=4),
                           sq_s[:, 4 * g:4 * g + 4, b:b + 1].broadcast_to([P, 4, P]),
                           ident[:, :].unsqueeze(1).broadcast_to([P, 4, P])).then_inc(vch, 1)
                    e.wait_ge(vch, c(vch))
                    e.sem_inc(v2p, 1)

                def sample_scores(s):
                    b, g = s // 2, s % 2
                    i = CACHE_OF[b]
                    prod = ops_b0[:, :, :].rearrange("p q c -> p (q c)")
                    e.wait_ge(fullV[0], c(fullV[0]))
                    if g == 0:
                        e.wait_ge(cache_in[i], c(cache_in[i], 16))
                    for m in range(2):
                        for h in range(2):
                            a, o = m * D + (2 * g + h) * 256, b * NXH + 2 * g + h
                            e.tensor_tensor_reduce(prod[:, 0:256], cache_buf[i][:, a:a + 256],
                                                   psum[:, 0, h * 256:h * 256 + 256], 1.0, 0.0,
                                                   ALU.mult, ALU.add, sscore[:, m, o:o + 1]).then_inc(vch, 1)
                            e.wait_ge(vch, c(vch))
                    e.sem_inc(free[0], 1)
                    if g:
                        e.sem_inc(cache_free[i], 1)

                def head_out(h):
                    for d in range(2):
                        k = 2 * h + d
                        e.wait_ge(fullV[2 + d], c(fullV[2 + d]))
                        e.tensor_copy(stage[:, d, :], psum[:, 2 + d, :]).then_inc(vch, 1)
                        e.wait_ge(vch, c(vch))
                        e.sem_inc(free[2 + d], 1)
                        e.sem_inc(st_ready, 1)
                    e.sem_inc(pT_free, 1)
                    lo(2 * h)
                    lo(2 * h + 1)

                maximum(0)
                maximum(1)
                for n, (h, t) in enumerate(units):
                    j = n % 3
                    e.wait_ge(a2v, c(a2v))
                    e.sem_inc(free[SCORE[j]], 1)
                    e.reciprocal(sm[:, 12 + j:13 + j], sm[:, 8 + j:9 + j]).then_inc(vch, 1)
                    e.wait_ge(vch, c(vch))
                    e.tensor_scalar(pr[j], pr[j], sm[:, 12 + j:13 + j], None, ALU.mult).then_inc(v2p, 1)
                    if n + 2 < len(units):
                        maximum(n + 2)
                    if last and n > 1:
                        sample_scores(n - 2)
                    if last and n:
                        query(n - 1)
                    if n % 4 == 1 and n > 4:
                        head_out(h - 1)
                head_out(NXH - 1)
                if last:
                    sample_scores(2 * B - 2)
                    query(2 * B - 1)
                    sample_scores(2 * B - 1)

            def ffn_conv(i, last):
                for a, tile in ((0, 2 * i), (1, 2 * i + NF), (2, 2 * i + 1), (3, 2 * i + NF + 1)):
                    w = [fcw[:, bass.ds(tile + t * 2 * NF, 1)] for t in range(3)]
                    e.wait_ge(eb_carry[a], c(eb_carry[a]))
                    e.tensor_scalar(fc[:, a, :], eb[:, a, 0:TB], w[0], None, ALU.mult).then_inc(vch, 1)
                    e.wait_ge(vch, c(vch))
                    stt(fc[:, a, :], eb[:, a, 1:TB + 1], w[1], fc[:, a, :], ALU.mult, ALU.add).then_inc(vch, 1)
                    e.wait_ge(vch, c(vch))
                    stt(fc[:, a, :], eb[:, a, 2:TB + 2], w[2], fc[:, a, :], ALU.mult, ALU.add).then_inc(vch, 1)
                    e.wait_ge(vch, c(vch))
                    e.sem_inc(eb_free[a], 1)
                    if a % 2:
                        e.sem_inc(v2a, 1)
                    e.wait_ge(slab_done[a % 2], c(slab_done[a % 2]))
                    if last:
                        u = sup[:, bass.ds(tile, 1), :].rearrange("p a b -> p (a b)")
                        e.tensor_copy(u, psum[:, 4 + a % 2, 0:B]).then_inc(vch, 1)
                        e.wait_ge(vch, c(vch))
                        tt(u, u, psum[:, 4 + a % 2, 2 * B:3 * B], ALU.add).then_inc(vch, 1)
                        e.wait_ge(vch, c(vch))
                        e.sem_inc(free[4 + a % 2], 1)
                        o = sw[:, (0, 2, 1, 3)[a], 0, :]
                        st = sffn[:, bass.ds(tile, 1), :].rearrange("p a (b r) -> p (a b) r", r=2)
                        e.tensor_scalar(o, st[:, :, 0], w[0], None, ALU.mult).then_inc(vch, 1)
                        e.wait_ge(vch, c(vch))
                        stt(o, st[:, :, 1], w[1], o, ALU.mult, ALU.add).then_inc(vch, 1)
                        e.wait_ge(vch, c(vch))
                        stt(o, u, w[2], o, ALU.mult, ALU.add).then_inc(vch, 1)
                        e.wait_ge(vch, c(vch))
                if last:
                    e.sem_inc(v2a, 1)

            def ffn_hidden(last):
                for j in range(2):
                    e.wait_ge(a2v, c(a2v))
                    tt(stage[:, j, :], fc[:, 2 * j, :], fc[:, 2 * j + 1, :]).then_inc(st_ready, 1)
                    e.wait_ge(st_ready, c(st_ready))
                for j in range(2):
                    lo(j, hi=hhi, lo_=hlo, ready=h_ready)
                if last:
                    e.wait_ge(a2v, c(a2v))
                    tt(sw[:, 6:8, 0, :], sw[:, 0:2, 0, :], sw[:, 4:6, 0, :]).then_inc(vch, 1)
                    e.wait_ge(vch, c(vch))
                    e.tensor_copy(sh2[:, :, 0, :], sw[:, 6:8, 0, :]).then_inc(vch, 1)
                    e.wait_ge(vch, c(vch))
                    tt(sh2[:, :, 1, :], sw[:, 6:8, 0, :], sh2[:, :, 0, :].bitcast(F32), ALU.subtract).then_inc(vch, 1)
                    e.wait_ge(vch, c(vch))
                    e.sem_inc(v2p, 1)

            def ffn_add(last, final=False):
                for k in range(KT):
                    bk = down_bank(k, last)
                    if k % 4 < 3:
                        e.wait_ge(fullV[bk], c(fullV[bk]))
                    else:
                        e.wait_ge(slab_done[k // 4], c(slab_done[k // 4]))
                    tt(xT[:, k, :], xT[:, k, :], psum[:, bk, :], ALU.add).then_inc(vch, 1)
                    e.wait_ge(vch, c(vch))
                    e.sem_inc(free[bk], 1)
                    if final:
                        e.sem_inc(xT_new, 1)
                        if k:
                            acc_add((k - 1) % 2)
                if final:
                    acc_add((KT - 1) % 2)
                if last:
                    new = psum[:, 6, 0:KT * 2 * B].rearrange("p (k a b) -> p k a b", k=KT, a=2)
                    tt(xs[:, :, :], xs[:, :, :], new[:, :, 0, :], ALU.add).then_inc(vch, 1)
                    e.wait_ge(vch, c(vch))
                    tt(xs[:, :, :], xs[:, :, :], new[:, :, 1, :], ALU.add).then_inc(vch, 1)
                    e.wait_ge(vch, c(vch))
                    e.sem_inc(free[6], 1)

            def one_block(b, last):
                acc_start()
                for k in range(KT):
                    acc_add(k % 2)
                stats("norm_mix", last)
                normalise("norm_mix")
                if last:
                    tt(shn[:, :, B], xhi[:, :, TB - 1].bitcast(F32), xlo[:, :, TB - 1].bitcast(F32), ALU.add).then_inc(vch, 1)
                    e.wait_ge(vch, c(vch))
                e.tensor_copy(cb[:, :, 0:2], ccarry[:, :, :]).then_inc(vch, 1)
                e.wait_ge(vch, c(vch))

                def sample_out(m, j):
                    if last:
                        o = sp[:, bass.ds(m, 1), :].rearrange("p a b -> p (a b)")
                        e.tensor_copy(o, psum[:, 4 + j, 0:2 * B]).then_inc(vch, 1)
                        e.wait_ge(vch, c(vch))
                        tt(o, o, psum[:, 4 + j, 2 * B:4 * B], ALU.add).then_inc(vch, 1)
                        e.wait_ge(vch, c(vch))
                        e.sem_inc(free[4 + j], 1)

                with c.loop("shift" + "s" * last, NRW // 2) as i:
                    for j in range(2):
                        m = 2 * i + j
                        e.wait_ge(shf[j], c(shf[j]))
                        e.wait_ge(slab_done[j], c(slab_done[j]))
                        stt(Z[:, bass.ds(m, 1), :].rearrange("p a t -> p (a t)"), psum[:, j, :],
                            omu[:, bass.ds(m, 1)], shifted[:, j, 0:TB], ALU.mult, ALU.add).then_inc(vch, 1)
                        e.wait_ge(vch, c(vch))
                        e.sem_inc(free[j], 1)
                        e.sem_inc(shf_free[j], 1)
                        sample_out(m, j)
                e.memset(L[:, :, :, 0], 0.0).then_inc(vch, 1)
                e.wait_ge(vch, c(vch))
                e.sem_inc(v2a, 1)
                for p in range(NP):
                    e.tensor_scalar(kkn[:, p, :], Z[:, 4 + p, :], pcol("k_k", p), None, ALU.mult).then_inc(vch, 1)
                    e.wait_ge(vch, c(vch))
                    sq = stage[:, p, :] if p < 2 else shifted[:, p - 2, 0:TB]
                    tt(sq, kkn[:, p, :], kkn[:, p, :]).then_inc(vch, 1)
                    e.wait_ge(vch, c(vch))
                e.sem_inc(v2p, 1)
                for j in range(2):
                    e.wait_ge(slab_done[j], c(slab_done[j]))
                    sample_out(NRW + j, j)
                e.wait_ge(a2v, c(a2v))
                e.sem_inc(free[3], 1)
                e.tensor_scalar(sm[:, 8:40], sm[:, 8:40], 1e-12, None, ALU.max).then_inc(vch, 1)
                e.wait_ge(vch, c(vch))
                e.reciprocal(sm[:, 40:72], sm[:, 8:40]).then_inc(vch, 1)
                e.wait_ge(vch, c(vch))
                e.sem_inc(v2p, 1)
                for j in range(2):
                    e.wait_ge(slab_done[j], c(slab_done[j]))
                    sample_out(NRW + 2 + j, j)
                e.wait_ge(a2v, c(a2v))
                for p in range(NP):
                    t = shifted[:, p % 2, 0:TB]
                    e.wait_ge(fullV[4 + p], c(fullV[4 + p]))
                    tt(kkn[:, p, :], kkn[:, p, :], psum[:, 4 + p, :]).then_inc(vch, 1)
                    e.wait_ge(vch, c(vch))
                    e.sem_inc(free[4 + p], 1)
                    e.tensor_scalar(t, kka[:, p, :], pcol("k_a", p), oka[:, p:p + 1], ALU.mult, ALU.add).then_inc(vch, 1)
                    e.wait_ge(vch, c(vch))
                    tt(Z[:, 4 + p, :], Z[:, 4 + p, :], t).then_inc(vch, 1)
                    e.wait_ge(vch, c(vch))
                    tt(kka[:, p, :], kka[:, p, :], kkn[:, p, :]).then_inc(vch, 1)
                    e.wait_ge(vch, c(vch))
                with c.loop("gate_c" + "s" * last, 2) as i:
                    for j in range(2):
                        e.wait_ge(slab_done[j], c(slab_done[j]))
                        sample_out(2 * i + j + 18, j)
                e.wait_ge(a2v, c(a2v, 4))
                with c.loop("h_in" + "s" * last, 2) as i:
                    for j in range(2):
                        n = 2 * i + j
                        e.wait_ge(slab_done[j], c(slab_done[j]))
                        v = cb[:, bass.ds(n, 1), :].rearrange("p a t -> p (a t)")
                        tt(v[:, 2:TB + 2], v[:, 2:TB + 2], psum[:, j, :]).then_inc(vch, 1)
                        e.wait_ge(vch, c(vch))
                        e.sem_inc(free[j], 1)
                        sample_out(n + 22, j)
                        t, g = shifted[:, j, 0:TB], gb[:, bass.ds(n, 1), :].rearrange("p a t -> p (a t)")
                        e.tensor_scalar(t, v[:, 0:TB], pcol("conv_w", n), None, ALU.mult).then_inc(vch, 1)
                        e.wait_ge(vch, c(vch))
                        stt(t, v[:, 1:TB + 1], pcol("conv_w", n + 4), t, ALU.mult, ALU.add).then_inc(vch, 1)
                        e.wait_ge(vch, c(vch))
                        stt(t, v[:, 2:TB + 2], pcol("conv_w", n + 8), t, ALU.mult, ALU.add).then_inc(vch, 1)
                        e.wait_ge(vch, c(vch))
                        tt(g, g, t).then_inc(vch, 1)
                        e.wait_ge(vch, c(vch))
                e.sem_inc(v2a, 1)
                e.tensor_copy(ccarry[:, :, :], cb[:, :, TB:TB + 2]).then_inc(vch, 1)
                e.wait_ge(vch, c(vch))
                e.wait_ge(a2v, c(a2v))
                for p in range(NP):
                    ins = e.tensor_tensor_scan(Lf[:, p, :], scan_mask[:, :], Lf[:, p, :], 0.0, ALU.mult, ALU.add)
                ins.then_inc(vch, 1)
                e.wait_ge(vch, c(vch))
                e.sem_inc(wkv_inA, 1)
                e.sem_inc(wkv_inG, 1)
                for j in range(4):
                    e.wait_ge(sthi, c(sthi))
                    tt(xlo[:, 4 + j, :], gb[:, j, :], xhi[:, 4 + j, :].bitcast(F32), ALU.subtract).then_inc(x_ready, 1)
                    e.wait_ge(x_ready, c(x_ready))
                e.wait_ge(x_out, c(x_out, 16))
                operands(0, 0)
                operands(1, C)
                with c.loop("wkv", NC // 2 - 1) as i:
                    wkv_pair(i * (2 * C) + 2 * C)
                wkv_pair(None)
                e.sem_inc(ws_free, 1)
                for p in range(NP + 1):
                    if p < NP:
                        t = shifted[:, p % 2, 0:TB]
                        stt(t, Z[:, p, :], pcol("r_k", p), Z[:, 4 + p, :]).then_inc(v2p, 1)
                        e.wait_ge(v2p, c(v2p))
                    if p:
                        q = p - 1
                        e.wait_ge(fullV[4 + q], c(fullV[4 + q]))
                        tt(Z[:, q, :], Z[:, 8 + q, :], psum[:, 4 + q, :]).then_inc(vch, 1)
                        e.wait_ge(vch, c(vch))
                        e.sem_inc(free[4 + q], 1)
                for p in range(NP):
                    e.wait_ge(fullV[4 + p], c(fullV[4 + p]))
                    stt(Y[:, p, :], psum[:, 4 + p, :], -1.0 / N, Y[:, p, :], ALU.mult, ALU.add).then_inc(vch, 1)
                    e.wait_ge(vch, c(vch))
                    e.sem_inc(free[4 + p], 1)
                    e.sem_inc(v2a, 1)
                e.wait_ge(a2v, c(a2v))
                e.sem_inc(free[4], 1)
                e.reciprocal(sm[:, 40:72], sm[:, 8:40]).then_inc(vch, 1)
                e.wait_ge(vch, c(vch))
                e.sem_inc(v2p, 1)
                for p in range(NP):
                    e.wait_ge(fullV[4 + p], c(fullV[4 + p]))
                    tt(Y[:, p, :], Y[:, p, :], psum[:, 4 + p, :]).then_inc(vch, 1)
                    e.wait_ge(vch, c(vch))
                    e.sem_inc(free[4 + p], 1)
                    e.tensor_scalar(Y[:, p, :], Y[:, p, :], pcol("ln_x_w", p), pcol("ln_x_b", p), ALU.mult, ALU.add).then_inc(vch, 1)
                    e.wait_ge(vch, c(vch))
                    tt(Y[:, p, :], Y[:, p, :], Z[:, p, :], ALU.add).then_inc(vch, 1)
                    e.wait_ge(vch, c(vch))

                def gated(k, out):
                    e.wait_ge(fullV[4 + k], c(fullV[4 + k]))
                    tt(out, Y[:, k, :], psum[:, 4 + k, :]).then_inc(vch, 1)
                    e.wait_ge(vch, c(vch))
                    return e.sem_inc(free[4 + k], 1)

                before = None
                for k in range(NP):
                    gated(k, stage[:, k % 2, :])
                    e.sem_inc(st_ready, 1)
                    if before is not None:
                        lo(before)
                    before = k
                lo(before)
                if last:
                    sample_wkv()
                    for j in range(3):
                        e.sem_inc(cache_free[j], 1)
                else:
                    e.sem_inc(xin_free, 1)
                e.wait_ge(x_back, c(x_back, 16))
                residual("out", last)
                stats("norm_x", last)
                normalise("norm_x")
                with c.loop("q" + "s" * last, KT // 2) as i:
                    for j in range(2):
                        e.wait_ge(slab_done[j], c(slab_done[j]))
                        if last:
                            o = sq_s[:, bass.ds(2 * i + j, 1), :].rearrange("p a b -> p (a b)")
                            e.tensor_copy(o, psum[:, 4 + j, 0:B]).then_inc(vch, 1)
                            e.wait_ge(vch, c(vch))
                            tt(o, o, psum[:, 4 + j, 2 * B:3 * B], ALU.add).then_inc(vch, 1)
                            e.wait_ge(vch, c(vch))
                            e.sem_inc(free[4 + j], 1)
                attention(last)
                if last:
                    sample_attention()
                residual("o", last)
                stats("norm_ffn", last)
                normalise("norm_ffn")
                ffn_conv(0, last)
                ffn_hidden(last)
                with c.loop("ffn" + "s" * last, NF // 2 - 1) as i:
                    ffn_conv(i + 1, last)
                    ffn_add(last)
                    ffn_hidden(last)
                acc_start()
                ffn_add(last, True)
                stats("norm_final", False)
                e.wait_ge(fullV[5], c(fullV[5]))
                for k in range(KT):
                    stt(xT[:, k, :], xT[:, k, :], pcol("norm_final", k), psum[:, 5, :]).then_inc(vch, 1)
                    e.wait_ge(vch, c(vch))
                    e.sem_inc(v2p, 1)
                e.sem_inc(free[5], 1)
                for t in range(TT):
                    if t >= 2:
                        e.wait_ge(y_st[t % 2], c(y_st[t % 2], 16))
                    e.wait_ge(fullV[7], c(fullV[7]))
                    e.tensor_copy(yrow[:, t % 2, TB:2 * TB], psum[:, 7, :]).then_inc(vch, 1)
                    e.wait_ge(vch, c(vch))
                    e.sem_inc(free[7], 1)
                    e.sem_inc(y_go[t % 2], 1)
                for j in range(2):
                    e.wait_ge(y_st[j], c(y_st[j], 16))
                if last:
                    sample_norm("norm_final", split=False)

            def sample_wkv():
                mu, om = bc8(pcol("mu_shift", 0, NRW)), bc8(omu[:, :])
                tt(sz[:, :, :], sp[:, 0:NRW, B:2 * B], mu).then_inc(vch, 1)
                e.wait_ge(vch, c(vch))
                tt(sp[:, 0:NRW, B:2 * B], sp[:, 0:NRW, 0:B], om).then_inc(vch, 1)
                e.wait_ge(vch, c(vch))
                tt(sz[:, :, :], sz[:, :, :], sp[:, 0:NRW, B:2 * B], ALU.add).then_inc(vch, 1)
                e.wait_ge(vch, c(vch))
                e.sem_inc(v2a, 1)
                r, k, v = sz[:, 0:4, :], sz[:, 4:8, :], sz[:, 8:12, :]
                W = [sw[:, n, :, :] for n in range(12)]
                new, t = W[10], W[9]
                st = sconv[:, :, :].rearrange("p j (b r) -> p j b r", r=2)
                tt(new, sp[:, 18:22, 0:B], sp[:, 22:26, 0:B]).then_inc(vch, 1)
                e.wait_ge(vch, c(vch))
                tt(W[8], st[:, :, :, 0], bc8(pcol("conv_w", 0, 4))).then_inc(vch, 1)
                e.wait_ge(vch, c(vch))
                tt(t, st[:, :, :, 1], bc8(pcol("conv_w", 4, 4))).then_inc(vch, 1)
                e.wait_ge(vch, c(vch))
                tt(W[8], W[8], t, ALU.add).then_inc(vch, 1)
                e.wait_ge(vch, c(vch))
                tt(t, new, bc8(pcol("conv_w", 8, 4))).then_inc(vch, 1)
                e.wait_ge(vch, c(vch))
                tt(W[8], W[8], t, ALU.add).then_inc(vch, 1)
                e.wait_ge(vch, c(vch))
                tt(xsn[:, 4:8, 0:B], W[8], sp[:, 14:18, 0:B]).then_inc(vch, 1)
                e.wait_ge(vch, c(vch))
                e.tensor_copy(fin[:, 80:112].rearrange("p (j b) -> p j b", j=4), new).then_inc(vch, 1)
                e.wait_ge(vch, c(vch))
                tt(W[4], k, bc8(pcol("k_k", 0, 4))).then_inc(vch, 1)
                e.wait_ge(vch, c(vch))
                tt(W[11], W[4], W[4]).then_inc(vch, 1)
                e.wait_ge(vch, c(vch))
                e.wait_ge(a2v, c(a2v))
                e.sem_inc(free[6], 1)
                e.sem_inc(free[7], 1)
                e.sem_inc(v2p, 1)
                e.wait_ge(a2v, c(a2v))
                e.sem_inc(free[7], 1)
                e.tensor_scalar(W[3], W[3], 1e-12, None, ALU.max).then_inc(vch, 1)
                e.wait_ge(vch, c(vch))
                e.reciprocal(W[3], W[3]).then_inc(vch, 1)
                e.wait_ge(vch, c(vch))
                tt(W[4], W[4], W[3]).then_inc(vch, 1)
                e.wait_ge(vch, c(vch))
                tt(W[5], W[1], bc8(pcol("k_a", 0, 4))).then_inc(vch, 1)
                e.wait_ge(vch, c(vch))
                tt(W[5], W[5], bc8(oka[:, :]), ALU.add).then_inc(vch, 1)
                e.wait_ge(vch, c(vch))
                tt(W[5], W[5], k).then_inc(vch, 1)
                e.wait_ge(vch, c(vch))
                tt(W[6], W[4], W[1]).then_inc(vch, 1)
                e.wait_ge(vch, c(vch))
                e.tensor_scalar(W[4], W[4], -1.0, None, ALU.mult).then_inc(vch, 1)
                e.wait_ge(vch, c(vch))
                e.wait_ge(s_state, c(s_state, 16 * 16))
                state = cl[:, 0:2048].rearrange("p (n k) -> p n k", k=N)
                work = flat(kka[:, :, :]).rearrange("p (n k) -> p n k", k=N)
                u = W[8]
                ubc = flat(u).unsqueeze(2).broadcast_to([P, 4 * B, N])
                vbc = flat(v).unsqueeze(2).broadcast_to([P, 4 * B, N])
                along = (W[4], W[0], W[6], W[5], r)

                def expand(j):
                    out = flat(Y if j % 2 else kkn).rearrange("p (n k) -> p n k", k=N)
                    tt(out, flat(along[j]).unsqueeze(2).broadcast_to([P, 4 * B, N]),
                           ident64[:, :].unsqueeze(1).broadcast_to([P, 4 * B, N])).then_inc(vch, 1)
                    e.wait_ge(vch, c(vch))
                    e.sem_inc(v2p, 1)

                expand(0)
                for j in range(5):
                    if j < 4:
                        expand(j + 1)
                    b0 = 4 * (j % 2)
                    bcast = psum[:, b0:b0 + 4, :].rearrange("p g (n k) -> p (g n) k", k=N)
                    e.wait_ge(fullV[b0 + 3], c(fullV[b0 + 3]))
                    if j == 0:
                        tt(work, state, bcast).then_inc(vch, 1)
                        e.wait_ge(vch, c(vch))
                        e.tensor_reduce(flat(u), work, AX.X, ALU.add).then_inc(vch, 1)
                        e.wait_ge(vch, c(vch))
                    elif j == 1:
                        tt(state, state, bcast).then_inc(vch, 1)
                        e.wait_ge(vch, c(vch))
                    elif j < 4:
                        tt(work, ubc if j == 2 else vbc, bcast).then_inc(vch, 1)
                        e.wait_ge(vch, c(vch))
                        tt(state, state, work, ALU.add).then_inc(vch, 1)
                        e.wait_ge(vch, c(vch))
                    else:
                        tt(work, state, bcast).then_inc(vch, 1)
                        e.wait_ge(vch, c(vch))
                        e.tensor_reduce(flat(W[7]), work, AX.X, ALU.add).then_inc(vch, 1)
                        e.wait_ge(vch, c(vch))
                    for g in range(4):
                        e.sem_inc(free[b0 + g], 1)
                ps7 = psum[:, 7, 0:4 * B].rearrange("p (a b) -> p a b", a=4)
                tt(W[11], r, W[5]).then_inc(vch, 1)
                e.wait_ge(vch, c(vch))
                tt(W[11], W[11], bc8(pcol("r_k", 0, 4))).then_inc(vch, 1)
                e.wait_ge(vch, c(vch))
                e.sem_inc(v2p, 1)
                e.wait_ge(fullV[7], c(fullV[7]))
                tt(W[8], v, ps7).then_inc(vch, 1)
                e.wait_ge(vch, c(vch))
                e.sem_inc(free[7], 1)
                e.tensor_copy(W[11], W[7]).then_inc(vch, 1)
                e.wait_ge(vch, c(vch))
                e.sem_inc(v2p, 1)
                e.wait_ge(fullV[7], c(fullV[7]))
                stt(W[7], ps7, -1.0 / N, W[7], ALU.mult, ALU.add).then_inc(vch, 1)
                e.wait_ge(vch, c(vch))
                e.sem_inc(free[7], 1)
                tt(W[11], W[7], W[7]).then_inc(vch, 1)
                e.wait_ge(vch, c(vch))
                e.sem_inc(v2p, 1)
                e.wait_ge(a2v, c(a2v))
                e.sem_inc(free[7], 1)
                e.reciprocal(W[3], W[3]).then_inc(vch, 1)
                e.wait_ge(vch, c(vch))
                tt(W[7], W[7], W[3]).then_inc(vch, 1)
                e.wait_ge(vch, c(vch))
                tt(W[7], W[7], bc8(pcol("ln_x_w", 0, 4))).then_inc(vch, 1)
                e.wait_ge(vch, c(vch))
                tt(W[7], W[7], bc8(pcol("ln_x_b", 0, 4)), ALU.add).then_inc(vch, 1)
                e.wait_ge(vch, c(vch))
                tt(W[7], W[7], W[8], ALU.add).then_inc(vch, 1)
                e.wait_ge(vch, c(vch))
                tt(xsn[:, 0:4, 0:B], W[7], W[2]).then_inc(vch, 1)
                e.wait_ge(vch, c(vch))
                sample_split()

            def sample_attention():
                for j in (3, 4):
                    e.sem_inc(cache_free[j], 1)
                e.sem_inc(v2p, 1)
                e.wait_ge(fullV[6], c(fullV[6]))
                e.tensor_copy(sprob[0:32, :], psum[0:32, 6, 0:NMEM]).then_inc(vch, 1)
                e.wait_ge(vch, c(vch))
                e.sem_inc(free[6], 1)
                e.reduce_max(sm[0:32, 88:89], sprob[0:32, :], AX.X).then_inc(vch, 1)
                e.wait_ge(vch, c(vch))
                e.tensor_scalar(sm[0:32, 89:90], sm[0:32, 88:89], -XSCALE, None, ALU.mult).then_inc(vch, 1)
                e.wait_ge(vch, c(vch))
                e.sem_inc(v2a, 1)
                e.wait_ge(a2v, c(a2v))
                e.reciprocal(sm[0:32, 91:92], sm[0:32, 90:91]).then_inc(vch, 1)
                e.wait_ge(vch, c(vch))
                e.tensor_scalar(sprob[0:32, :], sprob[0:32, :], sm[0:32, 91:92], None, ALU.mult).then_inc(vch, 1)
                e.wait_ge(vch, c(vch))
                e.sem_inc(v2p, 1)
                e.wait_ge(fullV[7], c(fullV[7]))
                e.tensor_copy(sprobT[:, :], psum[:, 7, 0:64]).then_inc(vch, 1)
                e.wait_ge(vch, c(vch))
                e.sem_inc(free[7], 1)
                e.sem_inc(v2p, 1)
                for b in range(B):
                    i = CACHE_OF[B + b]
                    e.wait_ge(cache_done[i], c(cache_done[i]))
                    if i in CACHE_OF[B + b + 1:]:
                        e.sem_inc(cache_free[i], 1)
                e.tensor_copy(xsn[:, :, 0:B], psum[:, 6, 0:KT * B].rearrange("p (k b) -> p k b", k=KT)).then_inc(vch, 1)
                e.wait_ge(vch, c(vch))
                e.sem_inc(free[6], 1)
                sample_split()

            with c.loop("block", NB - 1) as b:
                one_block(b, False)
            one_block(NB - 1, True)
            e.tensor_copy(fin[:, 0:64].rearrange("p (b k) -> p k b", k=KT), shn[:, :, 0:B]).then_inc(vch, 1)
            e.wait_ge(vch, c(vch))
            e.tensor_copy(fin[:, 64:72].rearrange("p (r j) -> p j r", j=4), ccarry[:, :, :]).then_inc(vch, 1)
            e.wait_ge(vch, c(vch))
            e.tensor_copy(fin[:, 72:80], shn[:, :, B]).then_inc(vch, 1)
            e.wait_ge(vch, c(vch))
            e.tensor_copy(fin[:, 112:176].rearrange("p (b k) -> p k b", k=KT), xsn[:, :, 0:B]).then_inc(vch, 1)
            e.wait_ge(vch, c(vch))
            e.sem_inc(v2p, 1)


_OUTS = (("y_prompt", (1, SEQ, D)), ("y_sample", (B, 1, D)), ("shift_p", (1, 1, D)),
         ("wkv_p", (1, 1, H, N, N)), ("conv_p", (1, 1, 2, RW)), ("ffn_p", (1, 1, 2, 2 * FFN)),
         ("mem_k_p", (1, 1, NMEM, NXH, 256)), ("mem_v_p", (1, 1, NMEM, NXH, 256)), ("shift_s", (1, B, D)),
         ("wkv_s", (1, B, H, N, N)), ("conv_s", (1, B, 2, RW)), ("ffn_s", (1, B, 2, 2 * FFN)))
_UNUSED = ("v0", "v1", "v2")


def kernel(**inputs):
    import concourse.bacc as bacc
    from concourse.bass_utils import run_bass_kernel_spmd

    nc = bacc.Bacc("TRN2", target_bir_lowering=False, num_devices=1)
    arrays, I, O = {}, {}, {}
    for name, a in inputs.items():
        if name in _UNUSED:
            continue
        a = np.ascontiguousarray(a)
        arrays[f"in_{name}"] = a
        I[name] = nc.dram_tensor(f"in_{name}", a.shape, mybir.dt.from_np(a.dtype), kind="ExternalInput").ap()
    for name, shape in _OUTS:
        O[name] = nc.dram_tensor(f"out_{name}", shape, F32, kind="ExternalOutput").ap()
    hybrid_decoder_step(nc, I, O)
    r = run_bass_kernel_spmd(nc, [arrays], core_ids=[0])
    return tuple(r.results[0][f"out_{name}"] for name, _ in _OUTS)
```
